# Optimizing a Trainium2 kernel written in Bass

```python
import jax
import jax.numpy as jnp
from jax import lax
import numpy as np

D_MODEL = 1024
BATCH = 1
SEQ = 256
DEPTH = 2

GRID_W = 64
CTX_LEN = 256
HEAD_DIM = 64
NORM_EPS = 1e-6
L2_EPS = 1e-12
N_EVEN = (DEPTH + 1) // 2
N_ODD = DEPTH // 2

GLA_DV = 64
GLA_DK = 32
GLA_HEADS = (D_MODEL // 2) // GLA_DV
GLA_LOWRANK = 16
GLA_TAU = 16.0
GLA_CHUNK = 64

ATT_HEADS = (D_MODEL // 2) // HEAD_DIM
ATT_KV_HEADS = ATT_HEADS // 4
WINDOW = 128
ATT_BLOCK = 128
ROPE_THETA = 10000.0

FOURIER_GROUP_DIM = 64
FOURIER_WIDTH = D_MODEL // 4
FOURIER_GROUPS = FOURIER_WIDTH // FOURIER_GROUP_DIM

RWKV_DIM = D_MODEL - FOURIER_WIDTH
RWKV_HEADS = RWKV_DIM // HEAD_DIM
RWKV_W_RANK = 64
RWKV_A_RANK = 64
RWKV_G_RANK = 128
RWKV_GN_EPS = 64e-5

N_EXPERTS = 16
N_GROUPS = 4
TOP_K = 2
D_EXPERT = 512

EVEN_SPLIT = (GLA_HEADS * GLA_DK, GLA_HEADS * GLA_DK, GLA_HEADS * GLA_DV, GLA_HEADS * GLA_DV,
              2 * GLA_LOWRANK, ATT_HEADS * HEAD_DIM, ATT_KV_HEADS * HEAD_DIM, ATT_KV_HEADS * HEAD_DIM)
EVEN_COLS = sum(EVEN_SPLIT)
RWKV_SPLIT = (RWKV_DIM, RWKV_DIM, RWKV_DIM, 2 * RWKV_W_RANK, 2 * RWKV_A_RANK, RWKV_G_RANK)
RWKV_COLS = sum(RWKV_SPLIT)
ODD_COLS = FOURIER_WIDTH + RWKV_COLS

kernel_name = "hybrid_gla_swa_fourier_rwkv7_moe_prefix_dit"

def rms_norm(x, gain, eps=NORM_EPS):
    xf = x.astype(jnp.float32)
    y = xf * lax.rsqrt(jnp.mean(xf * xf, axis=-1, keepdims=True) + eps)
    return (y * gain.astype(jnp.float32)).astype(x.dtype)

def modulate(x, gain, shift, scale):
    return rms_norm(x, gain) * (1.0 + scale) + shift

def split_cols(z, sizes):
    return jnp.split(z, np.cumsum(sizes)[:-1].tolist(), axis=-1)

def _ident(t):
    return t

def _flip(t):
    return jnp.flip(t, axis=1)

def axial_rope_tables(n_lat):
    rows = n_lat // GRID_W
    row = jnp.repeat(jnp.arange(rows, dtype=jnp.float32), GRID_W)
    col = jnp.tile(jnp.arange(GRID_W, dtype=jnp.float32), rows)
    n_freq = HEAD_DIM // 4
    inv_freq = ROPE_THETA ** (-jnp.arange(n_freq, dtype=jnp.float32) / n_freq)
    ang = jnp.concatenate([row[:, None] * inv_freq, col[:, None] * inv_freq], axis=-1)
    return jnp.cos(ang), jnp.sin(ang)

def apply_rope(t, cos, sin):
    half = t.shape[-1] // 2
    t1, t2 = t[..., :half], t[..., half:]
    c, s = cos[None, :, None, :], sin[None, :, None, :]
    return jnp.concatenate([t1 * c - t2 * s, t1 * s + t2 * c], axis=-1).astype(t.dtype)

def gla_log_decay(z_dec, dec_w, dec_b, direction):
    B, L, _ = z_dec.shape
    zd = z_dec[..., direction * GLA_LOWRANK:(direction + 1) * GLA_LOWRANK].astype(jnp.float32)
    la = jax.nn.log_sigmoid(zd @ dec_w[direction].astype(jnp.float32)
                            + dec_b[direction].astype(jnp.float32)) / GLA_TAU
    return la.reshape(B, L, GLA_HEADS, GLA_DK)

def gla_chunk_scan(k, v, log_a, s0, q=None):
    B, L, H, _ = k.shape
    dv = v.shape[-1]
    C = GLA_CHUNK
    nc = L // C
    emit = q is not None

    def chunks(t):
        return jnp.moveaxis(t.reshape(B, nc, C, H, t.shape[-1]), 1, 0)

    causal = jnp.tril(jnp.ones((C, C), dtype=bool))[None, :, :, None, None]

    def step(S, inp):
        k_c, v_c, g_c = inp[0], inp[1], inp[2]
        b = jnp.cumsum(g_c, axis=1)
        b_last = b[:, -1]
        S_new = (jnp.exp(b_last)[..., None] * S
                 + jnp.einsum('bjhd,bjhe->bhde', k_c * jnp.exp(b_last[:, None] - b), v_c))
        if not emit:
            return S_new, None
        q_c = inp[3]
        diff = jnp.where(causal, b[:, :, None] - b[:, None], -jnp.inf)
        att = jnp.einsum('bihd,bjhd,bijhd->bhij', q_c, k_c, jnp.exp(diff))
        o = (jnp.einsum('bhij,bjhe->bihe', att, v_c)
             + jnp.einsum('bihd,bhde->bihe', q_c * jnp.exp(b), S))
        return S_new, o

    xs = (chunks(k), chunks(v), chunks(log_a)) + ((chunks(q),) if emit else ())
    S, o = lax.scan(step, s0, xs)
    o = jnp.moveaxis(o, 0, 1).reshape(B, L, H, dv) if emit else None
    return o, S

def gla_bidirectional(ctx_t, lat_t, need_ctx):
    qc, kc, vc, dc = ctx_t
    ql, kl, vl, dl = lat_t
    B = kl.shape[0]
    s0 = jnp.zeros((B, GLA_HEADS, GLA_DK, GLA_DV), jnp.float32)
    o_lat, o_ctx = 0.0, 0.0
    for d in range(2):
        f = _ident if d == 0 else _flip
        oc, s_ctx = gla_chunk_scan(f(kc), f(vc), f(dc[d]), s0, f(qc) if need_ctx else None)
        ol, _ = gla_chunk_scan(f(kl), f(vl), f(dl[d]), s_ctx, f(ql))
        o_lat = o_lat + f(ol)
        if need_ctx:
            o_ctx = o_ctx + f(oc)
    return o_lat, (o_ctx if need_ctx else None)

def window_attention(q, k, v, k_ctx, v_ctx, sink):
    B, N, Hq, hd = q.shape
    G = Hq // ATT_KV_HEADS
    nb = N // ATT_BLOCK
    scale = hd ** -0.5
    qb = q.reshape(B, nb, ATT_BLOCK, ATT_KV_HEADS, G, hd)

    def windows(t):
        tp = jnp.pad(t, ((0, 0), (ATT_BLOCK, ATT_BLOCK), (0, 0), (0, 0)))
        tp = tp.reshape(B, nb + 2, ATT_BLOCK, ATT_KV_HEADS, hd)
        return jnp.concatenate([tp[:, :-2], tp[:, 1:-1], tp[:, 2:]], axis=2)

    kw, vw = windows(k), windows(v)
    s_loc = jnp.einsum('bnqkgd,bnjkd->bnkgqj', qb, kw).astype(jnp.float32) * scale
    s_ctx = jnp.einsum('bnqkgd,bckd->bnkgqc', qb, k_ctx).astype(jnp.float32) * scale
    blk = jnp.arange(nb)[:, None, None] * ATT_BLOCK
    qpos = blk + jnp.arange(ATT_BLOCK)[None, :, None]
    kpos = blk - ATT_BLOCK + jnp.arange(3 * ATT_BLOCK)[None, None, :]
    valid = (jnp.abs(kpos - qpos) <= WINDOW) & (kpos >= 0) & (kpos < N)
    s_loc = jnp.where(valid[None, :, None, None], s_loc, -jnp.inf)
    sk = sink.reshape(ATT_KV_HEADS, G).astype(jnp.float32)[None, None, :, :, None, None]
    m = jnp.maximum(jnp.maximum(s_loc.max(-1, keepdims=True), s_ctx.max(-1, keepdims=True)), sk)
    p_loc = jnp.exp(s_loc - m)
    p_ctx = jnp.exp(s_ctx - m)
    denom = p_loc.sum(-1) + p_ctx.sum(-1) + jnp.exp(sk - m)[..., 0]
    o = (jnp.einsum('bnkgqj,bnjkd->bnqkgd', p_loc, vw.astype(jnp.float32))
         + jnp.einsum('bnkgqc,bckd->bnqkgd', p_ctx, v_ctx.astype(jnp.float32)))
    o = o * jnp.transpose(1.0 / denom, (0, 1, 4, 2, 3))[..., None]
    return o.reshape(B, N, Hq * hd)

def context_attention(q, k, v, sink):
    B, Lc, Hq, hd = q.shape
    G = Hq // ATT_KV_HEADS
    qc = q.reshape(B, Lc, ATT_KV_HEADS, G, hd)
    s = jnp.einsum('bqkgd,bckd->bkgqc', qc, k).astype(jnp.float32) * hd ** -0.5
    sk = sink.reshape(ATT_KV_HEADS, G).astype(jnp.float32)[None, :, :, None, None]
    m = jnp.maximum(s.max(-1, keepdims=True), sk)
    p = jnp.exp(s - m)
    p = p / (p.sum(-1, keepdims=True) + jnp.exp(sk - m))
    o = jnp.einsum('bkgqc,bckd->bqkgd', p, v.astype(jnp.float32))
    return o.reshape(B, Lc, Hq * hd)

def even_mixer(h_ctx, h_lat, cos, sin, w_in, w_out, dec_w, dec_b, out_norm,
               q_norm, k_norm, sink, need_ctx):
    def project(h):
        B, L, _ = h.shape
        gq, gk, gv, gg, gdec, aq, ak, av = split_cols(h @ w_in, EVEN_SPLIT)
        hf = lambda t: t.reshape(B, L, GLA_HEADS, -1).astype(jnp.float32)
        gla = (hf(gq) * GLA_DK ** -0.5, hf(gk), hf(gv),
               tuple(gla_log_decay(gdec, dec_w, dec_b, d) for d in range(2)))
        att = (rms_norm(aq.reshape(B, L, ATT_HEADS, HEAD_DIM), q_norm),
               rms_norm(ak.reshape(B, L, ATT_KV_HEADS, HEAD_DIM), k_norm),
               av.reshape(B, L, ATT_KV_HEADS, HEAD_DIM))
        return gla, att, gg

    gla_c, att_c, gg_c = project(h_ctx)
    gla_l, att_l, gg_l = project(h_lat)
    q_l = apply_rope(att_l[0], cos, sin)
    k_l = apply_rope(att_l[1], cos, sin)
    o_gla_l, o_gla_c = gla_bidirectional(gla_c, gla_l, need_ctx)

    def merge(o_gla, gg, o_att, dtype):
        B, L = gg.shape[:2]
        g = rms_norm(o_gla, out_norm).reshape(B, L, -1) * jax.nn.silu(gg.astype(jnp.float32))
        return jnp.concatenate([g, o_att], axis=-1).astype(dtype) @ w_out

    o_att_l = window_attention(q_l, k_l, att_l[2], att_c[1], att_c[2], sink)
    out_lat = merge(o_gla_l, gg_l, o_att_l, h_lat.dtype)
    out_ctx = None
    if need_ctx:
        o_att_c = context_attention(att_c[0], att_c[1], att_c[2], sink)
        out_ctx = merge(o_gla_c, gg_c, o_att_c, h_ctx.dtype)
    return out_lat, out_ctx

def fourier_mix(z):
    B, L, _ = z.shape
    zg = z.astype(jnp.float32).reshape(B, L, FOURIER_GROUPS, FOURIER_GROUP_DIM)
    y = jnp.real(jnp.fft.fft2(zg, axes=(1, 3), norm='ortho'))
    return y.reshape(B, L, FOURIER_WIDTH)

def centred_shift(z, mu):
    zp = jnp.pad(z, ((0, 0), (1, 1), (0, 0)))
    return z + mu * (0.5 * (zp[:, :-2] + zp[:, 2:]) - z)

def rwkv_prepare(z, mu, w0, w2, a0, a2, kk_scale, k_a):
    B, L, _ = z.shape
    z = centred_shift(z.astype(jnp.float32), mu)
    r, k, v, zw, za, zg = split_cols(z, RWKV_SPLIT)
    heads = lambda t: t.reshape(B, L, RWKV_HEADS, HEAD_DIM)
    kk = heads(k * kk_scale)
    kk = kk * lax.rsqrt(jnp.sum(kk * kk, axis=-1, keepdims=True) + L2_EPS)
    per_dir = []
    for d in range(2):
        zw_d = zw[..., d * RWKV_W_RANK:(d + 1) * RWKV_W_RANK]
        za_d = za[..., d * RWKV_A_RANK:(d + 1) * RWKV_A_RANK]
        w_log = -jax.nn.softplus(-(w0[d] + jnp.tanh(zw_d) @ w2[d])) - 0.5
        decay = jnp.exp(-jnp.exp(w_log))
        a = jax.nn.sigmoid(a0[d] + za_d @ a2[d])
        k_d = k * (1.0 + (a - 1.0) * k_a)
        per_dir.append((heads(decay), heads(k_d), heads(a)))
    return heads(r), heads(v), kk, zg, per_dir

def rwkv_scan(decay, k, v, kk, a, s0, r=None):
    emit = r is not None
    xs = (decay, k, v, kk, a) + ((r,) if emit else ())
    xs = tuple(jnp.moveaxis(t, 1, 0) for t in xs)

    def step(S, inp):
        w_t, k_t, v_t, kk_t, a_t = inp[:5]
        S = (S * w_t[:, :, None, :]
             - jnp.einsum('bhvk,bhk->bhv', S, kk_t)[..., None] * (kk_t * a_t)[:, :, None, :]
             + v_t[..., None] * k_t[:, :, None, :])
        y = jnp.einsum('bhvk,bhk->bhv', S, inp[5]) if emit else None
        return S, y

    S, ys = lax.scan(step, s0, xs)
    return (jnp.moveaxis(ys, 0, 1) if emit else None), S

def rwkv_bonus(r, k, v, r_k):
    return jnp.sum(r * k * r_k, axis=-1, keepdims=True) * v

def rwkv_bidirectional(ctx_p, lat_p, r_k, need_ctx):
    rc, vc, kkc, _, dirs_c = ctx_p
    rl, vl, kkl, _, dirs_l = lat_p
    B = rl.shape[0]
    s0 = jnp.zeros((B, RWKV_HEADS, HEAD_DIM, HEAD_DIM), jnp.float32)
    y_lat, y_ctx = 0.0, 0.0
    for d in range(2):
        f = _ident if d == 0 else _flip
        dec_c, k_c, a_c = dirs_c[d]
        dec_l, k_l, a_l = dirs_l[d]
        yc, s_ctx = rwkv_scan(f(dec_c), f(k_c), f(vc), f(kkc), f(a_c), s0,
                              f(rc) if need_ctx else None)
        yl, _ = rwkv_scan(f(dec_l), f(k_l), f(vl), f(kkl), f(a_l), s_ctx, f(rl))
        y_lat = y_lat + f(yl) + rwkv_bonus(rl, k_l, vl, r_k)
        if need_ctx:
            y_ctx = y_ctx + f(yc) + rwkv_bonus(rc, k_c, vc, r_k)
    return y_lat, (y_ctx if need_ctx else None)

def rwkv_output(y, zg, g2, ln_g, ln_b):
    B, L = y.shape[:2]
    mean = jnp.mean(y, axis=-1, keepdims=True)
    var = jnp.mean(jnp.square(y - mean), axis=-1, keepdims=True)
    yn = ((y - mean) * lax.rsqrt(var + RWKV_GN_EPS)).reshape(B, L, RWKV_DIM)
    return (yn * ln_g + ln_b) * (jax.nn.sigmoid(zg) @ g2)

def odd_mixer(h_ctx, h_lat, w_in, w_out, mu, w0, w2, a0, a2, g2, kk_scale, k_a, r_k,
              ln_g, ln_b, need_ctx):
    f32 = lambda t: t.astype(jnp.float32)
    mu, w0, w2, a0, a2, g2 = f32(mu), f32(w0), f32(w2), f32(a0), f32(a2), f32(g2)
    kk_scale, k_a, r_k, ln_g, ln_b = f32(kk_scale), f32(k_a), f32(r_k), f32(ln_g), f32(ln_b)
    z_ctx, z_lat = h_ctx @ w_in, h_lat @ w_in
    prep = lambda z: rwkv_prepare(z[..., FOURIER_WIDTH:], mu, w0, w2, a0, a2, kk_scale, k_a)
    p_ctx, p_lat = prep(z_ctx), prep(z_lat)
    y_lat, y_ctx = rwkv_bidirectional(p_ctx, p_lat, r_k, need_ctx)

    def merge(z, p, y, dtype):
        rw = rwkv_output(y, p[3], g2, ln_g, ln_b)
        cat = jnp.concatenate([fourier_mix(z[..., :FOURIER_WIDTH]), rw], axis=-1)
        return cat.astype(dtype) @ w_out

    out_lat = merge(z_lat, p_lat, y_lat, h_lat.dtype)
    out_ctx = merge(z_ctx, p_ctx, y_ctx, h_ctx.dtype) if need_ctx else None
    return out_lat, out_ctx

def routed_moe(h, router_w, router_b, w_gate, w_up, w_down):
    logits = jnp.einsum('bld,de->ble', h, router_w).astype(jnp.float32)
    scores = jax.nn.sigmoid(logits)
    sel = scores + router_b.astype(jnp.float32)
    B, L, E = sel.shape
    per_group = E // N_GROUPS
    grp_score = lax.top_k(sel.reshape(B, L, N_GROUPS, per_group), TOP_K)[0].sum(-1)
    best = jnp.argmax(grp_score, axis=-1)
    in_group = (jnp.arange(E) // per_group)[None, None, :] == best[..., None]
    _, idx = lax.top_k(jnp.where(in_group, sel, -jnp.inf), TOP_K)
    w = jnp.take_along_axis(scores, idx, axis=-1)
    w = w / jnp.sum(w, axis=-1, keepdims=True)
    gates = jnp.sum(jax.nn.one_hot(idx, E, dtype=jnp.float32) * w[..., None], axis=-2)
    out = jnp.zeros(h.shape, jnp.float32)
    for e in range(N_EXPERTS):
        he = (jax.nn.silu(h @ w_gate[e]) * (h @ w_up[e])) @ w_down[e]
        out = out + gates[..., e:e + 1] * he
    return out.astype(h.dtype)

def setup_inputs(seed: int = 0) -> dict:
    key = jax.random.key(seed)
    ks = iter(jax.random.split(key, 40))
    D = D_MODEL

    def nrm(shape, s):
        return jax.random.normal(next(ks), shape, jnp.float32) * s

    def gain(shape):
        return 1.0 + nrm(shape, 0.05)

    w0_base = jnp.tile(jnp.linspace(-6.0, -1.0, HEAD_DIM), RWKV_HEADS)[None, None, :]
    return {
        'x': nrm((BATCH, SEQ, D), 1.0),
        'c': nrm((BATCH, D), 1.0),
        'ctx': nrm((BATCH, CTX_LEN, D), 1.0),
        'c_ctx': nrm((D,), 1.0),
        'ada_w': nrm((DEPTH, D, 6 * D), 0.5 * D ** -0.5),
        'ada_b': nrm((DEPTH, 6 * D), 0.02),
        'norm_mix': gain((DEPTH, D)),
        'norm_ffn': gain((DEPTH, D)),
        'even_w_in': nrm((N_EVEN, D, EVEN_COLS), D ** -0.5),
        'even_w_out': nrm((N_EVEN, D, D), D ** -0.5),
        'gla_dec_w': nrm((N_EVEN, 2, GLA_LOWRANK, GLA_HEADS * GLA_DK), GLA_LOWRANK ** -0.5),
        'gla_dec_b': 1.0 + nrm((N_EVEN, 2, GLA_HEADS * GLA_DK), 0.5),
        'gla_out_norm': gain((N_EVEN, GLA_DV)),
        'att_q_norm': gain((N_EVEN, HEAD_DIM)),
        'att_k_norm': gain((N_EVEN, HEAD_DIM)),
        'att_sink': nrm((N_EVEN, ATT_HEADS), 0.5),
        'odd_w_in': nrm((N_ODD, D, ODD_COLS), D ** -0.5),
        'odd_w_out': nrm((N_ODD, D, D), D ** -0.5),
        'rwkv_mu': jax.random.uniform(next(ks), (N_ODD, RWKV_COLS), jnp.float32),
        'rwkv_w0': w0_base + nrm((N_ODD, 2, RWKV_DIM), 0.1),
        'rwkv_w2': nrm((N_ODD, 2, RWKV_W_RANK, RWKV_DIM), RWKV_W_RANK ** -0.5),
        'rwkv_a0': nrm((N_ODD, 2, RWKV_DIM), 0.1),
        'rwkv_a2': nrm((N_ODD, 2, RWKV_A_RANK, RWKV_DIM), RWKV_A_RANK ** -0.5),
        'rwkv_g2': nrm((N_ODD, RWKV_G_RANK, RWKV_DIM), RWKV_G_RANK ** -0.5),
        'rwkv_kk_scale': 0.85 + nrm((N_ODD, RWKV_DIM), 0.05),
        'rwkv_k_a': gain((N_ODD, RWKV_DIM)),
        'rwkv_r_k': nrm((N_ODD, RWKV_HEADS, HEAD_DIM), 0.1),
        'rwkv_ln_g': gain((N_ODD, RWKV_DIM)),
        'rwkv_ln_b': nrm((N_ODD, RWKV_DIM), 0.02),
        'router_w': nrm((D, N_EXPERTS), D ** -0.5),
        'router_b': nrm((N_EXPERTS,), 0.01),
        'moe_w_gate': nrm((DEPTH, N_EXPERTS, D, D_EXPERT), D ** -0.5),
        'moe_w_up': nrm((DEPTH, N_EXPERTS, D, D_EXPERT), D ** -0.5),
        'moe_w_down': nrm((DEPTH, N_EXPERTS, D_EXPERT, D), D_EXPERT ** -0.5),
    }

def reference(x, c, ctx, c_ctx, ada_w, ada_b, norm_mix, norm_ffn,
              even_w_in, even_w_out, gla_dec_w, gla_dec_b, gla_out_norm,
              att_q_norm, att_k_norm, att_sink,
              odd_w_in, odd_w_out, rwkv_mu, rwkv_w0, rwkv_w2, rwkv_a0, rwkv_a2,
              rwkv_g2, rwkv_kk_scale, rwkv_k_a, rwkv_r_k, rwkv_ln_g, rwkv_ln_b,
              router_w, router_b, moe_w_gate, moe_w_up, moe_w_down):
    n_lat = x.shape[1]
    lc = ctx.shape[1]
    cos, sin = axial_rope_tables(n_lat)
    silu_c = jax.nn.silu(c)
    silu_cc = jax.nn.silu(c_ctx)
    x_lat, x_ctx = x, ctx
    for layer in range(DEPTH):
        need_ctx = layer < DEPTH - 1
        mod_l = jnp.split((silu_c @ ada_w[layer] + ada_b[layer])[:, None, :], 6, axis=-1)
        mod_c = jnp.split((silu_cc @ ada_w[layer] + ada_b[layer])[None, None, :], 6, axis=-1)
        h_lat = modulate(x_lat, norm_mix[layer], mod_l[0], mod_l[1])
        h_ctx = modulate(x_ctx, norm_mix[layer], mod_c[0], mod_c[1])
        i = layer // 2
        if layer % 2 == 0:
            o_lat, o_ctx = even_mixer(h_ctx, h_lat, cos, sin, even_w_in[i], even_w_out[i],
                                      gla_dec_w[i], gla_dec_b[i], gla_out_norm[i],
                                      att_q_norm[i], att_k_norm[i], att_sink[i], need_ctx)
        else:
            o_lat, o_ctx = odd_mixer(h_ctx, h_lat, odd_w_in[i], odd_w_out[i], rwkv_mu[i],
                                     rwkv_w0[i], rwkv_w2[i], rwkv_a0[i], rwkv_a2[i], rwkv_g2[i],
                                     rwkv_kk_scale[i], rwkv_k_a[i], rwkv_r_k[i],
                                     rwkv_ln_g[i], rwkv_ln_b[i], need_ctx)
        x_lat = x_lat + mod_l[2] * o_lat
        h_lat = modulate(x_lat, norm_ffn[layer], mod_l[3], mod_l[4])
        if need_ctx:
            x_ctx = x_ctx + mod_c[2] * o_ctx
            h_ctx = modulate(x_ctx, norm_ffn[layer], mod_c[3], mod_c[4])
            y = routed_moe(jnp.concatenate([h_ctx, h_lat], axis=1), router_w, router_b,
                           moe_w_gate[layer], moe_w_up[layer], moe_w_down[layer])
            x_ctx = x_ctx + mod_c[5] * y[:, :lc]
            x_lat = x_lat + mod_l[5] * y[:, lc:]
        else:
            x_lat = x_lat + mod_l[5] * routed_moe(h_lat, router_w, router_b, moe_w_gate[layer],
                                                  moe_w_up[layer], moe_w_down[layer])
    return x_lat


_drawn_inputs = setup_inputs


def setup_inputs(seed=0):
    import zlib

    import numpy as np

    out = dict(_drawn_inputs(seed))
    spreads = {}
    factors = {'att_q_norm': 8.0,
     'att_k_norm': 3.895,
     'att_sink': 8.0,
     'rwkv_a0': 8.0,
     'rwkv_r_k': 4.418,
     'rwkv_ln_g': 3.738,
     'rwkv_ln_b': 8.0}
    for name, (base, spread) in spreads.items():
        noise = np.random.default_rng([zlib.crc32(name.encode()), seed]).standard_normal(out[name].shape)
        drawn = base * np.exp(spread * noise) if base else spread * noise
        out[name] = jnp.asarray(drawn.astype(out[name].dtype))
    for name, factor in factors.items():
        out[name] = (out[name] * factor).astype(out[name].dtype)
    return out
```

```python
from contextlib import ExitStack

import numpy as np

import concourse.bass as bass
from concourse import mybir

P = 128
D = 1024
KD = D // P
T = 512
NT = T // P
SEG = 256
DEPTH = 2
NSLOT = 6

GLA_H, GLA_DK, GLA_DV, GLA_RANK, GLA_TAU = 8, 32, 64, 16, 16.0
GLA_C = 32
NCH = T // GLA_C
ATT_H, ATT_KV, HD, WINDOW = 8, 2, 64, 128
GRP = ATT_H // ATT_KV
RW_DIM, RW_H, NPAIR = 768, 12, 6
FOUR = 256
N_EXP, D_EXP = 16, 512
NORM_EPS = 1e-6
L2_EPS = 1e-12
GN_EPS = 64e-5
BIG = 1e30
LEVELS = (1, 2, 4, 8, 16, 32, 64)
EXP_M05 = float(np.exp(-0.5))

F32 = mybir.dt.float32
ALU = mybir.AluOpType
ACT = mybir.ActivationFunctionType
AX = mybir.AxisListType
ds = bass.ds

CONST_COLS = [("ident", P), ("ones", P), ("head_ones", P), ("att_mask", 2 * P), ("level", 14 * P),
              ("strict", 2 * P), ("incl", 2 * P), ("gla_incl", 2 * P), ("gla_heads", 256),
              ("reset32", T), ("reset128", T), ("dft_tok", 2 * T), ("dft_ch", 2 * P),
              ("rope", 2 * 2 * 32), ("first4", 4), ("first16", 16)]
PARAM_COLS = [("norm", 4 * KD), ("cond", 2 * KD), ("ada_b", 96), ("lora_mu", 3), ("router", KD * 16)]
PAIR_COLS = 12
ROW_COLS = [("router_b", 16), ("sink", 8), ("qk_gain", 5 * HD), ("gla_gain", GLA_DV)]


def columns(table):
    at, n = {}, 0
    for name, width in table:
        at[name] = (n, n + width)
        n += width
    return at, n


def shape_constants():
    at, n = columns(CONST_COLS)
    c = np.zeros((P, n), np.float32)

    def put(name, a):
        c[:, at[name][0]:at[name][1]] = a.reshape(P, -1)

    a, b = np.arange(P)[:, None], np.arange(P)[None, :]
    put("ident", (a == b).astype(np.float32))
    put("ones", np.ones((P, P), np.float32))
    put("head_ones", (a // 64 == b // 64).astype(np.float32))
    put("att_mask", np.stack([np.where(b <= a, 0.0, -BIG), np.where(b >= a, 0.0, -BIG)], 1).astype(np.float32))
    low = [((a // (2 * m) == b // (2 * m)) & (a // m % 2 == 1) & (b // m % 2 == 0)).astype(np.float32) for m in LEVELS]
    put("level", np.stack([m.T for m in low] + low, 1))
    put("strict", np.stack([a < b, a > b], 1).astype(np.float32))
    put("incl", np.stack([a <= b, a >= b], 1).astype(np.float32))
    same = a // GLA_C == b // GLA_C
    put("gla_incl", np.stack([same & (a <= b), same & (a >= b)], 1).astype(np.float32))
    put("gla_heads", (a // GLA_DK == np.arange(256)[None, :] // GLA_DV).astype(np.float32))
    t = np.arange(T)[None, :]
    put("reset32", np.broadcast_to(t % GLA_C != 0, (P, T)).astype(np.float32))
    put("reset128", np.broadcast_to(t % P != 0, (P, T)).astype(np.float32))
    ang = 2 * np.pi * (np.outer(np.arange(SEG), np.arange(SEG)) % SEG) / SEG
    tok = np.concatenate([np.cos(ang), np.sin(ang)], 1) / np.sqrt(SEG)
    put("dft_tok", tok.reshape(2, P, T).transpose(1, 0, 2).astype(np.float32))
    ch = 2 * np.pi * (np.outer(np.arange(64), np.arange(64)) % 64) / 64
    both = np.zeros((P, 2, P))
    for h in range(2):
        s = slice(64 * h, 64 * h + 64)
        both[s, 0, s], both[s, 1, s] = np.cos(ch) / 8, -np.sin(ch) / 8
    put("dft_ch", both.astype(np.float32))
    n_freq = HD // 4
    inv = (np.float32(10000.0) ** (-np.arange(n_freq, dtype=np.float32) / np.float32(n_freq))).astype(np.float32)
    pos = np.arange(SEG)
    rot = np.concatenate([(pos // 64).astype(np.float32)[:, None] * inv,
                          (pos % 64).astype(np.float32)[:, None] * inv], -1)
    rope = np.stack([np.cos(rot), np.sin(rot)], 0).astype(np.float32)
    put("rope", rope.reshape(2, 2, P, 32).transpose(2, 0, 1, 3))
    put("first4", np.broadcast_to(np.arange(4, 0, -1, dtype=np.float32), (P, 4)))
    put("first16", np.broadcast_to(np.arange(16, 0, -1, dtype=np.float32), (P, 16)))
    return c


def build(nc, x, ctx_in, ada_w, even_w_in, even_w_out, odd_w_in, odd_w_out, moe_w_gate, moe_w_up, moe_w_down,
          consts, params, rows, gla_small, pair_small, pair_w, out):
    CA, CN = columns(CONST_COLS)
    PA, PN = columns(PARAM_COLS)
    RA, RN = columns(ROW_COLS)

    with ExitStack() as stack:
        def sb(name, shape):
            return stack.enter_context(nc.sbuf_tensor(name, shape, F32))

        def sem(name):
            return stack.enter_context(nc.semaphore(name))

        PS = stack.enter_context(nc.psum_tensor("PS", [P, 8, 512], F32))
        slots = sb("slots", [P, NSLOT, KD, 512])
        X = sb("X", [P, NT, D])
        HT = sb("HT", [P, KD, T])
        XN = sb("XN", [P, NT, D])
        SCR = sb("SCR", [P, 8192])
        CST = sb("CST", [P, CN])
        PRM = sb("PRM", [P, PN])
        ROW = sb("ROW", [P, RN])
        COND = sb("COND", [P, KD, 2])
        MODC = sb("MODC", [P, DEPTH * 96])
        GAIN = sb("GAIN", [P, 4, KD, 2])
        SS = sb("SS", [P, 64])
        RS = sb("RS", [P, 64])
        EPS = sb("EPS", [P, 4])

        def cst(name):
            return CST[:, CA[name][0]:CA[name][1]]

        def prm(name):
            return PRM[:, PA[name][0]:PA[name][1]]

        def row(name):
            return ROW[:, RA[name][0]:RA[name][1]]

        ident, ones, head_ones = cst("ident"), cst("ones"), cst("head_ones")
        mod = MODC[:].rearrange("p (l m v) -> p l m v", l=DEPTH, v=2)

        def split(buf, sizes):
            pieces, n = [], 0
            for s in sizes:
                pieces.append(buf[:, n:n + s])
                n += s
            assert n <= buf.shape[1], (n, buf.shape)
            return pieces

        w_ready = [sem(f"w_ready{s}") for s in range(NSLOT)]
        w_free = [sem(f"w_free{s}") for s in range(NSLOT)]
        in_ready = sem("in_ready")
        phase = sem("phase")
        out_stored = sem("out_stored")

        ENGINES = 3

        def meet(eng, n):
            eng.drain().then_inc(phase, 1)
            eng.wait_ge(phase, ENGINES * n)

        ada_rows, ada_copied = sem("ada_rows"), sem("ada_copied")
        ada_turned, ada_stored = sem("ada_turned"), sem("ada_stored")
        cond_th, cond_ready = sem("cond_th"), sem("cond_ready")
        cat_turned = sem("cat_turned_all")
        norm_ev = {k: sem(k) for k in ("rstd_ready", "xn_ready", "xt_turned")}
        gate_ev = {k: sem(k) for k in ("gate_diag", "gate_spread", "gate_copied")}
        cat_turned_k = sem("cat_turned_k")
        proj_ev = {k: sem(k) for k in ("out_done", "out_added")}
        rt_ev = {k: sem(k) for k in ("logits_done", "logits_exp")}
        moe_ev = {k: sem(k) for k in ("gateup_done", "tanh_done", "hidden_done", "down_done", "y_added")}
        XN_BEFORE = (0, 4, 8, 12)
        OUT_BEFORE = (0, 8)
        HIDDEN_BEFORE = (0, 4 * N_EXP)
        DOWN_BEFORE = (0, 8 * N_EXP)

        ADA_ROW = SCR[:, 0:1024].rearrange("p (b n) -> p b n", b=2)
        N_ADA = 12

        def ada_pe(pe):
            pe.wait_ge(cond_ready, 1)
            for i in range(DEPTH):
                for b in range(N_ADA + 1):
                    if b < N_ADA:
                        pe.wait_ge(w_ready[b % NSLOT], i * 32 + 16 * (b // NSLOT + 1))
                        if i * N_ADA + b >= 2:
                            pe.wait_ge(ada_copied, i * N_ADA + b - 1)
                        for k in range(KD):
                            mm = pe.matmul(PS[0:2, b % 2, :], COND[:, k, :], slots[:, b % NSLOT, k, :],
                                           start=(k == 0), stop=(k == KD - 1))
                        mm.then_inc(ada_rows, 1)
                    if b >= 1:
                        pe.wait_ge(ada_copied, i * N_ADA + b)
                        if i * N_ADA + b >= 3:
                            pe.wait_ge(ada_stored, i * N_ADA + b - 2)
                        for q in range(4):
                            mm = pe.matmul(PS[:, 2 + b % 2, 2 * q:2 * q + 2], ADA_ROW[0:2, (b - 1) % 2, q * P:q * P + P],
                                           ident[0:2, 0:2], start=True, stop=True)
                        mm.then_inc(ada_turned, 1)

        def ada_act(act):
            for i in range(DEPTH):
                for b in range(N_ADA):
                    act.wait_ge(ada_rows, i * N_ADA + b + 1)
                    if i * N_ADA + b >= 2:
                        act.wait_ge(ada_turned, i * N_ADA + b - 1)
                    act.activation(ADA_ROW[0:2, b % 2, :], PS[0:2, b % 2, :], ACT.Copy).then_inc(ada_copied, 1)

        def ada_dve(dve):
            bias = prm("ada_b")
            for i in range(DEPTH):
                for b in range(N_ADA):
                    dve.wait_ge(ada_turned, i * N_ADA + b + 1)
                    dve.tensor_tensor(MODC[:, i * 96 + b * 8:i * 96 + b * 8 + 8].rearrange("p (m v) -> p m v", v=2),
                                      PS[:, 2 + (b + 1) % 2, 0:8].rearrange("p (m v) -> p m v", v=2),
                                      bias[:, i * 48 + b * 4:i * 48 + b * 4 + 4].rearrange("p (m o) -> p m o", o=1)
                                      .broadcast_to([P, 4, 2]), ALU.add).then_inc(ada_stored, 1)
            dve.drain()
            for n in range(4):
                lay, which = n // 2, n % 2
                g = prm("norm")[:, n * KD:(n + 1) * KD].rearrange("p (k o) -> p k o", o=1)
                m = KD * (3 * which + 1)
                dve.scalar_tensor_tensor(GAIN[:, n, :, :], mod[:, lay, m:m + KD, :], 1.0,
                                         g.broadcast_to([P, KD, 2]), ALU.add, ALU.mult)

        def sides_of(tiles):
            return ((1, 0), (0, SEG)) if 0 in tiles else ((0, SEG),)

        def norm_act(act, n, tiles):
            ev = norm_ev
            for t in tiles:
                act.activation(XN[:, t, :], X[:, t, :], ACT.Square, accum_out=SS[:, t:t + 1])
            act.drain()
            a, b = tiles[0], tiles[-1] + 1
            act.activation(RS[:, a:b], SS[:, a:b], ACT.Ln, scale=1.0 / D, bias=EPS[:, 0:1])
            act.drain()
            act.activation(RS[:, a:b], RS[:, a:b], ACT.Exp, scale=-0.5).then_inc(ev["rstd_ready"], 1)
            lay, m = n // 2, KD * 3 * (n % 2)
            for k in range(0, KD, 2):
                act.wait_ge(ev["xt_turned"], KD * n + k + 1)
                for v, c0 in sides_of(tiles):
                    act.activation(HT[:, k, c0:c0 + SEG], PS[:, k, c0:c0 + SEG], ACT.Identity,
                                   bias=mod[:, lay, m + k, v:v + 1], scale=GAIN[:, n, k, v:v + 1])

        def norm_dve(dve, n, tiles):
            ev = norm_ev
            dve.wait_ge(ev["rstd_ready"], n + 1)
            for t in tiles:
                dve.tensor_scalar(XN[:, t, :], X[:, t, :], RS[:, t:t + 1], None,
                                  ALU.mult).then_inc(ev["xn_ready"], 1)
            lay, m = n // 2, KD * 3 * (n % 2)
            for k in range(1, KD, 2):
                dve.wait_ge(ev["xt_turned"], KD * n + k + 1)
                for v, c0 in sides_of(tiles):
                    dve.tensor_scalar(HT[:, k, c0:c0 + SEG], PS[:, k, c0:c0 + SEG], GAIN[:, n, k, v:v + 1],
                                      mod[:, lay, m + k, v:v + 1], ALU.mult, ALU.add)

        def norm_pe(pe, n, tiles):
            ev = norm_ev
            pe.wait_ge(ev["xn_ready"], XN_BEFORE[n] + len(tiles))
            for k in range(KD):
                for t in tiles:
                    mm = pe.transpose(PS[:, k, t * P:t * P + P], XN[:, t, k * P:k * P + P], ident)
                mm.then_inc(ev["xt_turned"], 1)

        GATE = SCR[:, 0:2 * D].rearrange("p (v n) -> p v n", v=2)
        DIAG = SCR[:, 2 * D:4 * D].rearrange("p (v n) -> p v n", v=2)

        def gate_dve(dve, n, sides):
            lay, part = n // 2, 2 + 3 * (n % 2)
            for v in sides:
                for k in range(KD):
                    ins = dve.tensor_scalar(DIAG[:, v, k * P:k * P + P], ident,
                                            mod[:, lay, part * KD + k, v:v + 1], None, ALU.mult)
            ins.then_inc(gate_ev["gate_diag"], 1)

        def gate_pe(pe, n, sides):
            pe.wait_ge(gate_ev["gate_diag"], n + 1)
            for v in sides:
                for h in range(2):
                    mm = pe.matmul(PS[:, 2 * v + h, :], ones, DIAG[:, v, h * 512:h * 512 + 512], start=True, stop=True)
            mm.then_inc(gate_ev["gate_spread"], 1)

        def gate_act(act, n, sides):
            act.wait_ge(gate_ev["gate_spread"], n + 1)
            for v in sides:
                ins = act.activation(GATE[:, v, :].rearrange("p (h n) -> p h n", h=2), PS[:, 2 * v:2 * v + 2, :], ACT.Copy)
            ins.then_inc(gate_ev["gate_copied"], 1)

        def out_pe(pe, n, tiles, first_slot, ready, cat):
            ev = proj_ev
            for j, (t, h) in enumerate((t, h) for t in tiles for h in range(2)):
                if j < 2:
                    pe.wait_ge(w_ready[first_slot + j], ready[j])
                if j >= 4:
                    pe.wait_ge(ev["out_added"], OUT_BEFORE[n] + j - 3)
                for k in range(KD):
                    a = (t - tiles[0]) * P
                    mm = pe.matmul(PS[:, 4 + j % 4, :], cat[:, k, a:a + P], slots[:, first_slot + h, k, :],
                                   start=(k == 0), stop=(k == KD - 1))
                mm.then_inc(ev["out_done"], 1)

        def out_dve(dve, n, tiles):
            ev = proj_ev
            dve.wait_ge(gate_ev["gate_copied"], 2 * n + 1)
            TMP = SCR[:, 4096:8192].rearrange("p (b n) -> p b n", b=8)
            for j, (t, h) in enumerate((t, h) for t in tiles for h in range(2)):
                v = 1 if t < 2 else 0
                cols = slice(h * 512, h * 512 + 512)
                dve.wait_ge(ev["out_done"], OUT_BEFORE[n] + j + 1)
                dve.tensor_tensor(TMP[:, j, :], PS[:, 4 + j % 4, :], GATE[:, v, cols],
                                  ALU.mult).then_inc(ev["out_added"], 1)
                dve.wait_ge(ev["out_added"], OUT_BEFORE[n] + j + 1)
                dve.tensor_tensor(X[:, t, cols], X[:, t, cols], TMP[:, j, :], ALU.add)

        Y = XN
        LG = SCR[:, 0:64]
        GATES = sb("GATES", [P, NT, N_EXP])
        GCOL = sb("GCOL", [P, NT, 2])
        TH = SCR[:, 4096:5120].rearrange("p (b n) -> p b n", b=2)
        TG = SCR[:, 5120:6144].rearrange("p (b n) -> p b n", b=2)
        HID = SCR[:, 6144:8192].rearrange("p (f n) -> p f n", f=4)

        def router_pe(pe, n, tiles):
            for t in tiles:
                for k in range(KD):
                    mm = pe.matmul(PS[:, 7, t * 16:t * 16 + 16], HT[:, k, t * P:t * P + P],
                                   prm("router")[:, k * 16:k * 16 + 16], start=(k == 0), stop=(k == KD - 1))
            mm.then_inc(rt_ev["logits_done"], 1)

        def router_act(act, n, tiles):
            a, b = tiles[0] * 16, tiles[-1] * 16 + 16
            act.wait_ge(rt_ev["logits_done"], n + 1)
            act.activation(LG[:, a:b], PS[:, 7, a:b], ACT.Exp, scale=-1.0).then_inc(rt_ev["logits_exp"], 1)

        def router_dve(dve, n, tiles):
            drain = dve.drain
            nt = len(tiles)
            ng = nt * 4
            a = tiles[0] * 16
            w = SCR[:, 64:2048]
            sc, sel, ms, eq, key, o1, o2 = [x[:, a:a + nt * 16] for x in split(w, [64] * 7)]
            pr = w[:, 448:448 + ng * 6].rearrange("p (g c) -> p g c", c=6)
            gs = w[:, 640:640 + ng]
            geq, bg = w[:, 660:660 + ng], w[:, 680:680 + ng]
            m1 = w[:, 700:700 + nt]
            m2, m3 = w[:, 710:710 + nt], w[:, 720:720 + nt]

            def v3(ap, c):
                return ap.rearrange("p (t c) -> p t c", c=c)

            def wide(ap, m, c):
                return ap.rearrange("p (t o) -> p t o", o=1).broadcast_to([P, m, c])

            def narrow(ap, m, c):
                return ap.rearrange("p (o c) -> p o c", o=1).broadcast_to([P, m, c])

            dve.wait_ge(rt_ev["logits_exp"], n + 1)
            dve.tensor_scalar(sc, LG[:, a:a + nt * 16], 1.0, None, ALU.add)
            drain()
            dve.reciprocal(sc, sc)
            drain()
            dve.tensor_tensor(v3(sel, 16), v3(sc, 16), narrow(row("router_b"), nt, 16), ALU.add)
            drain()
            s4 = v3(sel, 4)
            dve.tensor_tensor(pr[:, :, 0:3], s4[:, :, 1:4], s4[:, :, 0:1].broadcast_to([P, ng, 3]), ALU.add)
            dve.tensor_tensor(pr[:, :, 3:5], s4[:, :, 2:4], s4[:, :, 1:2].broadcast_to([P, ng, 2]), ALU.add)
            dve.tensor_tensor(pr[:, :, 5:6], s4[:, :, 3:4], s4[:, :, 2:3], ALU.add)
            drain()
            dve.tensor_reduce(gs, pr, AX.X, ALU.max)
            drain()

            def one_hot(out, scores, c, weights, m):
                dve.tensor_reduce(m, v3(scores, c), AX.X, ALU.max)
                drain()
                e = geq if c == 4 else eq
                dve.tensor_tensor(v3(e, c), v3(scores, c), wide(m, nt, c), ALU.is_equal)
                drain()
                dve.tensor_tensor(v3(e, c), v3(e, c), narrow(weights, nt, c), ALU.mult)
                drain()
                dve.tensor_reduce(m2, v3(e, c), AX.X, ALU.max)
                drain()
                dve.tensor_tensor(v3(out, c), v3(e, c), wide(m2, nt, c), ALU.is_equal)
                drain()

            one_hot(bg, gs, 4, cst("first4"), m1)
            dve.tensor_tensor(v3(ms, 4), s4, wide(bg, ng, 4), ALU.mult)
            dve.tensor_scalar(geq, bg, -1.0, BIG, ALU.add, ALU.mult)
            drain()
            dve.tensor_tensor(v3(ms, 4), v3(ms, 4), wide(geq, ng, 4), ALU.add)
            drain()
            one_hot(o1, ms, 16, cst("first16"), m1)
            dve.tensor_scalar(key, o1, -2 * BIG, None, ALU.mult)
            drain()
            dve.tensor_tensor(ms, ms, key, ALU.add)
            drain()
            one_hot(o2, ms, 16, cst("first16"), m1)
            dve.tensor_tensor(o1, o1, o2, ALU.add)
            drain()
            dve.tensor_tensor(key, o1, sc, ALU.mult)
            drain()
            dve.tensor_reduce(m3, v3(key, 16), AX.X, ALU.add)
            drain()
            dve.reciprocal(m3, m3)
            drain()
            dve.tensor_tensor(GATES[:, tiles[0]:tiles[0] + nt, :], v3(key, 16), wide(m3, nt, 16), ALU.mult)
            for t in tiles:
                dve.memset(Y[:, t, :], 0.0)
            drain()

        EXPERT_SLOTS = ((2, 3, 4), (5, 0, 1))

        def moe_pe(pe, n, tiles, ready):
            ev = moe_ev
            hb, db = HIDDEN_BEFORE[n], DOWN_BEFORE[n]
            a = tiles[0] * P
            width = len(tiles) * P
            outs = [(t, h) for t in tiles for h in range(2)]
            no = len(outs)
            def expert(i, e, first):
                g, u, dn = EXPERT_SLOTS[e]
                for f in range(4):
                    if f == 0:
                        pe.wait_ge(w_ready[g], i * 16 + ready[g] + 16)
                        pe.wait_ge(w_ready[u], i * 16 + ready[u] + 16)
                    c = 4 * e + f
                    if not (first and c < 2):
                        pe.wait_ge(ev["hidden_done"], i * 8 + hb + c - 1)
                    for bank, s in ((2 * (f % 2), g), (2 * (f % 2) + 1, u)):
                        for k in range(KD):
                            mm = pe.matmul(PS[:, bank, 0:width], slots[:, s, k, f * P:f * P + P],
                                           HT[:, k, a:a + width], start=(k == 0), stop=(k == KD - 1))
                    mm.then_inc(ev["gateup_done"], 1)
                pe.wait_ge(ev["hidden_done"], i * 8 + hb + 4 * e + 4)
                pe.wait_ge(w_ready[dn], i * 16 + ready[dn] + 16)
                wd = slots[:, dn, :, :].rearrange("p (f h) n -> p f h n", h=2)
                for j, (t, h) in enumerate(outs):
                    c = no * e + j
                    if not (first and c < 4):
                        pe.wait_ge(ev["y_added"], i * 2 * no + db + c - 3)
                    for f in range(4):
                        mm = pe.matmul(PS[:, 4 + j % 4, :], HID[:, f, t * P - a:t * P - a + P], wd[:, f, h, :],
                                       start=(f == 0), stop=(f == 3))
                    mm.then_inc(ev["down_done"], 1)

            expert(0, 0, True)
            expert(0, 1, False)
            with pe.Fori(1, N_EXP // 2) as i:
                expert(i, 0, False)
                expert(i, 1, False)

        def moe_act(act, n, tiles):
            ev = moe_ev
            hb, db = HIDDEN_BEFORE[n], DOWN_BEFORE[n]
            width = len(tiles) * P

            def expert(i, e, first):
                for f in range(4):
                    c = 4 * e + f
                    act.wait_ge(ev["gateup_done"], i * 8 + hb + c + 1)
                    if not (first and c < 2):
                        act.wait_ge(ev["hidden_done"], i * 8 + hb + c - 1)
                    act.activation(TH[:, f % 2, 0:width], PS[:, 2 * (f % 2), 0:width], ACT.Tanh,
                                   scale=0.5).then_inc(ev["tanh_done"], 1)

            expert(0, 0, True)
            expert(0, 1, False)
            with act.Fori(1, N_EXP // 2) as i:
                expert(i, 0, False)
                expert(i, 1, False)

        def moe_dve(dve, n, tiles):
            ev = moe_ev
            hb, db = HIDDEN_BEFORE[n], DOWN_BEFORE[n]
            width = len(tiles) * P
            outs = [(t, h) for t in tiles for h in range(2)]
            no = len(outs)
            with dve.Fori(0, N_EXP // 2) as i:
                dve.drain()
                dve.tensor_copy(GCOL[:], GATES[:, :, ds(i * 2, 2)])
                for e in range(2):
                    for f in range(4):
                        dve.wait_ge(ev["tanh_done"], i * 8 + hb + 4 * e + f + 1)
                        dve.scalar_tensor_tensor(TG[:, f % 2, 0:width], TH[:, f % 2, 0:width], 1.0,
                                                 PS[:, 2 * (f % 2), 0:width], ALU.add, ALU.mult)
                        dve.drain()
                        dve.scalar_tensor_tensor(HID[:, f, 0:width], TG[:, f % 2, 0:width], 0.5,
                                                 PS[:, 2 * (f % 2) + 1, 0:width], ALU.mult,
                                                 ALU.mult).then_inc(ev["hidden_done"], 1)
                    for j, (t, h) in enumerate(outs):
                        dve.wait_ge(ev["down_done"], i * 2 * no + db + no * e + j + 1)
                        y = Y[:, t, h * 512:h * 512 + 512]
                        dve.scalar_tensor_tensor(y, PS[:, 4 + j % 4, :], GCOL[:, t, e:e + 1], y, ALU.mult,
                                                 ALU.add).then_inc(ev["y_added"], 1)
            dve.drain()

        def moe_end_dve(dve, n, tiles):
            dve.wait_ge(gate_ev["gate_copied"], 2 * n + 2)
            for t in tiles:
                dve.tensor_tensor(Y[:, t, :], Y[:, t, :], GATE[:, 1 if t < 2 else 0, :], ALU.mult)
            dve.drain()
            for t in tiles:
                dve.tensor_tensor(X[:, t, :], X[:, t, :], Y[:, t, :], ALU.add)

        ADA_BASE = [0] * NSLOT
        EVEN_BASE = [64] * NSLOT
        OUT0_READY = [64 + 96 + 16, 64 + 64 + 16]
        MOE0_BASE = [OUT0_READY[0], OUT0_READY[1], 64 + 96, 64, 64, 64]
        MOE_FILLS = 16 * N_EXP // 2
        ODD_BASE = [b + MOE_FILLS for b in MOE0_BASE]

        ESC = slots[:, 3:6, :, :].rearrange("p s k n -> p (s k n)")
        eU, eS, eATT, eQK, eO = split(ESC, [4096, 4096, 2048, 1024, 1024])
        U3 = eU.rearrange("p (n e) -> p n e", n=NCH)
        S3 = eS.rearrange("p (n e) -> p n e", n=NCH)
        ATT4 = eATT.rearrange("p (h t q) -> p h t q", h=4, t=NT)
        QK = eQK.rearrange("p (a n) -> p a n", a=2)
        O3 = eO.rearrange("p (t n) -> p t n", t=NT)
        gVG, gA, gC, gG, gQH, gKH, gKT, gF, gW = split(SCR[:, :], [2048, 1024, 1024, 1024, 1024, 1024, 512, 128, 260])
        VG = gVG.rearrange("p (t n) -> p t n", t=NT)
        A2, C2, G2, QH, KH = [b.rearrange("p (d n) -> p d n", d=2) for b in (gA, gC, gG, gQH, gKH)]
        ZD = QH
        F3 = gF[:, 0:32].rearrange("p (d n) -> p d n", d=2)
        DN = gF[:, 32:64].rearrange("p (d n) -> p d n", d=2)
        GW = gW
        gla = {k: sem(f"gla_{k}") for k in (
            "small", "abs", "proj", "qkv_stored", "zd", "logits", "soft", "expo", "exp", "kh", "kturned", "ktok", "ds",
            "ds_masked", "states", "att", "att_masked", "out", "out_stored", "ss", "rstd", "cat")}
        att = {k: sem(f"att_{k}") for k in (
            "proj", "stored", "ss", "rstd", "qk", "turned", "tstored", "scores", "max", "exp", "es", "pturned",
            "pt_stored", "pv", "out")}
        even_part = sem("even_part")
        aAQ, aSQ, aQT, aP, aPT, aR, aM = split(ESC, [1536, 1280, 2560, 1024, 1024, 1280, 128])
        AQ = aAQ.rearrange("p (t n) -> p t n", t=NT)
        SQ = aSQ.rearrange("p (t n) -> p t n", t=NT)
        QT = aQT.rearrange("p (h n) -> p h n", h=5)
        PB = aP.rearrange("p (b n) -> p b n", b=2)
        PTB = aPT.rearrange("p (b n) -> p b n", b=2)
        RT = [r.rearrange("p (t h n) -> p t h n", t=2, h=5) for r in split(aR, [320] * 4)]
        aMX, aNM, aRS, aES, aRD, aSK = split(aM, [16] * 5 + [4])
        ORD = (list(range(NCH)), list(range(NCH // 2 - 1, -1, -1)) + list(range(NCH - 1, NCH // 2 - 1, -1)))

        def gla_pe(pe, i, base):
            def w_wait(s, n, per):
                pe.wait_ge(w_ready[s], i * per + base[s] + n)

            w_wait(0, 48, 48)
            for a in range(2):
                for k in range(KD):
                    mm = pe.matmul(PS[:, a, :], slots[:, 0, k, a * P:a * P + P], HT[:, k, :],
                                   start=(k == 0), stop=(k == KD - 1))
                mm.then_inc(gla["proj"], 1)
            w_wait(1, 32, 32)
            for d in range(2):
                for k in range(KD):
                    mm = pe.matmul(PS[0:16, 2 + d, :], slots[:, 1, k, 256 + 16 * d:272 + 16 * d], HT[:, k, :],
                                   start=(k == 0), stop=(k == KD - 1))
            mm.then_inc(gla["proj"], 1)
            for t in range(NT):
                for s, c0 in ((0, 256), (1, 0)):
                    for k in range(KD):
                        mm = pe.matmul(PS[:, 4 + t, 256 * s:256 * s + 256], HT[:, k, t * P:t * P + P],
                                       slots[:, s, k, c0:c0 + 256], start=(k == 0), stop=(k == KD - 1))
                mm.then_inc(gla["proj"], 1)
            pe.wait_ge(gla["small"], 16 * i + 16)
            pe.wait_ge(gla["zd"], i + 1)
            for d in range(2):
                mm = pe.matmul(PS[:, 2 + d, :], GW[0:16, d * P:d * P + P], ZD[0:16, d, :], start=True, stop=True)
            mm.then_inc(gla["logits"], 1)
            pe.wait_ge(gla["qkv_stored"], 6 * i + 6)
            pe.wait_ge(gla["kh"], i + 1)
            for d in range(2):
                if d == 1:
                    pe.wait_ge(gla["att_masked"], 2 * i + 1)
                for t in range(NT):
                    mm = pe.transpose(PS[:, 0, t * P:t * P + P], KH[:, d, t * P:t * P + P], ident)
                mm.then_inc(gla["kturned"], 1)
                if d == 1:
                    pe.wait_ge(gla["out_stored"], 8 * i + 4)
                pe.wait_ge(gla["ktok"], 2 * i + d + 1)
                for pr in range(2):
                    if pr == 1:
                        pe.wait_ge(gla["ds_masked"], 4 * i + 2 * d + 1)
                    for c in range(4):
                        for tt in range(2):
                            t = 2 * pr + tt
                            mm = pe.matmul(PS[:, 4 + c, tt * 256:tt * 256 + 256], gKT[32 * c:32 * c + 32, t * P:t * P + P],
                                           VG[32 * c:32 * c + 32, t, 0:256], start=True, stop=True)
                    mm.then_inc(gla["ds"], 1)
                for h in range(4):
                    for t in range(NT):
                        mm = pe.matmul(PS[:, h, t * P:t * P + P], KH[32 * h:32 * h + 32, d, t * P:t * P + P],
                                       QH[32 * h:32 * h + 32, d, t * P:t * P + P], start=True, stop=True)
                mm.then_inc(gla["att"], 1)
                pe.wait_ge(gla["states"], 2 * i + d + 1)
                pe.wait_ge(gla["att_masked"], 2 * i + d + 1)
                for t in range(NT):
                    for c in range(4):
                        pe.matmul(PS[32 * c:32 * c + 32, 4 + t, 0:256], QH[:, d, t * P + 32 * c:t * P + 32 * c + 32],
                                  S3[:, 4 * t + c, :], start=True, stop=False, skip_group_check=True)
                    for h in range(4):
                        mm = pe.matmul(PS[:, 4 + t, 64 * h:64 * h + 64], ATT4[:, h, t, :],
                                       VG[:, t, 64 * h:64 * h + 64], start=False, stop=(h == 3), skip_group_check=True)
                    mm.then_inc(gla["out"], 1)

        def gla_act(act, i):
            for a in range(2):
                act.wait_ge(gla["proj"], 7 * i + a + 1)
                act.activation(QK[:, a, :], PS[:, a, :], ACT.Copy,
                               scale=GLA_DK ** -0.5 if a == 0 else 1.0).then_inc(gla["qkv_stored"], 1)
            for t in range(NT):
                act.wait_ge(gla["proj"], 7 * i + 4 + t)
                act.activation(VG[:, t, :], PS[:, 4 + t, :], ACT.Copy).then_inc(gla["qkv_stored"], 1)
            act.wait_ge(gla["logits"], i + 1)
            act.wait_ge(gla["small"], 16 * i + 16)
            for d in range(2):
                act.activation(A2[:, d, :], PS[:, 2 + d, :], ACT.Abs,
                               bias=GW[:, 256 + d:257 + d]).then_inc(gla["abs"], 1)
            act.drain()
            act.activation(gA, gA, ACT.Exp, scale=-1.0)
            act.drain()
            act.activation(gA, gA, ACT.Ln, bias=1.0).then_inc(gla["soft"], 1)
            act.wait_ge(gla["expo"], i + 1)
            act.activation(gQH, gA, ACT.Exp, scale=1.0 / GLA_TAU)
            act.activation(gKH, gA, ACT.Exp, scale=-1.0 / GLA_TAU)
            act.activation(gF[:, 0:32], gF[:, 0:32], ACT.Exp, scale=1.0 / GLA_TAU).then_inc(gla["exp"], 1)
            for d in range(2):
                act.wait_ge(gla["kturned"], 2 * i + d + 1)
                if d == 1:
                    act.wait_ge(gla["ds"], 4 * i + 2)
                act.activation(gKT, PS[:, 0, :], ACT.Copy).then_inc(gla["ktok"], 1)
            act.wait_ge(gla["ss"], i + 1)
            act.activation(RS[:, 0:16], SS[:, 0:16], ACT.Ln, scale=1.0 / GLA_DV, bias=EPS[:, 0:1])
            act.drain()
            act.activation(RS[:, 0:16], RS[:, 0:16], ACT.Exp, scale=-0.5)
            act.activation(gKH.rearrange("p (t n) -> p t n", t=NT), VG[:, :, 256:512], ACT.Tanh,
                           scale=0.5).then_inc(gla["rstd"], 1)

        def gla_dve(dve, i):
            drain = dve.drain
            dve.wait_ge(gla["proj"], 7 * i + 3)
            dve.tensor_copy(ZD[0:16, :, :], PS[0:16, 2:4, :]).then_inc(gla["zd"], 1)
            dve.wait_ge(gla["small"], 16 * i + 16)
            dve.wait_ge(gla["abs"], 2 * i + 2)
            for d in range(2):
                dve.tensor_scalar(G2[:, d, :], PS[:, 2 + d, :], GW[:, 256 + d:257 + d], 0.0, ALU.add, ALU.min)
            drain()
            dve.wait_ge(gla["soft"], i + 1)
            dve.tensor_tensor(gG, gG, gA, ALU.subtract)
            drain()
            for d in range(2):
                dve.tensor_tensor_scan(C2[:, d, :], cst("reset32"), G2[:, d, :], 0.0, ALU.mult, ALU.add)
            drain()
            cv = gC.rearrange("p (n s) -> p n s", s=GLA_C)
            dve.tensor_tensor(gA.rearrange("p (n s) -> p n s", s=GLA_C), cv,
                              cv[:, :, 15:16].broadcast_to([P, 2 * NCH, GLA_C]), ALU.subtract)
            c4 = gC.rearrange("p (d n s) -> p d n s", d=2, s=GLA_C)
            dve.tensor_tensor(DN, c4[:, :, :, 31], c4[:, :, :, 15], ALU.subtract)
            drain()
            dve.tensor_tensor(A2[:, 1, :], G2[:, 1, :], A2[:, 1, :], ALU.subtract)
            n = NCH - 1
            dve.memset(F3[:, 0, n:NCH], 0.0)
            dve.tensor_tensor(F3[:, 0, 0:n], DN[:, 0, 0:n], c4[:, 0, 1:NCH, 15], ALU.add)
            dve.tensor_tensor(F3[:, 1, 1:NCH], DN[:, 1, 0:n], c4[:, 1, 1:NCH, 15], ALU.add)
            dve.tensor_tensor(F3[:, 1, 0:1], DN[:, 1, n:NCH], c4[:, 1, 0:1, 15], ALU.add)
            drain()
            dve.tensor_scalar(gA, gA, 85.0 * GLA_TAU, -85.0 * GLA_TAU, ALU.min, ALU.max).then_inc(gla["expo"], 1)
            dve.wait_ge(gla["exp"], i + 1)
            dve.wait_ge(gla["qkv_stored"], 6 * i + 6)
            for d in range(2):
                dve.tensor_tensor(QH[:, d, :], QH[:, d, :], QK[:, 0, :], ALU.mult)
                ins = dve.tensor_tensor(KH[:, d, :], KH[:, d, :], QK[:, 1, :], ALU.mult)
            ins.then_inc(gla["kh"], 1)
            heads = cst("gla_heads").rearrange("p (o e) -> p o e", o=1).broadcast_to([P, 2, 256])
            for d in range(2):
                u4 = eU.rearrange("p (t c e) -> p t c e", t=NT, c=4)
                for pr in range(2):
                    dve.wait_ge(gla["ds"], 4 * i + 2 * d + pr + 1)
                    for c in range(4):
                        ins = dve.tensor_tensor(u4[:, 2 * pr:2 * pr + 2, c, :],
                                                PS[:, 4 + c, :].rearrange("p (t e) -> p t e", t=2), heads, ALU.mult)
                    ins.then_inc(gla["ds_masked"], 1)
                dve.memset(S3[:, ORD[d][0], :], 0.0)
                drain()
                for a, n in zip(ORD[d], ORD[d][1:]):
                    f = F3[:, d, a:a + 1]
                    dve.tensor_scalar(S3[:, n, :], U3[:, a, :], f, None, ALU.mult)
                    dve.scalar_tensor_tensor(U3[:, n, :], U3[:, a, :], f, U3[:, n, :], ALU.mult, ALU.add)
                    drain()
                drain().then_inc(gla["states"], 1)
                dve.wait_ge(gla["att"], 2 * i + d + 1)
                mask = (cst("gla_incl")[:, d * P:d * P + P].rearrange("p (o q) -> p o q", o=1)
                        .broadcast_to([P, NT, P]))
                for h in range(4):
                    ins = dve.tensor_tensor(ATT4[:, h, :, :], PS[:, h, :].rearrange("p (t q) -> p t q", t=NT),
                                            mask, ALU.mult)
                ins.then_inc(gla["att_masked"], 1)
                for t in range(NT):
                    dve.wait_ge(gla["out"], 8 * i + 4 * d + t + 1)
                    if d == 0:
                        dve.tensor_copy(O3[:, t, :], PS[:, 4 + t, 0:256]).then_inc(gla["out_stored"], 1)
                    else:
                        dve.tensor_tensor(O3[:, t, :], O3[:, t, :], PS[:, 4 + t, 0:256],
                                          ALU.add).then_inc(gla["out_stored"], 1)
                drain()
            o16 = eO.rearrange("p (g e) -> p g e", e=GLA_DV)
            q16 = gQH.rearrange("p (g e) -> p g e", e=GLA_DV)
            dve.tensor_tensor(gQH, eO, eO, ALU.mult)
            drain()
            dve.tensor_reduce(SS[:, 0:16], q16, AX.X, ALU.add).then_inc(gla["ss"], 1)
            dve.wait_ge(gla["rstd"], i + 1)
            dve.tensor_tensor(o16, o16, RS[:, 0:16].rearrange("p (g o) -> p g o", o=1).broadcast_to([P, 16, GLA_DV]),
                              ALU.mult)
            dve.scalar_tensor_tensor(QH[:, :, :].rearrange("p d (t n) -> p (d t) n", t=2),
                                     gKH.rearrange("p (t n) -> p t n", t=NT), 1.0, VG[:, :, 256:512], ALU.add, ALU.mult)
            drain()
            dve.tensor_tensor(o16, o16, row("gla_gain").rearrange("p (o e) -> p o e", o=1).broadcast_to([P, 16, GLA_DV]),
                              ALU.mult)
            drain()
            dve.scalar_tensor_tensor(XN[:, :, ds(i * 256, 256)], O3, 0.5,
                                     gQH.rearrange("p (t n) -> p t n", t=NT), ALU.mult, ALU.mult)

        UNITS = [(h, t) for h in range(GRP) for t in range(NT)]
        NU = len(UNITS)

        def att_pe(pe, i, base):
            pe.wait_ge(w_ready[2], i * 48 + base[2] + 48)
            for t in range(NT):
                for k in range(KD):
                    mm = pe.matmul(PS[:, t, 0:384], HT[:, k, t * P:t * P + P], slots[:, 2, k, 0:384],
                                   start=(k == 0), stop=(k == KD - 1))
                mm.then_inc(att["proj"], 1)
            pe.wait_ge(att["qk"], i + 1)
            for h in range(5):
                for t in range(NT):
                    src, dst = AQ[:, t, h * HD:h * HD + HD], PS[0:HD, (4 + h) % 8, t * P:t * P + P]
                    if h == 0 and t == 0:
                        mm = pe.matmul(dst, src, ident, start=True, stop=True)
                    else:
                        mm = pe.transpose(dst, src, ident)
                mm.then_inc(att["turned"], 1)
            pe.wait_ge(att["tstored"], 5 * i + 5)
            for u in range(NU + 2):
                if u < NU:
                    h, t = UNITS[u]
                    nk = T if t >= 2 else SEG
                    if u >= 2:
                        pe.wait_ge(att["exp"], NU * i + u - 1)
                    pe.matmul(PS[:, u % 2, 0:nk], QT[0:HD, h, t * P:t * P + P], QT[0:HD, 4, 0:nk], start=True,
                              stop=True).then_inc(att["scores"], 1)
                if 1 <= u <= NU:
                    v = u - 1
                    pe.wait_ge(att["exp"], NU * i + v + 1)
                    if v >= 2:
                        pe.wait_ge(att["pt_stored"], NU * i + v - 1)
                    for c in range(4 if UNITS[v][1] >= 2 else 2):
                        mm = pe.transpose(PS[:, 2 + v % 2, c * P:c * P + P], PB[:, v % 2, c * P:c * P + P], ident)
                    mm.then_inc(att["pturned"], 1)
                if u >= 2:
                    v = u - 2
                    pe.wait_ge(att["pt_stored"], NU * i + v + 1)
                    if v >= 2:
                        pe.wait_ge(att["out"], NU * i + v - 1)
                    nt = 4 if UNITS[v][1] >= 2 else 2
                    for c in range(nt):
                        mm = pe.matmul(PS[:, 4 + v % 2, 0:HD], PTB[:, v % 2, c * P:c * P + P], AQ[:, c, 320:384],
                                       start=(c == 0), stop=(c == nt - 1))
                    mm.then_inc(att["pv"], 1)

        def att_act(act, i):
            for t in range(NT):
                act.wait_ge(att["proj"], NT * i + t + 1)
                act.activation(AQ[:, t, :], PS[:, t, 0:384], ACT.Copy).then_inc(att["stored"], 1)
            act.wait_ge(att["ss"], i + 1)
            act.activation(RS[:, 0:20], SS[:, 0:20], ACT.Ln, scale=1.0 / HD, bias=EPS[:, 0:1])
            act.drain()
            act.activation(RS[:, 0:20], RS[:, 0:20], ACT.Exp, scale=-0.5).then_inc(att["rstd"], 1)
            for h in range(5):
                act.wait_ge(att["turned"], 5 * i + h + 1)
                act.activation(QT[0:HD, h, :], PS[0:HD, (4 + h) % 8, :], ACT.Copy).then_inc(att["tstored"], 1)
            for u in range(NU + 1):
                if u < NU:
                    h, t = UNITS[u]
                    nk = T if t >= 2 else SEG
                    act.wait_ge(att["max"], NU * i + u + 1)
                    if u >= 2:
                        act.wait_ge(att["pturned"], NU * i + u - 1)
                    act.activation(PB[:, u % 2, 0:nk], PS[:, u % 2, 0:nk], ACT.Exp, scale=HD ** -0.5,
                                   bias=aNM[:, u:u + 1], accum_out=aRS[:, u:u + 1]).then_inc(att["exp"], 1)
                    act.activation(aES[:, u:u + 1], aSK[:, h:h + 1], ACT.Exp, bias=aNM[:, u:u + 1]).then_inc(att["es"], 1)
                if u >= 1:
                    v = u - 1
                    nk = T if UNITS[v][1] >= 2 else SEG
                    act.wait_ge(att["pturned"], NU * i + v + 1)
                    if v >= 2:
                        act.wait_ge(att["pv"], NU * i + v - 1)
                    act.activation(PTB[:, v % 2, 0:nk], PS[:, 2 + v % 2, 0:nk], ACT.Copy).then_inc(att["pt_stored"], 1)

        def att_dve(dve, i):
            drain = dve.drain
            dve.tensor_copy(aSK, row("sink")[:, ds(i * GRP, GRP)])
            dve.wait_ge(att["stored"], NT * i + NT)
            qk = AQ[:, :, 0:320]
            dve.tensor_tensor(SQ, qk, qk, ALU.mult)
            drain()
            dve.tensor_reduce(SS[:, 0:20], aSQ.rearrange("p (g e) -> p g e", e=HD), AX.X, ALU.add).then_inc(att["ss"], 1)
            dve.wait_ge(att["rstd"], i + 1)
            for t in range(NT):
                a3 = AQ[:, t, 0:320].rearrange("p (h e) -> p h e", h=5)
                dve.tensor_tensor(a3, a3, RS[:, 5 * t:5 * t + 5].rearrange("p (h o) -> p h o", o=1)
                                  .broadcast_to([P, 5, HD]), ALU.mult)
            drain()
            dve.tensor_tensor(qk, qk, row("qk_gain").rearrange("p (o n) -> p o n", o=1).broadcast_to([P, NT, 320]),
                              ALU.mult)
            drain()
            r4 = cst("rope").rearrange("p (c t n) -> p c t n", c=2, t=2)
            for t in range(2):
                a3 = AQ[:, 2 + t, 0:320].rearrange("p (h e) -> p h e", h=5)
                a, b = a3[:, :, 0:32], a3[:, :, 32:64]
                c, s = [r4[:, x, t, :].rearrange("p (o n) -> p o n", o=1).broadcast_to([P, 5, 32]) for x in range(2)]
                for buf, u, v in ((0, a, c), (1, b, s), (2, a, s), (3, b, c)):
                    dve.tensor_tensor(RT[buf][:, t, :, :], u, v, ALU.mult)
            drain()
            for t in range(2):
                a3 = AQ[:, 2 + t, 0:320].rearrange("p (h e) -> p h e", h=5)
                dve.tensor_tensor(a3[:, :, 0:32], RT[0][:, t, :, :], RT[1][:, t, :, :], ALU.subtract)
                ins = dve.tensor_tensor(a3[:, :, 32:64], RT[2][:, t, :, :], RT[3][:, t, :, :], ALU.add)
            ins.then_inc(att["qk"], 1)
            for u in range(NU + 2):
                if u < NU:
                    h, t = UNITS[u]
                    nk = T if t >= 2 else SEG
                    dve.wait_ge(att["scores"], NU * i + u + 1)
                    if t >= 2:
                        kt = 5 - t
                        blk = PS[:, u % 2, kt * P:kt * P + P]
                        dve.tensor_tensor(blk, blk, cst("att_mask")[:, (t - 2) * P:(t - 1) * P], ALU.add)
                        drain()
                    dve.tensor_reduce(aMX[:, u:u + 1], PS[:, u % 2, 0:nk], AX.X, ALU.max)
                    drain()
                    dve.tensor_scalar(aMX[:, u:u + 1], aMX[:, u:u + 1], HD ** -0.5, aSK[:, h:h + 1], ALU.mult, ALU.max)
                    drain()
                    dve.tensor_scalar(aNM[:, u:u + 1], aMX[:, u:u + 1], -1.0, None, ALU.mult).then_inc(att["max"], 1)
                if u >= 2:
                    v = u - 2
                    h, t = UNITS[v]
                    dve.wait_ge(att["es"], NU * i + v + 1)
                    dve.tensor_tensor(aRD[:, v:v + 1], aRS[:, v:v + 1], aES[:, v:v + 1], ALU.add)
                    drain()
                    dve.reciprocal(aRD[:, v:v + 1], aRD[:, v:v + 1])
                    drain()
                    dve.wait_ge(att["pv"], NU * i + v + 1)
                    dve.tensor_scalar(XN[:, t, ds(i * 256 + 512 + h * HD, HD)], PS[:, 4 + v % 2, 0:HD],
                                      aRD[:, v:v + 1], None, ALU.mult).then_inc(att["out"], 1)

        def turn_pe(pe):
            for k in range(KD):
                for t in range(NT):
                    mm = pe.transpose(PS[:, k, t * P:t * P + P], XN[:, t, k * P:k * P + P], ident)
                mm.then_inc(cat_turned_k, 1)

        def turn_copy(eng, ks):
            for k in ks:
                eng.wait_ge(cat_turned_k, k + 1)
                if eng.engine == nc.scalar.engine:
                    eng.activation(HT[:, k, :], PS[:, k, :], ACT.Copy)
                else:
                    eng.tensor_copy(HT[:, k, :], PS[:, k, :])

        def turned_meet(eng):
            eng.drain().then_inc(cat_turned, 1)
            eng.wait_ge(cat_turned, ENGINES)

        L2 = SEG
        ODD1 = slots[:, 1, :, :].rearrange("p k n -> p (k n)")
        ODD45 = slots[:, 4:6, :, :].rearrange("p s k n -> p (s k n)")
        XNF = XN[:].rearrange("p t n -> p (t n)")
        CATT, oTW, oZA, oSG, oPV, oPD, oLW, oBON = split(XNF, [KD * L2, T, T, L2, 12, 12, 384, L2])
        oG, oC, oE, oB, oKD, oPP, oPX, oS, oWS, oUS, oRZ, oF = split(
            SCR[:, :], [2 * T] * 6 + [T, 256, 256, 256, L2, 32])
        oXT, oMK, oNN, oTA = split(ODD45, [2048, 2048, 2048, 2048])
        oTB, oKZ, oVZ, oKK, oVT = split(ODD1, [2048, T, T, T, T])
        G_, C_, E_, B_, KD_, PP_, PX_ = [b.rearrange("p (d n) -> p d n", d=2) for b in (oG, oC, oE, oB, oKD, oPP, oPX)]
        BT_, KT_ = E_, G_
        ST_, WS_, US_ = [b.rearrange("p (d n) -> p d n", d=2) for b in (oS, oWS, oUS)]
        XT_, MK_, NN_ = [b.rearrange("p (d h c n) -> p d h c n", d=2, h=2, c=4) for b in (oXT, oMK, oNN)]
        LTS, XX, MT, T1 = zip(*[[x.rearrange("p (c n) -> p c n", c=4) for x in split(b, [512] * 4)] for b in (oTA, oTB)])
        ZP = [b.rearrange("p (s n) -> p s n", s=2) for b in split(oTA, [516, 516, 516])]
        MIXT, AVG = split(oTB, [512, 512])
        FZ = oXT[:, 0:512].rearrange("p (t n) -> p t n", t=2)
        FB = oMK[:, 0:1024].rearrange("p (m n) -> p m n", m=2)
        oMID, oDN, oFF = [x.rearrange("p (d c) -> p d c", d=2) for x in split(oF, [8, 8, 8])]
        pre = {k: sem(f"pre_{k}") for k in ("proj", "stored", "mixed", "four", "four_stored", "four_tok",
                                            "four_tok_stored", "four_ch")}
        rw = {k: sem(f"rw_{k}") for k in (
            "small", "derived", "proj", "lora", "zp", "tanh_w", "tanh_a", "sq", "kksum", "kkrs", "v", "vturned",
            "vstored", "expo", "exps", "hat", "tok", "tok_stored", "gram", "lt", "gram_read", "mt", "t1",
            "t1s", "p", "x", "w", "ws", "u", "us", "ds", "s", "y", "yb", "mean", "ysq", "var", "rstd", "bonus", "g2")}
        odd_part = sem("odd_part")
        RORD = ((0, 1, 2, 3), (1, 0, 3, 2))
        NL = len(LEVELS)

        def odd_meet(eng, value):
            eng.drain().then_inc(odd_part, 1)
            eng.wait_ge(odd_part, value)

        def odd_pre_pe(pe):
            pe.wait_ge(w_ready[2], ODD_BASE[2] + 16)
            for x in range(3):
                c0 = L2 if x == 2 else 0
                for k in range(KD):
                    mm = pe.matmul(PS[:, x, c0:T], slots[:, 2, k, x * P:x * P + P], HT[:, k, c0:T],
                                   start=(k == 0), stop=(k == KD - 1))
                mm.then_inc(pre["proj"], 1)
            pe.wait_ge(w_ready[3], ODD_BASE[3] + 16)
            for t in range(2):
                for k in range(KD):
                    mm = pe.matmul(PS[:, 3 + t, 0:FOUR], HT[:, k, L2 + t * P:L2 + t * P + P], slots[:, 3, k, 0:FOUR],
                                   start=(k == 0), stop=(k == KD - 1))
            mm.then_inc(pre["four"], 1)
            pe.wait_ge(pre["four_stored"], 1)
            tok = cst("dft_tok").rearrange("p (t n) -> p t n", t=2)
            for m in range(2):
                for t in range(2):
                    mm = pe.matmul(PS[:, 5 + m, :], FZ[:, t, m * P:m * P + P], tok[:, t, :],
                                   start=(t == 0), stop=(t == 1))
            mm.then_inc(pre["four_tok"], 1)
            pe.wait_ge(pre["four_tok_stored"], 1)
            for m in range(2):
                for s in range(2):
                    mm = pe.matmul(PS[:, 7, m * L2:m * L2 + L2], cst("dft_ch")[:, s * P:s * P + P],
                                   FB[:, m, s * L2:s * L2 + L2], start=(s == 0), stop=(s == 1))
            mm.then_inc(pre["four_ch"], 1)

        def odd_pre_act(act):
            for x in range(3):
                s0 = 1 if x == 2 else 0
                act.wait_ge(pre["proj"], x + 1)
                act.activation(ZP[x][:, s0:2, 1:L2 + 1], PS[:, x, s0 * L2:T].rearrange("p (s n) -> p s n", n=L2),
                               ACT.Copy).then_inc(pre["stored"], 1)
            act.wait_ge(pre["four"], 1)
            act.activation(FZ, PS[:, 3:5, 0:FOUR], ACT.Copy).then_inc(pre["four_stored"], 1)
            act.wait_ge(pre["four_tok"], 1)
            act.activation(FB, PS[:, 5:7, :], ACT.Copy).then_inc(pre["four_tok_stored"], 1)
            act.wait_ge(pre["four_ch"], 1)
            act.activation(CATT[:, 0:2 * L2], PS[:, 7, :], ACT.Copy)
            act.wait_ge(pre["mixed"], 1)
            act.activation(oTW, oTW, ACT.Tanh)
            act.activation(oSG, oSG, ACT.Tanh, scale=0.5)

        def shift_mix(dve, out, zp, s0, mu_half, one_mu):
            n = 2 - s0
            t3 = MIXT[:, 0:n * L2].rearrange("p (s n) -> p s n", n=L2)
            a3 = AVG[:, 0:n * L2].rearrange("p (s n) -> p s n", n=L2)
            dve.tensor_scalar(t3, zp[:, s0:2, 1:L2 + 1], one_mu, None, ALU.mult)
            dve.tensor_tensor(a3, zp[:, s0:2, 0:L2], zp[:, s0:2, 2:L2 + 2], ALU.add)
            dve.drain()
            return dve.scalar_tensor_tensor(out.rearrange("p (s n) -> p s n", n=L2), a3, mu_half, t3, ALU.mult, ALU.add)

        def zero_edges(dve):
            for z in ZP:
                dve.memset(z[:, :, 0:1], 0.0)
                dve.memset(z[:, :, L2 + 1:L2 + 2], 0.0)

        def odd_pre_dve(dve):
            zero_edges(dve)
            mu = prm("lora_mu")
            dve.tensor_scalar(oPD[:, 0:3], mu, 0.5, None, ALU.mult)
            dve.tensor_scalar(oPD[:, 3:6], mu, -1.0, 1.0, ALU.mult, ALU.add)
            dve.wait_ge(pre["stored"], 3)
            dve.drain()
            for x, dst in enumerate((oTW, oZA, oSG)):
                ins = shift_mix(dve, dst, ZP[x], 1 if x == 2 else 0, oPD[:, x:x + 1], oPD[:, 3 + x:4 + x])
                dve.drain()
            dve.drain().then_inc(pre["mixed"], 1)

        def pair_pe(pe, i):
            pe.wait_ge(w_ready[0], i * 48 + ODD_BASE[0] + 48)
            for x, bank in ((1, 1), (2, 2), (0, 0)):
                c0 = L2 if x == 0 else 0
                for k in range(KD):
                    mm = pe.matmul(PS[:, bank, c0:T], slots[:, 0, k, x * P:x * P + P], HT[:, k, c0:T],
                                   start=(k == 0), stop=(k == KD - 1))
                mm.then_inc(rw["proj"], 1)
            pe.wait_ge(rw["small"], i * 32 + 32)
            for x, src, bank in ((0, oTW, 3), (1, oZA, 5)):
                for d in range(2):
                    q = slice(64 * d, 64 * d + 64)
                    mm = pe.matmul(PS[:, bank + d, :], oLW[q, x * P:x * P + P], src[q, :], start=True, stop=True)
                mm.then_inc(rw["lora"], 1)
            pe.wait_ge(rw["sq"], i + 1)
            pe.matmul(PS[:, 7, :], head_ones, E_[:, 0, :], start=True, stop=True).then_inc(rw["kksum"], 1)
            pe.wait_ge(rw["v"], i + 1)
            pe.wait_ge(rw["zp"], 3 * i + 3)
            for c in range(4):
                mm = pe.transpose(PS[:, 0, c * P:c * P + P], oVZ[:, c * P:c * P + P], ident)
            mm.then_inc(rw["vturned"], 1)
            pe.wait_ge(rw["hat"], i + 1)
            for b, src in enumerate((B_, KD_)):
                for d in range(2):
                    for c in range(4):
                        mm = pe.transpose(PS[:, 1 + 2 * b + d, c * P:c * P + P], src[:, d, c * P:c * P + P], ident)
                    mm.then_inc(rw["tok"], 1)
            pe.wait_ge(rw["tok_stored"], 4 * i + 4)
            pe.wait_ge(rw["vstored"], i + 1)
            for d in range(2):
                for h in range(2):
                    q = slice(64 * h, 64 * h + 64)
                    if d == 1:
                        pe.wait_ge(rw["x"], 24 * i + 11 + h)
                    for c in range(4):
                        cc = slice(c * P, c * P + P)
                        for bank, l, r in ((0, B_, PP_), (1, KD_, PP_), (2, PP_, B_)):
                            mm = pe.matmul(PS[:, 4 * h + bank, cc], l[q, d, cc], r[q, d, cc], start=True, stop=True)
                    for c in range(2):
                        for bank, l in ((0, B_), (2, KD_)):
                            mm = pe.matmul(PS[:, 4 * h + 3, (bank + c) * P:(bank + c) * P + P],
                                           l[q, d, L2 + c * P:L2 + c * P + P], PX_[q, d, c * P:c * P + P],
                                           start=True, stop=True)
                    mm.then_inc(rw["gram"], 1)
                for n in range(1, NL):
                    lv = (2 * i + d) * (NL - 1) * 2 + 2 * (n - 1)
                    for h in range(2):
                        if n == 1:
                            pe.wait_ge(rw["gram_read"], 4 * i + 2 * d + h + 1)
                        else:
                            pe.wait_ge(rw["x"], lv - 2 + h + 1)
                        pe.wait_ge(rw["mt"], lv + h + 1)
                        for c in range(4):
                            mm = pe.matmul(PS[:, 4 * h, c * P:c * P + P], MT[h][:, c, :], XX[h][:, c, :],
                                           start=True, stop=True)
                        mm.then_inc(rw["t1"], 1)
                    for h in range(2):
                        pe.wait_ge(rw["t1s"], lv + h + 1)
                        for c in range(4):
                            cc = slice(c * P, c * P + P)
                            mm = pe.matmul(PS[:, 4 * h + 2, cc], T1[h][:, c, :], XT_[:, d, h, c, :], start=True, stop=True)
                            if n < NL - 1:
                                mm = pe.matmul(PS[:, 4 * h + 1, cc], XT_[:, d, h, c, :], T1[h][:, c, :],
                                               start=True, stop=True)
                        mm.then_inc(rw["p"], 1)
            pe.wait_ge(rw["x"], 24 * i + 24)
            for m in range(4):
                step = [(d, RORD[d][m]) for d in range(2)]
                for d, c in step:
                    if m > 0:
                        pe.wait_ge(rw["s"], 6 * i + 2 * (m - 1) + d + 1)
                        pe.matmul(PS[:, d, 0:P], PP_[:, d, c * P:c * P + P], ST_[:, d, :], start=True, stop=False,
                                  skip_group_check=True)
                    for h in range(2):
                        mm = pe.matmul(PS[:, d, 64 * h:64 * h + 64], MK_[:, d, h, c, :], oVT[:, c * P + 64 * h:c * P + 64 * h + 64],
                                       start=(m == 0), stop=True, skip_group_check=True)
                    mm.then_inc(rw["w"], 1)
                for d, c in step:
                    pe.wait_ge(rw["ws"], 8 * i + 2 * m + d + 1)
                    for h in range(2):
                        mm = pe.matmul(PS[:, 2 + d, 64 * h:64 * h + 64], XT_[:, d, h, c, :], WS_[:, d, 64 * h:64 * h + 64],
                                       start=True, stop=True)
                    mm.then_inc(rw["u"], 1)
                for d, c in step:
                    vt = oVT[:, c * P:c * P + P]
                    pe.wait_ge(rw["us"], 8 * i + 2 * m + d + 1)
                    if m >= 2:
                        mm = pe.matmul(PS[:, 4 + c, 0:P], ST_[:, d, :], PX_[:, d, (c - 2) * P:(c - 1) * P],
                                       start=(m == 2), stop=False, skip_group_check=True)
                        for h in range(2):
                            o = PS[64 * h:64 * h + 64, 4 + c, 0:P]
                            pe.matmul(o, US_[:, d, 64 * h:64 * h + 64], NN_[:, d, h, c - 2, :], start=False, stop=False,
                                      skip_group_check=True)
                            mm = pe.matmul(o, vt[:, 64 * h:64 * h + 64], NN_[:, d, h, c, :], start=False, stop=(m == 3),
                                           skip_group_check=True)
                        if m == 3:
                            mm.then_inc(rw["y"], 1)
                    if m < 3:
                        pe.matmul(PS[:, 4 + d, 0:P], BT_[:, d, c * P:c * P + P], US_[:, d, :], start=True, stop=False)
                        pe.matmul(PS[:, 4 + d, 0:P], KT_[:, d, c * P:c * P + P], vt, start=False,
                                  stop=True).then_inc(rw["ds"], 1)
            pe.matmul(PS[:, 0, 0:L2], oLW[:, 256:384], oSG, start=True, stop=True).then_inc(rw["g2"], 1)
            pe.matmul(PS[:, 1, 0:L2], head_ones, oBON, start=True, stop=True).then_inc(rw["bonus"], 1)
            pe.wait_ge(rw["yb"], i + 1)
            pe.matmul(PS[:, 2, 0:L2], head_ones, oPX[:, 0:L2], start=True, stop=True).then_inc(rw["mean"], 1)
            pe.wait_ge(rw["ysq"], i + 1)
            pe.matmul(PS[:, 3, 0:L2], head_ones, oPX[:, L2:2 * L2], start=True, stop=True).then_inc(rw["var"], 1)

        def pair_act(act, i):
            act.wait_ge(rw["proj"], 3 * i + 1)
            for x, bank in ((1, 1), (2, 2), (0, 0)):
                s0 = 1 if x == 0 else 0
                act.wait_ge(rw["proj"], 3 * i + {1: 1, 2: 2, 0: 3}[x])
                act.activation(ZP[x][:, s0:2, 1:L2 + 1], PS[:, bank, s0 * L2:T].rearrange("p (s n) -> p s n", n=L2),
                               ACT.Copy).then_inc(rw["zp"], 1)
            act.wait_ge(rw["derived"], i + 1)
            for x, dst, bank in ((0, G_, 3), (1, B_, 5)):
                act.wait_ge(rw["lora"], 2 * i + x + 1)
                for d in range(2):
                    ins = act.activation(dst[:, d, :], PS[:, bank + d, :], ACT.Tanh, scale=0.5,
                                         bias=oPD[:, 2 * x + d:2 * x + d + 1])
                ins.then_inc(rw["tanh_w"] if x == 0 else rw["tanh_a"], 1)
            act.wait_ge(rw["kksum"], i + 1)
            act.activation(E_[:, 1, :], PS[:, 7, :], ACT.Ln, bias=EPS[:, 1:2])
            act.drain()
            act.activation(E_[:, 1, :], E_[:, 1, :], ACT.Exp, scale=-0.5).then_inc(rw["kkrs"], 1)
            act.wait_ge(rw["vturned"], i + 1)
            act.activation(oVT, PS[:, 0, :], ACT.Copy).then_inc(rw["vstored"], 1)
            act.wait_ge(rw["expo"], i + 1)
            lat = slice(L2, T)
            act.activation(PP_[:, 0, :], G_[:, 0, :], ACT.Exp)
            act.activation(PP_[:, 1, :], E_[:, 1, :], ACT.Exp, scale=-1.0)
            act.activation(PX_[:, 0, 0:L2], E_[:, 0, lat], ACT.Exp)
            act.activation(PX_[:, 1, 0:L2], G_[:, 1, lat], ACT.Exp, scale=-1.0)
            act.activation(C_[:, 0, :], E_[:, 0, :], ACT.Exp, scale=-1.0)
            act.activation(C_[:, 1, :], G_[:, 1, :], ACT.Exp)
            act.activation(oFF, oFF, ACT.Exp).then_inc(rw["exps"], 1)
            for b, dst in enumerate((BT_, KT_)):
                for d in range(2):
                    act.wait_ge(rw["tok"], 4 * i + 2 * b + d + 1)
                    act.activation(dst[:, d, :], PS[:, 1 + 2 * b + d, :], ACT.Copy).then_inc(rw["tok_stored"], 1)
            for d in range(2):
                for h in range(2):
                    act.wait_ge(rw["gram"], 4 * i + 2 * d + h + 1)
                    act.activation(LTS[h], PS[:, 4 * h, :].rearrange("p (c n) -> p c n", c=4),
                                   ACT.Copy).then_inc(rw["lt"], 1)
                for n in range(1, NL):
                    lv = (2 * i + d) * (NL - 1) * 2 + 2 * (n - 1)
                    for h in range(2):
                        act.wait_ge(rw["t1"], lv + h + 1)
                        act.activation(T1[h], PS[:, 4 * h, :].rearrange("p (c n) -> p c n", c=4),
                                       ACT.Copy).then_inc(rw["t1s"], 1)
            for m in range(4):
                for d in range(2):
                    act.wait_ge(rw["w"], 8 * i + 2 * m + d + 1)
                    act.activation(WS_[:, d, :], PS[:, d, 0:P], ACT.Copy).then_inc(rw["ws"], 1)
                for d in range(2):
                    act.wait_ge(rw["u"], 8 * i + 2 * m + d + 1)
                    act.activation(US_[:, d, :], PS[:, 2 + d, 0:P], ACT.Copy, scale=-1.0).then_inc(rw["us"], 1)
            act.wait_ge(rw["var"], i + 1)
            act.activation(oPP[:, 0:L2], PS[:, 3, 0:L2], ACT.Ln, scale=1.0 / 64, bias=EPS[:, 2:3])
            act.drain()
            act.activation(oPP[:, 0:L2], oPP[:, 0:L2], ACT.Exp, scale=-0.5).then_inc(rw["rstd"], 1)

        def pair_pool(pool, i):
            lvl = cst("level").rearrange("p (d l n) -> p d l n", d=2, l=NL)
            for d in range(2):
                for n in range(1, NL):
                    lv = (2 * i + d) * (NL - 1) * 2 + 2 * (n - 1)
                    mask = lvl[:, d, n, :].rearrange("p (o n) -> p o n", o=1).broadcast_to([P, 4, P])
                    for h in range(2):
                        if n == 1:
                            pool.wait_ge(rw["lt"], 4 * i + 2 * d + h + 1)
                        else:
                            pool.wait_ge(rw["t1"], lv - 2 + h + 1)
                        pool.tensor_tensor(MT[h], LTS[h], mask, ALU.mult).then_inc(rw["mt"], 1)

        def pair_dve(dve, i):
            drain = dve.drain
            zero_edges(dve)
            dve.wait_ge(rw["small"], 32 * i + 32)
            dve.tensor_scalar(oPD[:, 0:4], oPV[:, 3:7], 0.5, None, ALU.mult)
            dve.tensor_scalar(oPD[:, 4:7], oPV[:, 0:3], 0.5, None, ALU.mult)
            dve.tensor_scalar(oPD[:, 7:10], oPV[:, 0:3], -1.0, 1.0, ALU.mult, ALU.add)
            dve.tensor_scalar(oPD[:, 10:11], oPV[:, 8:9], -1.0, 1.0, ALU.mult, ALU.add).then_inc(rw["derived"], 1)
            drain()
            dve.wait_ge(rw["zp"], 3 * i + 1)
            shift_mix(dve, oKZ, ZP[1], 0, oPD[:, 5:6], oPD[:, 8:9])
            drain()
            dve.tensor_scalar(oKK, oKZ, oPV[:, 7:8], None, ALU.mult)
            drain()
            dve.tensor_tensor(E_[:, 0, :], oKK, oKK, ALU.mult).then_inc(rw["sq"], 1)
            dve.wait_ge(rw["zp"], 3 * i + 2)
            shift_mix(dve, oVZ, ZP[2], 0, oPD[:, 6:7], oPD[:, 9:10]).then_inc(rw["v"], 1)
            drain()
            dve.wait_ge(rw["zp"], 3 * i + 3)
            shift_mix(dve, oRZ, ZP[0], 1, oPD[:, 4:5], oPD[:, 7:8])
            dve.wait_ge(rw["tanh_w"], i + 1)
            dve.tensor_scalar(oG, oG, 1.0, -0.5 * EXP_M05, ALU.add, ALU.mult)
            drain()
            for d in range(2):
                dve.tensor_tensor_scan(C_[:, d, :], cst("reset128"), G_[:, d, :], 0.0, ALU.mult, ALU.add)
            dve.wait_ge(rw["kkrs"], i + 1)
            dve.tensor_tensor(oKK, oKK, E_[:, 1, :], ALU.mult)
            drain()
            cv = oC.rearrange("p (n s) -> p n s", s=P)
            c4 = oC.rearrange("p (d c s) -> p d c s", d=2, s=P)
            dve.tensor_tensor(oE.rearrange("p (n s) -> p n s", s=P), cv, cv[:, :, 63:64].broadcast_to([P, 8, P]),
                              ALU.subtract)
            dve.tensor_copy(oMID, c4[:, :, :, 63])
            dve.tensor_tensor(oDN, c4[:, :, :, 127], c4[:, :, :, 63], ALU.subtract)
            drain()
            dve.tensor_tensor(oG, oE, oG, ALU.subtract)
            for d in range(2):
                a, b = (oDN, oMID) if d == 0 else (oMID, oDN)
                for c, e in zip(RORD[d], RORD[d][1:]):
                    dve.tensor_tensor(oFF[:, d, c:c + 1], a[:, d, c:c + 1], b[:, d, e:e + 1], ALU.add)
                dve.memset(oFF[:, d, RORD[d][3]:RORD[d][3] + 1], 0.0)
            drain().then_inc(rw["expo"], 1)
            dve.wait_ge(rw["tanh_a"], i + 1)
            dve.tensor_scalar(oB, oB, 0.5, 0.5, ALU.mult, ALU.add)
            drain()
            dve.tensor_scalar(oKD, oB, oPV[:, 8:9], oPD[:, 10:11], ALU.mult, ALU.add)
            drain()
            for d in range(2):
                dve.tensor_tensor(KD_[:, d, :], KD_[:, d, :], oKZ, ALU.mult)
                dve.tensor_tensor(B_[:, d, :], B_[:, d, :], oKK, ALU.mult)
            drain()
            dve.tensor_tensor(oBON, KD_[:, 0, L2:T], KD_[:, 1, L2:T], ALU.add)
            drain()
            dve.scalar_tensor_tensor(oBON, oBON, oPV[:, 9:10], oRZ, ALU.mult, ALU.mult)
            dve.wait_ge(rw["exps"], i + 1)
            dve.tensor_tensor(oB, oB, oC, ALU.mult)
            dve.tensor_tensor(oKD, oKD, oC, ALU.mult)
            for d in range(2):
                dve.tensor_tensor(PP_[:, d, :], PP_[:, d, :], oKK, ALU.mult)
                dve.tensor_tensor(PX_[:, d, 0:L2], PX_[:, d, 0:L2], oRZ, ALU.mult)
            drain().then_inc(rw["hat"], 1)
            lvl = cst("level").rearrange("p (d l n) -> p d l n", d=2, l=NL)

            def four(ap, n=4):
                return ap.rearrange("p (o n) -> p o n", o=1).broadcast_to([P, n, P])

            for d in range(2):
                for h in range(2):
                    dve.wait_ge(rw["gram"], 4 * i + 2 * d + h + 1)
                    bank = [PS[:, 4 * h + b, :].rearrange("p (c n) -> p c n", c=4) for b in range(4)]
                    dve.tensor_tensor(XX[h], bank[2], four(lvl[:, 1 - d, 0, :]), ALU.mult)
                    dve.tensor_tensor(MK_[:, d, h], bank[1], four(cst("strict")[:, d * P:d * P + P]), ALU.mult)
                    dve.tensor_tensor(NN_[:, d, h], bank[3], four(cst("incl")[:, d * P:d * P + P]), ALU.mult)
                    dve.wait_ge(rw["lt"], 4 * i + 2 * d + h + 1)
                    dve.tensor_tensor(XT_[:, d, h], LTS[h], four(lvl[:, d, 0, :]), ALU.mult)
                    drain()
                    dve.tensor_tensor(XX[h], four(ident), XX[h], ALU.subtract)
                    dve.tensor_tensor(XT_[:, d, h], four(ident), XT_[:, d, h], ALU.subtract)
                    drain().then_inc(rw["gram_read"], 1)
                for n in range(1, NL):
                    lv = (2 * i + d) * (NL - 1) * 2 + 2 * (n - 1)
                    for h in range(2):
                        dve.wait_ge(rw["p"], lv + h + 1)
                        if n < NL - 1:
                            dve.tensor_tensor(XX[h], XX[h], PS[:, 4 * h + 1, :].rearrange("p (c n) -> p c n", c=4),
                                              ALU.subtract)
                        dve.tensor_tensor(XT_[:, d, h], XT_[:, d, h],
                                          PS[:, 4 * h + 2, :].rearrange("p (c n) -> p c n", c=4),
                                          ALU.subtract).then_inc(rw["x"], 1)
                    drain()
            for m in range(3):
                for d in range(2):
                    c = RORD[d][m]
                    f = oFF[:, d, c:c + 1]
                    dve.wait_ge(rw["ds"], 6 * i + 2 * m + d + 1)
                    tmp = C_[:, d, 0:P]
                    dst = tmp if m > 0 else ST_[:, d, :]
                    ins = dve.scalar_tensor_tensor(dst, PS[:, 4 + d, 0:P], f, head_ones, ALU.mult, ALU.mult)
                    if m > 0:
                        drain()
                        ins = dve.scalar_tensor_tensor(ST_[:, d, :], ST_[:, d, :], f, tmp, ALU.mult, ALU.add)
                    ins.then_inc(rw["s"], 1)
            y, sq = oPX[:, 0:L2], oPX[:, L2:2 * L2]
            dve.wait_ge(rw["bonus"], i + 1)
            dve.tensor_tensor(oC[:, 0:L2], PS[:, 1, 0:L2], oVZ[:, L2:T], ALU.mult)
            drain()
            dve.wait_ge(rw["y"], 2 * i + 2)
            dve.tensor_tensor(y.rearrange("p (c n) -> p c n", c=2), oC[:, 0:L2].rearrange("p (c n) -> p c n", c=2),
                              PS[:, 6:8, 0:P], ALU.add).then_inc(rw["yb"], 1)
            drain()
            dve.wait_ge(rw["mean"], i + 1)
            dve.scalar_tensor_tensor(y, PS[:, 2, 0:L2], -1.0 / 64, y, ALU.mult, ALU.add)
            drain()
            dve.tensor_tensor(sq, y, y, ALU.mult).then_inc(rw["ysq"], 1)
            dve.wait_ge(rw["rstd"], i + 1)
            dve.tensor_tensor(y, y, oPP[:, 0:L2], ALU.mult)
            drain()
            dve.tensor_scalar(y, y, oPV[:, 10:11], oPV[:, 11:12], ALU.mult, ALU.add)
            drain()
            dve.tensor_tensor(CATT[:, ds(i * L2 + 2 * L2, L2)], y, PS[:, 0, 0:L2], ALU.mult)

        def weights_odd(sp):
            w = odd_w_in[0]
            no = 8
            rk = FOUR + 3 * RW_DIM
            ev = moe_ev
            sp.wait_ge(ev["gateup_done"], 60)
            weights_cols(sp, 2, 0, w, rk, 384)
            weights_cols(sp, 3, 0, w, 0, FOUR)
            sp.wait_ge(ev["gateup_done"], 64)
            sp.wait_ge(phase, 3 * 11)
            for i in range(NPAIR):
                if i > 0:
                    sp.wait_ge(rw["proj"], 3 * i)
                for x in range(3):
                    weights_cols(sp, 0, x * P, w, FOUR + x * RW_DIM + i * P, P)
                if i > 0:
                    sp.wait_ge(odd_part, 3 * i)
                sp.dma_start(oPV, pair_small[i]).then_inc(rw["small"], 16)
                sp.dma_start(oLW, pair_w[i]).then_inc(rw["small"], 16)
            sp.wait_ge(pre["four"], 1)
            for h in range(2):
                weights_cols(sp, 2 + h, 0, odd_w_out[0], 512 * h, 512)
            weights_moe1(sp)

        def weights_moe1(sp):
            no = 4
            sp.wait_ge(phase, 3 * 12)
            weights_down(sp, 1, 0, 0)
            sp.dma_start(slots[:, 5, :, :], moe_w_gate[1, 1].rearrange("(k p) n -> p k n", p=P)).then_inc(w_ready[5], 16)
            sp.dma_start(slots[:, 0, :, :], moe_w_up[1, 1].rearrange("(k p) n -> p k n", p=P)).then_inc(w_ready[0], 16)
            weights_down(sp, 1, 1, 0)
            sp.wait_ge(proj_ev["out_done"], OUT_BEFORE[1] + 4)
            weights_expert(sp, 1, 0, 0)
            weights_moe_rest(sp, 1, 1, no)

        OUT1_READY = [ODD_BASE[2] + 32, ODD_BASE[3] + 32]
        MOE1_BASE = [ODD_BASE[0] + 48 * NPAIR, ODD_BASE[1], OUT1_READY[0], OUT1_READY[1], ODD_BASE[4], ODD_BASE[5]]

        def odd_part_pe(pe):
            norm_pe(pe, 2, ALL)
            meet(pe, 10)
            odd_pre_pe(pe)
            meet(pe, 11)
            with pe.Fori(0, NPAIR) as i:
                pair_pe(pe, i)
                odd_meet(pe, i * 3 + 3)
            meet(pe, 12)
            gate_pe(pe, 2, (0,))
            meet(pe, 13)
            out_pe(pe, 1, LAT, 2, OUT1_READY, CATT.rearrange("p (k n) -> p k n", k=KD))
            meet(pe, 14)
            norm_pe(pe, 3, LAT)
            meet(pe, 15)
            router_pe(pe, 1, LAT)
            meet(pe, 16)
            gate_pe(pe, 3, (0,))
            meet(pe, 17)
            moe_pe(pe, 1, LAT, MOE1_BASE)
            meet(pe, 18)

        def odd_part_act(act):
            norm_act(act, 2, ALL)
            meet(act, 10)
            odd_pre_act(act)
            meet(act, 11)
            with act.Fori(0, NPAIR) as i:
                pair_act(act, i)
                odd_meet(act, i * 3 + 3)
            meet(act, 12)
            gate_act(act, 2, (0,))
            meet(act, 13)
            meet(act, 14)
            norm_act(act, 3, LAT)
            meet(act, 15)
            router_act(act, 1, LAT)
            meet(act, 16)
            gate_act(act, 3, (0,))
            meet(act, 17)
            moe_act(act, 1, LAT)
            meet(act, 18)

        def odd_part_dve(dve):
            norm_dve(dve, 2, ALL)
            meet(dve, 10)
            odd_pre_dve(dve)
            meet(dve, 11)
            dve.tensor_scalar(oSG, oSG, 0.5, 0.5, ALU.mult, ALU.add)
            with dve.Fori(0, NPAIR) as i:
                pair_dve(dve, i)
                odd_meet(dve, i * 3 + 3)
            meet(dve, 12)
            gate_dve(dve, 2, (0,))
            meet(dve, 13)
            out_dve(dve, 1, LAT)
            meet(dve, 14)
            norm_dve(dve, 3, LAT)
            meet(dve, 15)
            router_dve(dve, 1, LAT)
            meet(dve, 16)
            gate_dve(dve, 3, (0,))
            meet(dve, 17)
            moe_dve(dve, 1, LAT)
            moe_end_dve(dve, 1, LAT)
            meet(dve, 18)

        def weights_ada(sp):
            for n in range(DEPTH * N_ADA):
                lay, b = n // N_ADA, n % N_ADA
                if n >= NSLOT:
                    sp.wait_ge(ada_rows, n - NSLOT + 1)
                sp.dma_start(slots[:, b % NSLOT, :, :], ada_w[lay, :, b * 512:b * 512 + 512]
                             .rearrange("(k p) n -> p k n", p=P)).then_inc(w_ready[b % NSLOT], 16)

        def weights_cols(sp, s, at, w, c0, width):
            sp.dma_start(slots[:, s, :, at:at + width],
                         w[:, c0:c0 + width].rearrange("(k p) n -> p k n", p=P)).then_inc(w_ready[s], 16)

        def weights_even(sp):
            w = even_w_in[0]
            for g in range(2):
                if g == 0:
                    sp.wait_ge(ada_rows, 2 * N_ADA - 5)
                else:
                    sp.wait_ge(gla["proj"], 7)
                for at, c0, width in ((0, 128 * g, 128), (128, 256 + 128 * g, 128), (256, 512 + 256 * g, 256)):
                    weights_cols(sp, 0, at, w, c0, width)
                if g == 0:
                    sp.wait_ge(ada_rows, 2 * N_ADA - 4)
                weights_cols(sp, 1, 0, w, 1024 + 256 * g, 256)
                weights_cols(sp, 1, 256, w, 1536, 32)
                if g == 1:
                    sp.wait_ge(gla["logits"], 1)
                    sp.wait_ge(gla["expo"], 1)
                sp.dma_start(GW[:, :], gla_small[g]).then_inc(gla["small"], 16)
                if g == 0:
                    sp.wait_ge(ada_rows, 2 * N_ADA - 3)
                else:
                    sp.wait_ge(att["proj"], NT)
                for at, c0, width in ((0, 1568 + 256 * g, 256), (256, 2080 + 64 * g, 64), (320, 2208 + 64 * g, 64)):
                    weights_cols(sp, 2, at, w, c0, width)
            sp.wait_ge(gla["proj"], 14)
            for h in range(2):
                weights_cols(sp, h, 0, even_w_out[0], 512 * h, 512)

        def weights_expert(sp, lay, e, i):
            g, u, dn = EXPERT_SLOTS[e]
            k = i * 2 + e
            for s, w in ((g, moe_w_gate), (u, moe_w_up)):
                sp.dma_start(slots[:, s, :, :], w[lay, ds(k, 1), :, :].rearrange("e (k p) n -> p (e k) n", p=P)
                             if not isinstance(k, int) else w[lay, k].rearrange("(k p) n -> p k n", p=P)
                             ).then_inc(w_ready[s], 16)

        def weights_down(sp, lay, e, i):
            dn = EXPERT_SLOTS[e][2]
            k = i * 2 + e
            src = (moe_w_down[lay, ds(k, 1), :, :].rearrange("e (f p) n -> p (e f) n", p=P)
                   if not isinstance(k, int) else moe_w_down[lay, k].rearrange("(f p) n -> p f n", p=P))
            sp.dma_start(slots[:, dn, :, :].rearrange("p (f h) n -> p f (h n)", h=2), src).then_inc(w_ready[dn], 16)

        def weights_moe_rest(sp, n, lay, no):
            ev = moe_ev
            hb, db = HIDDEN_BEFORE[n], DOWN_BEFORE[n]
            with sp.Fori(1, N_EXP // 2) as i:
                for e in range(2):
                    sp.wait_ge(ev["gateup_done"], i * 8 - 8 + 4 * e + 4 + hb)
                    weights_expert(sp, lay, e, i)
                    sp.wait_ge(ev["down_done"], (i * 2 - 2 + e + 1) * no + db)
                    weights_down(sp, lay, e, i)

        LAST_PHASE = 18
        block = stack.enter_context(nc.Block())
        ALL, LAT = list(range(NT)), [2, 3]

        def even_meet(eng, value):
            eng.drain().then_inc(even_part, 1)
            eng.wait_ge(even_part, value)

        @block.sync
        def _(sp):
            sp.dma_start(X[:, 0:2, :], ctx_in[0].rearrange("(t p) n -> p t n", p=P)).then_inc(in_ready, 16)
            sp.dma_start(X[:, 2:4, :], x[0].rearrange("(t p) n -> p t n", p=P)).then_inc(in_ready, 16)
            sp.dma_start(CST[:, :], consts).then_inc(in_ready, 16)
            sp.dma_start(PRM[:, :], params).then_inc(in_ready, 16)
            sp.dma_start(ROW[:, :], rows.partition_broadcast(P)).then_inc(in_ready, 16)
            weights_ada(sp)
            weights_even(sp)
            sp.wait_ge(att["proj"], 2 * NT)
            sp.wait_ge(phase, 3 * 3)
            weights_expert(sp, 0, 0, 0)
            weights_down(sp, 0, 0, 0)
            sp.dma_start(slots[:, 5, :, :], moe_w_gate[0, 1].rearrange("(k p) n -> p k n", p=P)).then_inc(w_ready[5], 16)
            sp.wait_ge(proj_ev["out_done"], 8)
            sp.dma_start(slots[:, 0, :, :], moe_w_up[0, 1].rearrange("(k p) n -> p k n", p=P)).then_inc(w_ready[0], 16)
            weights_down(sp, 0, 1, 0)
            weights_moe_rest(sp, 0, 0, 8)
            weights_odd(sp)
            sp.wait_ge(phase, 3 * LAST_PHASE)
            sp.dma_start(out[0].rearrange("(t p) n -> p t n", p=P), X[:, 2:4, :]).then_inc(out_stored, 16)
            sp.wait_ge(out_stored, 16)

        @block.tensor
        def _(pe):
            pe.wait_ge(in_ready, 80)
            ada_pe(pe)
            meet(pe, 1)
            norm_pe(pe, 0, ALL)
            meet(pe, 2)
            with pe.Fori(0, 2) as i:
                gla_pe(pe, i, EVEN_BASE)
                even_meet(pe, i * 6 + 3)
                att_pe(pe, i, EVEN_BASE)
                even_meet(pe, i * 6 + 6)
            meet(pe, 3)
            gate_pe(pe, 0, (0, 1))
            meet(pe, 4)
            turn_pe(pe)
            turned_meet(pe)
            out_pe(pe, 0, ALL, 0, OUT0_READY, HT)
            meet(pe, 5)
            norm_pe(pe, 1, ALL)
            meet(pe, 6)
            router_pe(pe, 0, ALL)
            meet(pe, 7)
            gate_pe(pe, 1, (0, 1))
            meet(pe, 8)
            moe_pe(pe, 0, ALL, MOE0_BASE)
            meet(pe, 9)
            odd_part_pe(pe)

        @block.scalar
        def _(act):
            act.wait_ge(in_ready, 80)
            cond = prm("cond").rearrange("p (k v) -> p k v", v=2)
            act.activation(COND[:], cond, ACT.Tanh, scale=0.5).then_inc(cond_th, 1)
            ada_act(act)
            meet(act, 1)
            norm_act(act, 0, ALL)
            meet(act, 2)
            with act.Fori(0, 2) as i:
                gla_act(act, i)
                even_meet(act, i * 6 + 3)
                att_act(act, i)
                even_meet(act, i * 6 + 6)
            meet(act, 3)
            gate_act(act, 0, (0, 1))
            meet(act, 4)
            turn_copy(act, range(0, KD, 2))
            turned_meet(act)
            meet(act, 5)
            norm_act(act, 1, ALL)
            meet(act, 6)
            router_act(act, 0, ALL)
            meet(act, 7)
            gate_act(act, 1, (0, 1))
            meet(act, 8)
            moe_act(act, 0, ALL)
            meet(act, 9)
            odd_part_act(act)

        @block.gpsimd
        def _(pool):
            pool.wait_ge(in_ready, 80)
            with pool.Fori(0, NPAIR) as i:
                pair_pool(pool, i)

        @block.vector
        def _(dve):
            for c, value in enumerate((NORM_EPS, L2_EPS, GN_EPS, 0.0)):
                dve.memset(EPS[:, c:c + 1], value)
            dve.memset(GATES[:], 0.0)
            dve.wait_ge(in_ready, 80)
            dve.wait_ge(cond_th, 1)
            cond = prm("cond").rearrange("p (k v) -> p k v", v=2)
            dve.scalar_tensor_tensor(COND[:], COND[:], 1.0, cond, ALU.add, ALU.mult)
            dve.drain()
            dve.tensor_scalar(COND[:], COND[:], 0.5, None, ALU.mult).then_inc(cond_ready, 1)
            ada_dve(dve)
            meet(dve, 1)
            norm_dve(dve, 0, ALL)
            meet(dve, 2)
            with dve.Fori(0, 2) as i:
                gla_dve(dve, i)
                even_meet(dve, i * 6 + 3)
                att_dve(dve, i)
                even_meet(dve, i * 6 + 6)
            meet(dve, 3)
            gate_dve(dve, 0, (0, 1))
            meet(dve, 4)
            turn_copy(dve, range(1, KD, 2))
            turned_meet(dve)
            out_dve(dve, 0, ALL)
            meet(dve, 5)
            norm_dve(dve, 1, ALL)
            meet(dve, 6)
            router_dve(dve, 0, ALL)
            meet(dve, 7)
            gate_dve(dve, 1, (0, 1))
            meet(dve, 8)
            moe_dve(dve, 0, ALL)
            moe_end_dve(dve, 0, ALL)
            meet(dve, 9)
            odd_part_dve(dve)


def kernel(**inputs):
    import concourse.bacc as _bacc
    from concourse import mybir as _mybir
    from concourse.bass_utils import run_bass_kernel_spmd as _run

    a = {k: np.ascontiguousarray(v) for k, v in inputs.items()}

    def cols(v):
        return v.reshape(*v.shape[:-1], -1, P)

    norm = np.stack([a["norm_mix"][0], a["norm_ffn"][0], a["norm_mix"][1], a["norm_ffn"][1]])
    mu = a["rwkv_mu"][0]
    params = np.concatenate([
        cols(norm).reshape(-1, P).T,
        np.stack([a["c"][0].reshape(KD, P), a["c_ctx"].reshape(KD, P)], 1).reshape(-1, P).T,
        cols(a["ada_b"]).reshape(-1, P).T,
        mu[3 * RW_DIM:].reshape(3, P).T,
        a["router_w"].reshape(KD, P, 16).transpose(1, 0, 2).reshape(P, -1)], 1)
    rows = np.concatenate([a["router_b"], a["att_sink"][0], np.tile(a["att_q_norm"][0], GRP), a["att_k_norm"][0],
                           a["gla_out_norm"][0]])
    gla_small = np.zeros((2, P, 260), np.float32)
    for g in range(2):
        gla_small[g, 0:16, 0:256] = a["gla_dec_w"][0][:, :, g * P:g * P + P].transpose(1, 0, 2).reshape(16, 256)
        gla_small[g, :, 256:258] = a["gla_dec_b"][0][:, g * P:g * P + P].T
    vecs = [mu[0:RW_DIM], mu[RW_DIM:2 * RW_DIM], mu[2 * RW_DIM:3 * RW_DIM], a["rwkv_w0"][0][0], a["rwkv_w0"][0][1],
            a["rwkv_a0"][0][0], a["rwkv_a0"][0][1], a["rwkv_kk_scale"][0], a["rwkv_k_a"][0],
            a["rwkv_r_k"][0].reshape(-1), a["rwkv_ln_g"][0], a["rwkv_ln_b"][0]]
    pair_small = np.stack([v.reshape(NPAIR, P) for v in vecs], 2)
    pair_w = np.stack([a["rwkv_w2"][0].reshape(P, NPAIR, P), a["rwkv_a2"][0].reshape(P, NPAIR, P),
                       a["rwkv_g2"][0].reshape(P, NPAIR, P)], 0).transpose(2, 1, 0, 3).reshape(NPAIR, P, 3 * P)
    laid = {"x": a["x"], "ctx": a["ctx"]}
    for k in ("ada_w", "even_w_in", "even_w_out", "odd_w_in", "odd_w_out", "moe_w_gate", "moe_w_up", "moe_w_down"):
        laid[k] = a[k]
    laid.update(consts=shape_constants(), params=params, rows=rows, gla_small=gla_small, pair_small=pair_small,
                pair_w=pair_w)

    nc = _bacc.Bacc("TRN2", target_bir_lowering=False, num_devices=1)
    arrays, args = {}, []
    for name, v in laid.items():
        v = np.ascontiguousarray(v)
        arrays[f"in_{name}_dram"] = v
        args.append(nc.dram_tensor(f"in_{name}_dram", v.shape, _mybir.dt.from_np(v.dtype), kind="ExternalInput").ap())
    args.append(nc.dram_tensor("out_0_dram", (1, SEG, D), F32, kind="ExternalOutput").ap())
    build(nc, *args)
    r = _run(nc, [arrays], core_ids=[0])
    return r.results[0]["out_0_dram"]
```

```python
from contextlib import ExitStack

import numpy as np

import concourse.bass as bass
from concourse import mybir

P = 128
D = 1024
KD = D // P
T = 512
NT = T // P
SEG = 256
DEPTH = 2
NSLOT = 6

GLA_H, GLA_DK, GLA_DV, GLA_RANK, GLA_TAU = 8, 32, 64, 16, 16.0
GLA_C = 32
NCH = T // GLA_C
ATT_H, ATT_KV, HD, WINDOW = 8, 2, 64, 128
GRP = ATT_H // ATT_KV
RW_DIM, RW_H, NPAIR = 768, 12, 6
FOUR = 256
N_EXP, D_EXP, TOP_K = 16, 512, 2
MAX_JOBS = 24
NORM_EPS = 1e-6
L2_EPS = 1e-12
GN_EPS = 64e-5
BIG = 1e30
LEVELS = (1, 2, 4, 8, 16, 32, 64)
EXP_M05 = float(np.exp(-0.5))

F32, I32, U32 = mybir.dt.float32, mybir.dt.int32, mybir.dt.uint32
ALU = mybir.AluOpType
ACT = mybir.ActivationFunctionType
AX = mybir.AxisListType
ds = bass.ds

CONST_COLS = [("ident", P), ("ones", P), ("head_ones", P), ("att_mask", 2 * P), ("level", 14 * P),
              ("strict", 2 * P), ("incl", 2 * P), ("gla_incl", 2 * P), ("gla_heads", 256),
              ("reset32", T), ("reset128", T), ("dft_tok", 2 * T), ("dft_ch", 2 * P),
              ("rope", 2 * 2 * 32), ("first4", 4), ("first16", 16), ("job_index", MAX_JOBS)]
PARAM_COLS = [("norm", 4 * KD), ("cond", 2 * KD), ("ada_b", 96), ("lora_mu", 3), ("router", KD * 16)]
PAIR_COLS = 12
ROW_COLS = [("router_b", 16), ("sink", 8), ("qk_gain", 5 * HD), ("gla_gain", GLA_DV)]


def columns(table):
    at, n = {}, 0
    for name, width in table:
        at[name] = (n, n + width)
        n += width
    return at, n


def shape_constants():
    at, n = columns(CONST_COLS)
    c = np.zeros((P, n), np.float32)

    def put(name, a):
        c[:, at[name][0]:at[name][1]] = a.reshape(P, -1)

    a, b = np.arange(P)[:, None], np.arange(P)[None, :]
    put("ident", (a == b).astype(np.float32))
    put("ones", np.ones((P, P), np.float32))
    put("head_ones", (a // 64 == b // 64).astype(np.float32))
    put("att_mask", np.stack([np.where(b <= a, 0.0, -BIG), np.where(b >= a, 0.0, -BIG)], 1).astype(np.float32))
    low = [((a // (2 * m) == b // (2 * m)) & (a // m % 2 == 1) & (b // m % 2 == 0)).astype(np.float32) for m in LEVELS]
    put("level", np.stack([m.T for m in low] + low, 1))
    put("strict", np.stack([a < b, a > b], 1).astype(np.float32))
    put("incl", np.stack([a <= b, a >= b], 1).astype(np.float32))
    same = a // GLA_C == b // GLA_C
    put("gla_incl", np.stack([same & (a <= b), same & (a >= b)], 1).astype(np.float32))
    put("gla_heads", (a // GLA_DK == np.arange(256)[None, :] // GLA_DV).astype(np.float32))
    t = np.arange(T)[None, :]
    put("reset32", np.broadcast_to(t % GLA_C != 0, (P, T)).astype(np.float32))
    put("reset128", np.broadcast_to(t % P != 0, (P, T)).astype(np.float32))
    ang = 2 * np.pi * (np.outer(np.arange(SEG), np.arange(SEG)) % SEG) / SEG
    tok = np.concatenate([np.cos(ang), np.sin(ang)], 1) / np.sqrt(SEG)
    put("dft_tok", tok.reshape(2, P, T).transpose(1, 0, 2).astype(np.float32))
    ch = 2 * np.pi * (np.outer(np.arange(64), np.arange(64)) % 64) / 64
    both = np.zeros((P, 2, P))
    for h in range(2):
        s = slice(64 * h, 64 * h + 64)
        both[s, 0, s], both[s, 1, s] = np.cos(ch) / 8, -np.sin(ch) / 8
    put("dft_ch", both.astype(np.float32))
    n_freq = HD // 4
    inv = (np.float32(10000.0) ** (-np.arange(n_freq, dtype=np.float32) / np.float32(n_freq))).astype(np.float32)
    pos = np.arange(SEG)
    rot = np.concatenate([(pos // 64).astype(np.float32)[:, None] * inv,
                          (pos % 64).astype(np.float32)[:, None] * inv], -1)
    rope = np.stack([np.cos(rot), np.sin(rot)], 0).astype(np.float32)
    put("rope", rope.reshape(2, 2, P, 32).transpose(2, 0, 1, 3))
    put("first4", np.broadcast_to(np.arange(4, 0, -1, dtype=np.float32), (P, 4)))
    put("first16", np.broadcast_to(np.arange(16, 0, -1, dtype=np.float32), (P, 16)))
    put("job_index", np.broadcast_to(np.arange(MAX_JOBS, dtype=np.float32), (P, MAX_JOBS)))
    return c


def build(nc, x, ctx_in, ada_w, even_w_in, even_w_out, odd_w_in, odd_w_out, moe_w_gate, moe_w_up, moe_w_down,
          consts, params, rows, gla_small, pair_small, pair_w, out):
    CA, CN = columns(CONST_COLS)
    PA, PN = columns(PARAM_COLS)
    RA, RN = columns(ROW_COLS)

    with ExitStack() as stack:
        def sb(name, shape):
            return stack.enter_context(nc.sbuf_tensor(name, shape, F32))

        def sem(name):
            return stack.enter_context(nc.semaphore(name))

        PS = stack.enter_context(nc.psum_tensor("PS", [P, 8, 512], F32))
        slots = sb("slots", [P, NSLOT, KD, 512])
        X = sb("X", [P, NT, D])
        HT = sb("HT", [P, KD, T])
        XN = sb("XN", [P, NT, D])
        SCR = sb("SCR", [P, 8192])
        CST = sb("CST", [P, CN])
        PRM = sb("PRM", [P, PN])
        ROW = sb("ROW", [P, RN])
        COND = sb("COND", [P, KD, 2])
        MODC = sb("MODC", [P, DEPTH * 96])
        GAIN = sb("GAIN", [P, 4, KD, 2])
        SS = sb("SS", [P, 64])
        RS = sb("RS", [P, 64])
        EPS = sb("EPS", [P, 4])

        def cst(name):
            return CST[:, CA[name][0]:CA[name][1]]

        def prm(name):
            return PRM[:, PA[name][0]:PA[name][1]]

        def row(name):
            return ROW[:, RA[name][0]:RA[name][1]]

        ident, ones, head_ones = cst("ident"), cst("ones"), cst("head_ones")
        mod = MODC[:].rearrange("p (l m v) -> p l m v", l=DEPTH, v=2)

        def split(buf, sizes):
            pieces, n = [], 0
            for s in sizes:
                pieces.append(buf[:, n:n + s])
                n += s
            assert n <= buf.shape[1], (n, buf.shape)
            return pieces

        w_ready = [sem(f"w_ready{s}") for s in range(NSLOT)]
        w_free = [sem(f"w_free{s}") for s in range(NSLOT)]
        in_ready = sem("in_ready")
        phase = sem("phase")
        out_stored = sem("out_stored")

        ENGINES = 3

        def meet(eng, n):
            eng.drain().then_inc(phase, 1)
            eng.wait_ge(phase, ENGINES * n)

        ada_rows, ada_copied = sem("ada_rows"), sem("ada_copied")
        ada_turned, ada_stored = sem("ada_turned"), sem("ada_stored")
        cond_th, cond_ready = sem("cond_th"), sem("cond_ready")
        cat_turned = sem("cat_turned_all")
        norm_ev = {k: sem(k) for k in ("rstd_ready", "xn_ready", "xt_turned")}
        gate_ev = {k: sem(k) for k in ("gate_diag", "gate_spread", "gate_copied")}
        cat_turned_k = sem("cat_turned_k")
        proj_ev = {k: sem(k) for k in ("out_done", "out_added")}
        rt_ev = {k: sem(k) for k in ("logits_done", "logits_exp", "rows_turned", "rows_copied", "mask_ready",
                                     "ranks_done", "jobs_ready", "rows_ready", "rows_scattered", "rows_back")}
        moe_ev = {k: sem(k) for k in (
            "w_gate", "w_up", "w_down", "hg_loaded", "x_turned", "x_copied", "gate_done", "tanh", "up_done", "hidden",
            "hid_turned", "hid_copied", "down_done", "o_copied", "o_stored")}
        zeros_ready, hg_zeroed = sem("zeros_ready"), sem("hg_zeroed")
        XN_BEFORE = (0, 4, 8, 12)
        OUT_BEFORE = (0, 8)

        ADA_ROW = SCR[:, 0:1024].rearrange("p (b n) -> p b n", b=2)
        N_ADA = 12

        def ada_pe(pe):
            pe.wait_ge(cond_ready, 1)
            for i in range(DEPTH):
                for b in range(N_ADA + 1):
                    if b < N_ADA:
                        pe.wait_ge(w_ready[b % NSLOT], i * 32 + 16 * (b // NSLOT + 1))
                        if i * N_ADA + b >= 2:
                            pe.wait_ge(ada_copied, i * N_ADA + b - 1)
                        for k in range(KD):
                            mm = pe.matmul(PS[0:2, b % 2, :], COND[:, k, :], slots[:, b % NSLOT, k, :],
                                           start=(k == 0), stop=(k == KD - 1))
                        mm.then_inc(ada_rows, 1)
                    if b >= 1:
                        pe.wait_ge(ada_copied, i * N_ADA + b)
                        if i * N_ADA + b >= 3:
                            pe.wait_ge(ada_stored, i * N_ADA + b - 2)
                        for q in range(4):
                            mm = pe.matmul(PS[:, 2 + b % 2, 2 * q:2 * q + 2], ADA_ROW[0:2, (b - 1) % 2, q * P:q * P + P],
                                           ident[0:2, 0:2], start=True, stop=True)
                        mm.then_inc(ada_turned, 1)

        def ada_act(act):
            for i in range(DEPTH):
                for b in range(N_ADA):
                    act.wait_ge(ada_rows, i * N_ADA + b + 1)
                    if i * N_ADA + b >= 2:
                        act.wait_ge(ada_turned, i * N_ADA + b - 1)
                    act.activation(ADA_ROW[0:2, b % 2, :], PS[0:2, b % 2, :], ACT.Copy).then_inc(ada_copied, 1)

        def ada_dve(dve):
            bias = prm("ada_b")
            for i in range(DEPTH):
                for b in range(N_ADA):
                    dve.wait_ge(ada_turned, i * N_ADA + b + 1)
                    dve.tensor_tensor(MODC[:, i * 96 + b * 8:i * 96 + b * 8 + 8].rearrange("p (m v) -> p m v", v=2),
                                      PS[:, 2 + (b + 1) % 2, 0:8].rearrange("p (m v) -> p m v", v=2),
                                      bias[:, i * 48 + b * 4:i * 48 + b * 4 + 4].rearrange("p (m o) -> p m o", o=1)
                                      .broadcast_to([P, 4, 2]), ALU.add).then_inc(ada_stored, 1)
            dve.drain()
            for n in range(4):
                lay, which = n // 2, n % 2
                g = prm("norm")[:, n * KD:(n + 1) * KD].rearrange("p (k o) -> p k o", o=1)
                m = KD * (3 * which + 1)
                dve.scalar_tensor_tensor(GAIN[:, n, :, :], mod[:, lay, m:m + KD, :], 1.0,
                                         g.broadcast_to([P, KD, 2]), ALU.add, ALU.mult)

        def sides_of(tiles):
            return ((1, 0), (0, SEG)) if 0 in tiles else ((0, SEG),)

        def norm_act(act, n, tiles):
            ev = norm_ev
            for t in tiles:
                act.activation(XN[:, t, :], X[:, t, :], ACT.Square, accum_out=SS[:, t:t + 1])
            act.drain()
            a, b = tiles[0], tiles[-1] + 1
            act.activation(RS[:, a:b], SS[:, a:b], ACT.Ln, scale=1.0 / D, bias=EPS[:, 0:1])
            act.drain()
            act.activation(RS[:, a:b], RS[:, a:b], ACT.Exp, scale=-0.5).then_inc(ev["rstd_ready"], 1)
            lay, m = n // 2, KD * 3 * (n % 2)
            for k in range(0, KD, 2):
                act.wait_ge(ev["xt_turned"], KD * n + k + 1)
                for v, c0 in sides_of(tiles):
                    act.activation(HT[:, k, c0:c0 + SEG], PS[:, k, c0:c0 + SEG], ACT.Identity,
                                   bias=mod[:, lay, m + k, v:v + 1], scale=GAIN[:, n, k, v:v + 1])

        def norm_dve(dve, n, tiles):
            ev = norm_ev
            dve.wait_ge(ev["rstd_ready"], n + 1)
            for t in tiles:
                dve.tensor_scalar(XN[:, t, :], X[:, t, :], RS[:, t:t + 1], None,
                                  ALU.mult).then_inc(ev["xn_ready"], 1)
            lay, m = n // 2, KD * 3 * (n % 2)
            for k in range(1, KD, 2):
                dve.wait_ge(ev["xt_turned"], KD * n + k + 1)
                for v, c0 in sides_of(tiles):
                    dve.tensor_scalar(HT[:, k, c0:c0 + SEG], PS[:, k, c0:c0 + SEG], GAIN[:, n, k, v:v + 1],
                                      mod[:, lay, m + k, v:v + 1], ALU.mult, ALU.add)

        def norm_pe(pe, n, tiles):
            ev = norm_ev
            pe.wait_ge(ev["xn_ready"], XN_BEFORE[n] + len(tiles))
            for k in range(KD):
                for t in tiles:
                    mm = pe.transpose(PS[:, k, t * P:t * P + P], XN[:, t, k * P:k * P + P], ident)
                mm.then_inc(ev["xt_turned"], 1)

        GATE = SCR[:, 0:2 * D].rearrange("p (v n) -> p v n", v=2)
        DIAG = SCR[:, 2 * D:4 * D].rearrange("p (v n) -> p v n", v=2)

        def gate_dve(dve, n, sides):
            lay, part = n // 2, 2 + 3 * (n % 2)
            for v in sides:
                for k in range(KD):
                    ins = dve.tensor_scalar(DIAG[:, v, k * P:k * P + P], ident,
                                            mod[:, lay, part * KD + k, v:v + 1], None, ALU.mult)
            ins.then_inc(gate_ev["gate_diag"], 1)

        def gate_pe(pe, n, sides):
            pe.wait_ge(gate_ev["gate_diag"], n + 1)
            for v in sides:
                for h in range(2):
                    mm = pe.matmul(PS[:, 2 * v + h, :], ones, DIAG[:, v, h * 512:h * 512 + 512], start=True, stop=True)
            mm.then_inc(gate_ev["gate_spread"], 1)

        def gate_act(act, n, sides):
            act.wait_ge(gate_ev["gate_spread"], n + 1)
            for v in sides:
                ins = act.activation(GATE[:, v, :].rearrange("p (h n) -> p h n", h=2), PS[:, 2 * v:2 * v + 2, :], ACT.Copy)
            ins.then_inc(gate_ev["gate_copied"], 1)

        def out_pe(pe, n, tiles, first_slot, ready, cat):
            ev = proj_ev
            for j, (t, h) in enumerate((t, h) for t in tiles for h in range(2)):
                if j < 2:
                    pe.wait_ge(w_ready[first_slot + j], ready[j])
                if j >= 4:
                    pe.wait_ge(ev["out_added"], OUT_BEFORE[n] + j - 3)
                for k in range(KD):
                    a = (t - tiles[0]) * P
                    mm = pe.matmul(PS[:, 4 + j % 4, :], cat[:, k, a:a + P], slots[:, first_slot + h, k, :],
                                   start=(k == 0), stop=(k == KD - 1))
                mm.then_inc(ev["out_done"], 1)

        def out_dve(dve, n, tiles):
            ev = proj_ev
            dve.wait_ge(gate_ev["gate_copied"], 2 * n + 1)
            TMP = SCR[:, 4096:8192].rearrange("p (b n) -> p b n", b=8)
            for j, (t, h) in enumerate((t, h) for t in tiles for h in range(2)):
                v = 1 if t < 2 else 0
                cols = slice(h * 512, h * 512 + 512)
                dve.wait_ge(ev["out_done"], OUT_BEFORE[n] + j + 1)
                dve.tensor_tensor(TMP[:, j, :], PS[:, 4 + j % 4, :], GATE[:, v, cols],
                                  ALU.mult).then_inc(ev["out_added"], 1)
                dve.wait_ge(ev["out_added"], OUT_BEFORE[n] + j + 1)
                dve.tensor_tensor(X[:, t, cols], X[:, t, cols], TMP[:, j, :], ALU.add)

        RSC = slots[:, 5, :, :].rearrange("p k n -> p (k n)")
        mTH, mTG, mHID, mHIDT, mOB, mHGT, mHG = split(SCR[:, 2 * D:], [512, 512, 512, 512, D, D, D])
        HIDT = mHIDT.rearrange("p (f n) -> p f n", f=4)
        HGT = mHGT.rearrange("p (k n) -> p k n", k=KD)
        BACK = slots[:, 0:2, :, :].rearrange("p s k n -> p s (k n)").rearrange("p s (t n) -> p s t n", t=NT)
        MASK = sb("MASK", [P, NT, N_EXP])
        ROWI = stack.enter_context(nc.sbuf_tensor("ROWI", [P, TOP_K * NT], U32))
        JOBS = stack.enter_context(nc.sbuf_tensor("JOBS", [P, DEPTH * 32], I32))
        GSEL = sb("GSEL", [P, TOP_K * NT])
        hg = nc.dram_tensor("hg", (P * (MAX_JOBS + 1), D), F32, kind="Internal").ap()

        def router_pe(pe, n, tiles):
            for t in tiles:
                for k in range(KD):
                    mm = pe.matmul(PS[:, 7, t * 16:t * 16 + 16], HT[:, k, t * P:t * P + P],
                                   prm("router")[:, k * 16:k * 16 + 16], start=(k == 0), stop=(k == KD - 1))
            mm.then_inc(rt_ev["logits_done"], 1)
            for j, (t, h) in enumerate((t, h) for t in tiles for h in range(2)):
                if j >= 4:
                    pe.wait_ge(rt_ev["rows_copied"], OUT_BEFORE[n] + j - 3)
                for q in range(4):
                    k = 4 * h + q
                    mm = pe.transpose(PS[:, j % 4, q * P:q * P + P], HT[:, k, t * P:t * P + P], ident)
                mm.then_inc(rt_ev["rows_turned"], 1)
            pe.wait_ge(rt_ev["rows_copied"], OUT_BEFORE[n] + 2 * len(tiles))
            gate_pe(pe, 2 * n + 1, (0, 1) if n == 0 else (0,))
            pe.wait_ge(rt_ev["mask_ready"], n + 1)
            for t in tiles:
                for s in range(tiles[0], t):
                    pe.matmul(PS[:, 6, t * 16:t * 16 + 16], ones, MASK[:, s, :], start=(s == tiles[0]), stop=False)
                pe.matmul(PS[:, 6, t * 16:t * 16 + 16], cst("strict")[:, 0:P], MASK[:, t, :],
                          start=(t == tiles[0]), stop=True)
            for t in tiles:
                mm = pe.matmul(PS[:, 6, 64:80], ones, MASK[:, t, :], start=(t == tiles[0]), stop=(t == tiles[-1]))
            mm.then_inc(rt_ev["ranks_done"], 1)

        def router_act(act, n, tiles):
            a, b = tiles[0] * 16, tiles[-1] * 16 + 16
            act.wait_ge(rt_ev["logits_done"], n + 1)
            act.activation(RSC[:, a:b], PS[:, 7, a:b], ACT.Exp, scale=-1.0).then_inc(rt_ev["logits_exp"], 1)
            for j, (t, h) in enumerate((t, h) for t in tiles for h in range(2)):
                act.wait_ge(rt_ev["rows_turned"], OUT_BEFORE[n] + j + 1)
                act.activation(XN[:, t, h * 512:h * 512 + 512], PS[:, j % 4, :],
                               ACT.Copy).then_inc(rt_ev["rows_copied"], 1)
            gate_act(act, 2 * n + 1, (0, 1) if n == 0 else (0,))

        def router_dve(dve, n, tiles):
            drain = dve.drain
            nt = len(tiles)
            ng = nt * 4
            a = tiles[0] * 16
            LG, sc, sel, ms, eq, key, o1, o2, rk = [x[:, a:a + nt * 16] for x in split(RSC, [64] * 9)]
            w = RSC[:, 576:2304]
            pr = w[:, 0:ng * 6].rearrange("p (g c) -> p g c", c=6)
            gs, geq, bg, m1, m2, m3, cnt, jobs, ends, base = [
                x[:, 0:z] for x, z in zip(split(w[:, 96:], [16] * 10), (ng, ng, ng, nt, nt, nt, 16, 16, 16, 16))]
            ej = w[:, 288:288 + MAX_JOBS * 16].rearrange("p (j e) -> p j e", e=16)
            ejs = w[:, 700:700 + 32]
            rowf = w[:, 740:740 + TOP_K * NT]

            def v3(ap, c):
                return ap.rearrange("p (t c) -> p t c", c=c)

            def wide(ap, m, c):
                return ap.rearrange("p (t o) -> p t o", o=1).broadcast_to([P, m, c])

            def narrow(ap, m, c):
                return ap.rearrange("p (o c) -> p o c", o=1).broadcast_to([P, m, c])

            dve.wait_ge(rt_ev["logits_exp"], n + 1)
            dve.tensor_scalar(sc, LG, 1.0, None, ALU.add)
            drain()
            dve.reciprocal(sc, sc)
            drain()
            dve.tensor_tensor(v3(sel, 16), v3(sc, 16), narrow(row("router_b"), nt, 16), ALU.add)
            drain()
            s4 = v3(sel, 4)
            dve.tensor_tensor(pr[:, :, 0:3], s4[:, :, 1:4], s4[:, :, 0:1].broadcast_to([P, ng, 3]), ALU.add)
            dve.tensor_tensor(pr[:, :, 3:5], s4[:, :, 2:4], s4[:, :, 1:2].broadcast_to([P, ng, 2]), ALU.add)
            dve.tensor_tensor(pr[:, :, 5:6], s4[:, :, 3:4], s4[:, :, 2:3], ALU.add)
            drain()
            dve.tensor_reduce(gs, pr, AX.X, ALU.max)
            drain()

            def one_hot(out, scores, c, weights, m):
                dve.tensor_reduce(m, v3(scores, c), AX.X, ALU.max)
                drain()
                e = geq if c == 4 else eq
                dve.tensor_tensor(v3(e, c), v3(scores, c), wide(m, nt, c), ALU.is_equal)
                drain()
                dve.tensor_tensor(v3(e, c), v3(e, c), narrow(weights, nt, c), ALU.mult)
                drain()
                dve.tensor_reduce(m2, v3(e, c), AX.X, ALU.max)
                drain()
                dve.tensor_tensor(v3(out, c), v3(e, c), wide(m2, nt, c), ALU.is_equal)
                drain()

            one_hot(bg, gs, 4, cst("first4"), m1)
            dve.tensor_tensor(v3(ms, 4), s4, wide(bg, ng, 4), ALU.mult)
            dve.tensor_scalar(geq, bg, -1.0, BIG, ALU.add, ALU.mult)
            drain()
            dve.tensor_tensor(v3(ms, 4), v3(ms, 4), wide(geq, ng, 4), ALU.add)
            drain()
            one_hot(o1, ms, 16, cst("first16"), m1)
            dve.tensor_scalar(key, o1, -2 * BIG, None, ALU.mult)
            drain()
            dve.tensor_tensor(ms, ms, key, ALU.add)
            drain()
            one_hot(o2, ms, 16, cst("first16"), m1)
            dve.tensor_tensor(MASK[:, tiles[0]:tiles[0] + nt, :], v3(o1, 16), v3(o2, 16),
                              ALU.add).then_inc(rt_ev["mask_ready"], 1)
            gsel = GSEL[:].rearrange("p (k t) -> p k t", k=TOP_K)[:, :, tiles[0]:tiles[0] + nt]
            for k, o in enumerate((o1, o2)):
                dve.tensor_tensor(key, o, sc, ALU.mult)
                drain()
                dve.tensor_reduce(gsel[:, k, :], v3(key, 16), AX.X, ALU.add)
                drain()
            dve.tensor_tensor(m3, gsel[:, 0, :], gsel[:, 1, :], ALU.add)
            drain()
            dve.reciprocal(m3, m3)
            drain()
            for k in range(TOP_K):
                dve.tensor_tensor(gsel[:, k, :], gsel[:, k, :], m3, ALU.mult)
            dve.wait_ge(rt_ev["ranks_done"], n + 1)
            dve.tensor_copy(rk, PS[:, 6, a:a + nt * 16])
            dve.tensor_copy(cnt, PS[:, 6, 64:80])
            drain()
            dve.tensor_scalar(jobs, cnt, 0.0, None, ALU.is_gt)
            drain()
            for full in range(P, nt * P, P):
                dve.scalar_tensor_tensor(jobs, cnt, float(full), jobs, ALU.is_gt, ALU.add)
                drain()
            dve.tensor_tensor_scan(ends, ones[:, 0:16], jobs, 0.0, ALU.mult, ALU.add)
            drain()
            dve.tensor_tensor(base, ends, jobs, ALU.subtract)
            dve.tensor_tensor(ej, narrow(ends, MAX_JOBS, 16), wide(cst("job_index"), MAX_JOBS, 16), ALU.is_le)
            drain()
            dve.tensor_reduce(ejs[:, 0:MAX_JOBS], ej, AX.X, ALU.add)
            drain()
            dve.tensor_scalar(ejs[:, 0:MAX_JOBS], ejs[:, 0:MAX_JOBS], float(N_EXP - 1), None, ALU.min)
            dve.tensor_copy(ejs[:, MAX_JOBS:MAX_JOBS + 1], ends[:, 15:16])
            dve.scalar_tensor_tensor(v3(rk, 16), narrow(base, nt, 16), float(P), v3(rk, 16), ALU.mult, ALU.add)
            drain()
            dve.tensor_copy(JOBS[:, 32 * n:32 * n + MAX_JOBS + 1], ejs[:, 0:MAX_JOBS + 1]).then_inc(rt_ev["jobs_ready"], 1)
            for k, o in enumerate((o1, o2)):
                dve.tensor_tensor(key, o, rk, ALU.mult)
                drain()
                dve.tensor_reduce(rowf[:, k * NT + tiles[0]:k * NT + tiles[0] + nt], v3(key, 16), AX.X, ALU.add)
                drain()
            for k in range(TOP_K):
                c = slice(k * NT + tiles[0], k * NT + tiles[0] + nt)
                ins = dve.tensor_copy(ROWI[:, c], rowf[:, c])
            ins.then_inc(rt_ev["rows_ready"], 1)

        def rows_pool(pool, n, tiles):
            for v in ((0, 1) if n == 0 else (0,)):
                for k in range(KD):
                    ins = pool.tensor_scalar(DIAG[:, v, k * P:k * P + P], ident,
                                             mod[:, n, 5 * KD + k, v:v + 1], None, ALU.mult)
            ins.then_inc(gate_ev["gate_diag"], 1)
            pool.wait_ge(rt_ev["rows_copied"], OUT_BEFORE[n] + 2 * len(tiles))
            pool.wait_ge(rt_ev["rows_ready"], n + 1)
            for k in range(TOP_K):
                for t in tiles:
                    pool.indirect_dma_start(hg, bass.IndirectOffsetOnAxis(ROWI[:, k * NT + t:k * NT + t + 1], 0),
                                            XN[:, t, :], None).then_inc(rt_ev["rows_scattered"], 16)

        def back_pool(pool, n, tiles):
            J, b = jobs_of(pool, n)
            pool.wait_ge(moe_ev["o_stored"], (b + J) * 16 + 16)
            pool.tensor_tensor(SS[:, 60:61], ident[:, 0:1], ident[:, 0:1], ALU.mult)
            for k in range(TOP_K):
                for t in tiles:
                    pool.indirect_dma_start(BACK[:, k, t, :], None, hg,
                                            bass.IndirectOffsetOnAxis(ROWI[:, k * NT + t:k * NT + t + 1], 0)
                                            ).then_inc(rt_ev["rows_back"], 16)

        def jobs_of(eng, n):
            eng.wait_ge(rt_ev["jobs_ready"], n + 1)
            J = [eng.value_load(JOBS[0:1, 32 * x + MAX_JOBS:32 * x + MAX_JOBS + 1], min_val=1, max_val=MAX_JOBS)
                 for x in range(n, -1, -1)]
            return J[0], (J[1] if n == 1 else 0)

        MOE_SLOTS = (2, 3, 4)

        def moe_pe(pe, n):
            ev = moe_ev
            J, b = jobs_of(pe, n)
            sg, su, sd = MOE_SLOTS
            if n == 0:
                pe.drain().then_inc(ev["gate_done"], 1)
                pe.drain().then_inc(ev["up_done"], 1)
                pe.drain().then_inc(ev["down_done"], 2)

            def turn(j):
                pe.wait_ge(ev["hg_loaded"], (b + j) * 16 + 16 * (n + 1))
                for k in range(KD):
                    mm = pe.transpose(PS[:, k // 4, k % 4 * P:k % 4 * P + P], mHG[:, k * P:k * P + P], ident)
                mm.then_inc(ev["x_turned"], 1)

            turn(0)
            with pe.Fori(0, J) as j:
                q = b + j
                pe.wait_ge(ev["x_copied"], q * 2 + 2 * (n + 1))
                pe.wait_ge(ev["w_gate"], q * 16 + 16)
                for k in range(KD):
                    mm = pe.matmul(PS[:, 2, :], HGT[:, k, :], slots[:, sg, k, :], start=(k == 0), stop=(k == KD - 1))
                mm.then_inc(ev["gate_done"], 1)
                pe.wait_ge(ev["w_up"], q * 16 + 16)
                for k in range(KD):
                    mm = pe.matmul(PS[:, 3, :], HGT[:, k, :], slots[:, su, k, :], start=(k == 0), stop=(k == KD - 1))
                mm.then_inc(ev["up_done"], 1)
                turn(j + 1)
                pe.wait_ge(ev["hidden"], q + 1)
                for f in range(4):
                    mm = pe.transpose(PS[:, 4, f * P:f * P + P], mHID[:, f * P:f * P + P], ident)
                mm.then_inc(ev["hid_turned"], 1)
                pe.wait_ge(ev["hid_copied"], q + 1)
                pe.wait_ge(ev["w_down"], q * 16 + 16)
                pe.wait_ge(ev["o_copied"], q * 2 + 2)
                wd = slots[:, sd, :, :].rearrange("p (f h) n -> p f h n", h=2)
                for h in range(2):
                    for f in range(4):
                        mm = pe.matmul(PS[:, 5 + h, :], HIDT[:, f, :], wd[:, f, h, :], start=(f == 0), stop=(f == 3))
                    mm.then_inc(ev["down_done"], 1)

        def moe_act(act, n):
            ev = moe_ev
            J, b = jobs_of(act, n)

            def copy_x(j):
                act.wait_ge(ev["x_turned"], b + j + n + 1)
                act.activation(mHGT[:, 0:512], PS[:, 0, :], ACT.Copy).then_inc(ev["x_copied"], 1)

            copy_x(0)
            with act.Fori(0, J) as j:
                q = b + j
                act.wait_ge(ev["gate_done"], q + 2)
                act.activation(mTH, PS[:, 2, :], ACT.Tanh, scale=0.5).then_inc(ev["tanh"], 1)
                copy_x(j + 1)
                act.wait_ge(ev["hid_turned"], q + 1)
                act.activation(mHIDT, PS[:, 4, :], ACT.Copy).then_inc(ev["hid_copied"], 1)
                act.wait_ge(ev["down_done"], q * 2 + 3)
                act.wait_ge(ev["o_stored"], q * 16 + 16)
                act.activation(mOB[:, 0:512], PS[:, 5, :], ACT.Copy).then_inc(ev["o_copied"], 1)
                act.wait_ge(ev["o_copied"], q * 2 + 4)
                act.dma_start(hg[ds(j * P, P), :], mOB).then_inc(ev["o_stored"], 16)

        def moe_dve(dve, n):
            ev = moe_ev
            J, b = jobs_of(dve, n)
            if n == 0:
                dve.drain().then_inc(ev["o_copied"], 2)
                dve.drain().then_inc(ev["o_stored"], 16)

            def copy_x(j):
                dve.wait_ge(ev["x_turned"], b + j + n + 1)
                dve.tensor_copy(mHGT[:, 512:1024], PS[:, 1, :]).then_inc(ev["x_copied"], 1)

            copy_x(0)
            with dve.Fori(0, J) as j:
                q = b + j
                dve.wait_ge(ev["tanh"], q + 1)
                dve.scalar_tensor_tensor(mTG, mTH, 1.0, PS[:, 2, :], ALU.add, ALU.mult)
                dve.drain()
                dve.wait_ge(ev["up_done"], q + 2)
                dve.scalar_tensor_tensor(mHID, mTG, 0.5, PS[:, 3, :], ALU.mult, ALU.mult).then_inc(ev["hidden"], 1)
                copy_x(j + 1)
                dve.wait_ge(ev["down_done"], q * 2 + 4)
                dve.wait_ge(ev["o_stored"], q * 16 + 16)
                dve.tensor_copy(mOB[:, 512:1024], PS[:, 6, :]).then_inc(ev["o_copied"], 1)

        def moe_end_dve(dve, n, tiles):
            dve.wait_ge(gate_ev["gate_copied"], 2 * n + 2)
            dve.wait_ge(rt_ev["rows_back"], 16 * TOP_K * (4 * n + len(tiles)))
            for t in tiles:
                y = XN[:, t, :]
                dve.tensor_scalar(y, BACK[:, 0, t, :], GSEL[:, t:t + 1], None, ALU.mult)
                dve.drain()
                dve.scalar_tensor_tensor(y, BACK[:, 1, t, :], GSEL[:, NT + t:NT + t + 1], y, ALU.mult, ALU.add)
                dve.drain()
                dve.tensor_tensor(y, y, GATE[:, 1 if t < 2 else 0, :], ALU.mult)
                dve.drain()
                dve.tensor_tensor(X[:, t, :], X[:, t, :], y, ALU.add)

        ADA_BASE = [0] * NSLOT
        EVEN_BASE = [64] * NSLOT
        OUT0_READY = [64 + 96 + 16, 64 + 64 + 16]
        ODD_BASE = [OUT0_READY[0], OUT0_READY[1], 64 + 96, 64, 64, 64]

        ESC = slots[:, 3:6, :, :].rearrange("p s k n -> p (s k n)")
        eU, eS, eATT, eQK, eO = split(ESC, [4096, 4096, 2048, 1024, 1024])
        U3 = eU.rearrange("p (n e) -> p n e", n=NCH)
        S3 = eS.rearrange("p (n e) -> p n e", n=NCH)
        ATT4 = eATT.rearrange("p (h t q) -> p h t q", h=4, t=NT)
        QK = eQK.rearrange("p (a n) -> p a n", a=2)
        O3 = eO.rearrange("p (t n) -> p t n", t=NT)
        gVG, gA, gC, gG, gQH, gKH, gKT, gF, gW = split(SCR[:, :], [2048, 1024, 1024, 1024, 1024, 1024, 512, 128, 260])
        VG = gVG.rearrange("p (t n) -> p t n", t=NT)
        A2, C2, G2, QH, KH = [b.rearrange("p (d n) -> p d n", d=2) for b in (gA, gC, gG, gQH, gKH)]
        ZD = QH
        F3 = gF[:, 0:32].rearrange("p (d n) -> p d n", d=2)
        DN = gF[:, 32:64].rearrange("p (d n) -> p d n", d=2)
        GW = gW
        gla = {k: sem(f"gla_{k}") for k in (
            "small", "abs", "proj", "qkv_stored", "zd", "logits", "soft", "expo", "exp", "kh", "kturned", "ktok", "ds",
            "ds_masked", "states", "att", "att_masked", "out", "out_stored", "ss", "rstd", "cat")}
        att = {k: sem(f"att_{k}") for k in (
            "proj", "stored", "ss", "rstd", "qk", "turned", "tstored", "scores", "max", "exp", "es", "pturned",
            "pt_stored", "pv", "out")}
        even_part = sem("even_part")
        aAQ, aSQ, aQT, aP, aPT, aR, aM = split(ESC, [1536, 1280, 2560, 1024, 1024, 1280, 128])
        AQ = aAQ.rearrange("p (t n) -> p t n", t=NT)
        SQ = aSQ.rearrange("p (t n) -> p t n", t=NT)
        QT = aQT.rearrange("p (h n) -> p h n", h=5)
        PB = aP.rearrange("p (b n) -> p b n", b=2)
        PTB = aPT.rearrange("p (b n) -> p b n", b=2)
        RT = [r.rearrange("p (t h n) -> p t h n", t=2, h=5) for r in split(aR, [320] * 4)]
        aMX, aNM, aRS, aES, aRD, aSK = split(aM, [16] * 5 + [4])
        ORD = (list(range(NCH)), list(range(NCH // 2 - 1, -1, -1)) + list(range(NCH - 1, NCH // 2 - 1, -1)))

        def gla_pe(pe, i, base):
            def w_wait(s, n, per):
                pe.wait_ge(w_ready[s], i * per + base[s] + n)

            w_wait(0, 48, 48)
            for a in range(2):
                for k in range(KD):
                    mm = pe.matmul(PS[:, a, :], slots[:, 0, k, a * P:a * P + P], HT[:, k, :],
                                   start=(k == 0), stop=(k == KD - 1))
                mm.then_inc(gla["proj"], 1)
            w_wait(1, 32, 32)
            for d in range(2):
                for k in range(KD):
                    mm = pe.matmul(PS[0:16, 2 + d, :], slots[:, 1, k, 256 + 16 * d:272 + 16 * d], HT[:, k, :],
                                   start=(k == 0), stop=(k == KD - 1))
            mm.then_inc(gla["proj"], 1)
            for t in range(NT):
                for s, c0 in ((0, 256), (1, 0)):
                    for k in range(KD):
                        mm = pe.matmul(PS[:, 4 + t, 256 * s:256 * s + 256], HT[:, k, t * P:t * P + P],
                                       slots[:, s, k, c0:c0 + 256], start=(k == 0), stop=(k == KD - 1))
                mm.then_inc(gla["proj"], 1)
            pe.wait_ge(gla["small"], 16 * i + 16)
            pe.wait_ge(gla["zd"], i + 1)
            for d in range(2):
                mm = pe.matmul(PS[:, 2 + d, :], GW[0:16, d * P:d * P + P], ZD[0:16, d, :], start=True, stop=True)
            mm.then_inc(gla["logits"], 1)
            pe.wait_ge(gla["qkv_stored"], 6 * i + 6)
            pe.wait_ge(gla["kh"], i + 1)
            for d in range(2):
                if d == 1:
                    pe.wait_ge(gla["att_masked"], 2 * i + 1)
                for t in range(NT):
                    mm = pe.transpose(PS[:, 0, t * P:t * P + P], KH[:, d, t * P:t * P + P], ident)
                mm.then_inc(gla["kturned"], 1)
                if d == 1:
                    pe.wait_ge(gla["out_stored"], 8 * i + 4)
                pe.wait_ge(gla["ktok"], 2 * i + d + 1)
                for pr in range(2):
                    if pr == 1:
                        pe.wait_ge(gla["ds_masked"], 4 * i + 2 * d + 1)
                    for c in range(4):
                        for tt in range(2):
                            t = 2 * pr + tt
                            mm = pe.matmul(PS[:, 4 + c, tt * 256:tt * 256 + 256], gKT[32 * c:32 * c + 32, t * P:t * P + P],
                                           VG[32 * c:32 * c + 32, t, 0:256], start=True, stop=True)
                    mm.then_inc(gla["ds"], 1)
                for h in range(4):
                    for t in range(NT):
                        mm = pe.matmul(PS[:, h, t * P:t * P + P], KH[32 * h:32 * h + 32, d, t * P:t * P + P],
                                       QH[32 * h:32 * h + 32, d, t * P:t * P + P], start=True, stop=True)
                mm.then_inc(gla["att"], 1)
                pe.wait_ge(gla["states"], 2 * i + d + 1)
                pe.wait_ge(gla["att_masked"], 2 * i + d + 1)
                for t in range(NT):
                    for c in range(4):
                        pe.matmul(PS[32 * c:32 * c + 32, 4 + t, 0:256], QH[:, d, t * P + 32 * c:t * P + 32 * c + 32],
                                  S3[:, 4 * t + c, :], start=True, stop=False, skip_group_check=True)
                    for h in range(4):
                        mm = pe.matmul(PS[:, 4 + t, 64 * h:64 * h + 64], ATT4[:, h, t, :],
                                       VG[:, t, 64 * h:64 * h + 64], start=False, stop=(h == 3), skip_group_check=True)
                    mm.then_inc(gla["out"], 1)

        def gla_act(act, i):
            for a in range(2):
                act.wait_ge(gla["proj"], 7 * i + a + 1)
                act.activation(QK[:, a, :], PS[:, a, :], ACT.Copy,
                               scale=GLA_DK ** -0.5 if a == 0 else 1.0).then_inc(gla["qkv_stored"], 1)
            for t in range(NT):
                act.wait_ge(gla["proj"], 7 * i + 4 + t)
                act.activation(VG[:, t, :], PS[:, 4 + t, :], ACT.Copy).then_inc(gla["qkv_stored"], 1)
            act.wait_ge(gla["logits"], i + 1)
            act.wait_ge(gla["small"], 16 * i + 16)
            for d in range(2):
                act.activation(A2[:, d, :], PS[:, 2 + d, :], ACT.Abs,
                               bias=GW[:, 256 + d:257 + d]).then_inc(gla["abs"], 1)
            act.drain()
            act.activation(gA, gA, ACT.Exp, scale=-1.0)
            act.drain()
            act.activation(gA, gA, ACT.Ln, bias=1.0).then_inc(gla["soft"], 1)
            act.wait_ge(gla["expo"], i + 1)
            act.activation(gQH, gA, ACT.Exp, scale=1.0 / GLA_TAU)
            act.activation(gKH, gA, ACT.Exp, scale=-1.0 / GLA_TAU)
            act.activation(gF[:, 0:32], gF[:, 0:32], ACT.Exp, scale=1.0 / GLA_TAU).then_inc(gla["exp"], 1)
            for d in range(2):
                act.wait_ge(gla["kturned"], 2 * i + d + 1)
                if d == 1:
                    act.wait_ge(gla["ds"], 4 * i + 2)
                act.activation(gKT, PS[:, 0, :], ACT.Copy).then_inc(gla["ktok"], 1)
            act.wait_ge(gla["ss"], i + 1)
            act.activation(RS[:, 0:16], SS[:, 0:16], ACT.Ln, scale=1.0 / GLA_DV, bias=EPS[:, 0:1])
            act.drain()
            act.activation(RS[:, 0:16], RS[:, 0:16], ACT.Exp, scale=-0.5)
            act.activation(gKH.rearrange("p (t n) -> p t n", t=NT), VG[:, :, 256:512], ACT.Tanh,
                           scale=0.5).then_inc(gla["rstd"], 1)

        def gla_dve(dve, i):
            drain = dve.drain
            dve.wait_ge(gla["proj"], 7 * i + 3)
            dve.tensor_copy(ZD[0:16, :, :], PS[0:16, 2:4, :]).then_inc(gla["zd"], 1)
            dve.wait_ge(gla["small"], 16 * i + 16)
            dve.wait_ge(gla["abs"], 2 * i + 2)
            for d in range(2):
                dve.tensor_scalar(G2[:, d, :], PS[:, 2 + d, :], GW[:, 256 + d:257 + d], 0.0, ALU.add, ALU.min)
            drain()
            dve.wait_ge(gla["soft"], i + 1)
            dve.tensor_tensor(gG, gG, gA, ALU.subtract)
            drain()
            for d in range(2):
                dve.tensor_tensor_scan(C2[:, d, :], cst("reset32"), G2[:, d, :], 0.0, ALU.mult, ALU.add)
            drain()
            cv = gC.rearrange("p (n s) -> p n s", s=GLA_C)
            dve.tensor_tensor(gA.rearrange("p (n s) -> p n s", s=GLA_C), cv,
                              cv[:, :, 15:16].broadcast_to([P, 2 * NCH, GLA_C]), ALU.subtract)
            c4 = gC.rearrange("p (d n s) -> p d n s", d=2, s=GLA_C)
            dve.tensor_tensor(DN, c4[:, :, :, 31], c4[:, :, :, 15], ALU.subtract)
            drain()
            dve.tensor_tensor(A2[:, 1, :], G2[:, 1, :], A2[:, 1, :], ALU.subtract)
            n = NCH - 1
            dve.memset(F3[:, 0, n:NCH], 0.0)
            dve.tensor_tensor(F3[:, 0, 0:n], DN[:, 0, 0:n], c4[:, 0, 1:NCH, 15], ALU.add)
            dve.tensor_tensor(F3[:, 1, 1:NCH], DN[:, 1, 0:n], c4[:, 1, 1:NCH, 15], ALU.add)
            dve.tensor_tensor(F3[:, 1, 0:1], DN[:, 1, n:NCH], c4[:, 1, 0:1, 15], ALU.add)
            drain()
            dve.tensor_scalar(gA, gA, 85.0 * GLA_TAU, -85.0 * GLA_TAU, ALU.min, ALU.max).then_inc(gla["expo"], 1)
            dve.wait_ge(gla["exp"], i + 1)
            dve.wait_ge(gla["qkv_stored"], 6 * i + 6)
            for d in range(2):
                dve.tensor_tensor(QH[:, d, :], QH[:, d, :], QK[:, 0, :], ALU.mult)
                ins = dve.tensor_tensor(KH[:, d, :], KH[:, d, :], QK[:, 1, :], ALU.mult)
            ins.then_inc(gla["kh"], 1)
            heads = cst("gla_heads").rearrange("p (o e) -> p o e", o=1).broadcast_to([P, 2, 256])
            for d in range(2):
                u4 = eU.rearrange("p (t c e) -> p t c e", t=NT, c=4)
                for pr in range(2):
                    dve.wait_ge(gla["ds"], 4 * i + 2 * d + pr + 1)
                    for c in range(4):
                        ins = dve.tensor_tensor(u4[:, 2 * pr:2 * pr + 2, c, :],
                                                PS[:, 4 + c, :].rearrange("p (t e) -> p t e", t=2), heads, ALU.mult)
                    ins.then_inc(gla["ds_masked"], 1)
                dve.memset(S3[:, ORD[d][0], :], 0.0)
                drain()
                for a, n in zip(ORD[d], ORD[d][1:]):
                    f = F3[:, d, a:a + 1]
                    dve.tensor_scalar(S3[:, n, :], U3[:, a, :], f, None, ALU.mult)
                    dve.scalar_tensor_tensor(U3[:, n, :], U3[:, a, :], f, U3[:, n, :], ALU.mult, ALU.add)
                    drain()
                drain().then_inc(gla["states"], 1)
                dve.wait_ge(gla["att"], 2 * i + d + 1)
                mask = (cst("gla_incl")[:, d * P:d * P + P].rearrange("p (o q) -> p o q", o=1)
                        .broadcast_to([P, NT, P]))
                for h in range(4):
                    ins = dve.tensor_tensor(ATT4[:, h, :, :], PS[:, h, :].rearrange("p (t q) -> p t q", t=NT),
                                            mask, ALU.mult)
                ins.then_inc(gla["att_masked"], 1)
                for t in range(NT):
                    dve.wait_ge(gla["out"], 8 * i + 4 * d + t + 1)
                    if d == 0:
                        dve.tensor_copy(O3[:, t, :], PS[:, 4 + t, 0:256]).then_inc(gla["out_stored"], 1)
                    else:
                        dve.tensor_tensor(O3[:, t, :], O3[:, t, :], PS[:, 4 + t, 0:256],
                                          ALU.add).then_inc(gla["out_stored"], 1)
                drain()
            o16 = eO.rearrange("p (g e) -> p g e", e=GLA_DV)
            q16 = gQH.rearrange("p (g e) -> p g e", e=GLA_DV)
            dve.tensor_tensor(gQH, eO, eO, ALU.mult)
            drain()
            dve.tensor_reduce(SS[:, 0:16], q16, AX.X, ALU.add).then_inc(gla["ss"], 1)
            dve.wait_ge(gla["rstd"], i + 1)
            dve.tensor_tensor(o16, o16, RS[:, 0:16].rearrange("p (g o) -> p g o", o=1).broadcast_to([P, 16, GLA_DV]),
                              ALU.mult)
            dve.scalar_tensor_tensor(QH[:, :, :].rearrange("p d (t n) -> p (d t) n", t=2),
                                     gKH.rearrange("p (t n) -> p t n", t=NT), 1.0, VG[:, :, 256:512], ALU.add, ALU.mult)
            drain()
            dve.tensor_tensor(o16, o16, row("gla_gain").rearrange("p (o e) -> p o e", o=1).broadcast_to([P, 16, GLA_DV]),
                              ALU.mult)
            drain()
            dve.scalar_tensor_tensor(XN[:, :, ds(i * 256, 256)], O3, 0.5,
                                     gQH.rearrange("p (t n) -> p t n", t=NT), ALU.mult, ALU.mult)

        UNITS = [(h, t) for h in range(GRP) for t in range(NT)]
        NU = len(UNITS)

        def att_pe(pe, i, base):
            pe.wait_ge(w_ready[2], i * 48 + base[2] + 48)
            for t in range(NT):
                for k in range(KD):
                    mm = pe.matmul(PS[:, t, 0:384], HT[:, k, t * P:t * P + P], slots[:, 2, k, 0:384],
                                   start=(k == 0), stop=(k == KD - 1))
                mm.then_inc(att["proj"], 1)
            pe.wait_ge(att["qk"], i + 1)
            for h in range(5):
                for t in range(NT):
                    src, dst = AQ[:, t, h * HD:h * HD + HD], PS[0:HD, (4 + h) % 8, t * P:t * P + P]
                    if h == 0 and t == 0:
                        mm = pe.matmul(dst, src, ident, start=True, stop=True)
                    else:
                        mm = pe.transpose(dst, src, ident)
                mm.then_inc(att["turned"], 1)
            pe.wait_ge(att["tstored"], 5 * i + 5)
            for u in range(NU + 2):
                if u < NU:
                    h, t = UNITS[u]
                    nk = T if t >= 2 else SEG
                    if u >= 2:
                        pe.wait_ge(att["exp"], NU * i + u - 1)
                    pe.matmul(PS[:, u % 2, 0:nk], QT[0:HD, h, t * P:t * P + P], QT[0:HD, 4, 0:nk], start=True,
                              stop=True).then_inc(att["scores"], 1)
                if 1 <= u <= NU:
                    v = u - 1
                    pe.wait_ge(att["exp"], NU * i + v + 1)
                    if v >= 2:
                        pe.wait_ge(att["pt_stored"], NU * i + v - 1)
                    for c in range(4 if UNITS[v][1] >= 2 else 2):
                        mm = pe.transpose(PS[:, 2 + v % 2, c * P:c * P + P], PB[:, v % 2, c * P:c * P + P], ident)
                    mm.then_inc(att["pturned"], 1)
                if u >= 2:
                    v = u - 2
                    pe.wait_ge(att["pt_stored"], NU * i + v + 1)
                    if v >= 2:
                        pe.wait_ge(att["out"], NU * i + v - 1)
                    nt = 4 if UNITS[v][1] >= 2 else 2
                    for c in range(nt):
                        mm = pe.matmul(PS[:, 4 + v % 2, 0:HD], PTB[:, v % 2, c * P:c * P + P], AQ[:, c, 320:384],
                                       start=(c == 0), stop=(c == nt - 1))
                    mm.then_inc(att["pv"], 1)

        def att_act(act, i):
            for t in range(NT):
                act.wait_ge(att["proj"], NT * i + t + 1)
                act.activation(AQ[:, t, :], PS[:, t, 0:384], ACT.Copy).then_inc(att["stored"], 1)
            act.wait_ge(att["ss"], i + 1)
            act.activation(RS[:, 0:20], SS[:, 0:20], ACT.Ln, scale=1.0 / HD, bias=EPS[:, 0:1])
            act.drain()
            act.activation(RS[:, 0:20], RS[:, 0:20], ACT.Exp, scale=-0.5).then_inc(att["rstd"], 1)
            for h in range(5):
                act.wait_ge(att["turned"], 5 * i + h + 1)
                act.activation(QT[0:HD, h, :], PS[0:HD, (4 + h) % 8, :], ACT.Copy).then_inc(att["tstored"], 1)
            for u in range(NU + 1):
                if u < NU:
                    h, t = UNITS[u]
                    nk = T if t >= 2 else SEG
                    act.wait_ge(att["max"], NU * i + u + 1)
                    if u >= 2:
                        act.wait_ge(att["pturned"], NU * i + u - 1)
                    act.activation(PB[:, u % 2, 0:nk], PS[:, u % 2, 0:nk], ACT.Exp, scale=HD ** -0.5,
                                   bias=aNM[:, u:u + 1], accum_out=aRS[:, u:u + 1]).then_inc(att["exp"], 1)
                    act.activation(aES[:, u:u + 1], aSK[:, h:h + 1], ACT.Exp, bias=aNM[:, u:u + 1]).then_inc(att["es"], 1)
                if u >= 1:
                    v = u - 1
                    nk = T if UNITS[v][1] >= 2 else SEG
                    act.wait_ge(att["pturned"], NU * i + v + 1)
                    if v >= 2:
                        act.wait_ge(att["pv"], NU * i + v - 1)
                    act.activation(PTB[:, v % 2, 0:nk], PS[:, 2 + v % 2, 0:nk], ACT.Copy).then_inc(att["pt_stored"], 1)

        def att_dve(dve, i):
            drain = dve.drain
            dve.tensor_copy(aSK, row("sink")[:, ds(i * GRP, GRP)])
            dve.wait_ge(att["stored"], NT * i + NT)
            qk = AQ[:, :, 0:320]
            dve.tensor_tensor(SQ, qk, qk, ALU.mult)
            drain()
            dve.tensor_reduce(SS[:, 0:20], aSQ.rearrange("p (g e) -> p g e", e=HD), AX.X, ALU.add).then_inc(att["ss"], 1)
            dve.wait_ge(att["rstd"], i + 1)
            for t in range(NT):
                a3 = AQ[:, t, 0:320].rearrange("p (h e) -> p h e", h=5)
                dve.tensor_tensor(a3, a3, RS[:, 5 * t:5 * t + 5].rearrange("p (h o) -> p h o", o=1)
                                  .broadcast_to([P, 5, HD]), ALU.mult)
            drain()
            dve.tensor_tensor(qk, qk, row("qk_gain").rearrange("p (o n) -> p o n", o=1).broadcast_to([P, NT, 320]),
                              ALU.mult)
            drain()
            r4 = cst("rope").rearrange("p (c t n) -> p c t n", c=2, t=2)
            for t in range(2):
                a3 = AQ[:, 2 + t, 0:320].rearrange("p (h e) -> p h e", h=5)
                a, b = a3[:, :, 0:32], a3[:, :, 32:64]
                c, s = [r4[:, x, t, :].rearrange("p (o n) -> p o n", o=1).broadcast_to([P, 5, 32]) for x in range(2)]
                for buf, u, v in ((0, a, c), (1, b, s), (2, a, s), (3, b, c)):
                    dve.tensor_tensor(RT[buf][:, t, :, :], u, v, ALU.mult)
            drain()
            for t in range(2):
                a3 = AQ[:, 2 + t, 0:320].rearrange("p (h e) -> p h e", h=5)
                dve.tensor_tensor(a3[:, :, 0:32], RT[0][:, t, :, :], RT[1][:, t, :, :], ALU.subtract)
                ins = dve.tensor_tensor(a3[:, :, 32:64], RT[2][:, t, :, :], RT[3][:, t, :, :], ALU.add)
            ins.then_inc(att["qk"], 1)
            for u in range(NU + 2):
                if u < NU:
                    h, t = UNITS[u]
                    nk = T if t >= 2 else SEG
                    dve.wait_ge(att["scores"], NU * i + u + 1)
                    if t >= 2:
                        kt = 5 - t
                        blk = PS[:, u % 2, kt * P:kt * P + P]
                        dve.tensor_tensor(blk, blk, cst("att_mask")[:, (t - 2) * P:(t - 1) * P], ALU.add)
                        drain()
                    dve.tensor_reduce(aMX[:, u:u + 1], PS[:, u % 2, 0:nk], AX.X, ALU.max)
                    drain()
                    dve.tensor_scalar(aMX[:, u:u + 1], aMX[:, u:u + 1], HD ** -0.5, aSK[:, h:h + 1], ALU.mult, ALU.max)
                    drain()
                    dve.tensor_scalar(aNM[:, u:u + 1], aMX[:, u:u + 1], -1.0, None, ALU.mult).then_inc(att["max"], 1)
                if u >= 2:
                    v = u - 2
                    h, t = UNITS[v]
                    dve.wait_ge(att["es"], NU * i + v + 1)
                    dve.tensor_tensor(aRD[:, v:v + 1], aRS[:, v:v + 1], aES[:, v:v + 1], ALU.add)
                    drain()
                    dve.reciprocal(aRD[:, v:v + 1], aRD[:, v:v + 1])
                    drain()
                    dve.wait_ge(att["pv"], NU * i + v + 1)
                    dve.tensor_scalar(XN[:, t, ds(i * 256 + 512 + h * HD, HD)], PS[:, 4 + v % 2, 0:HD],
                                      aRD[:, v:v + 1], None, ALU.mult).then_inc(att["out"], 1)

        def turn_pe(pe):
            for k in range(KD):
                for t in range(NT):
                    mm = pe.transpose(PS[:, k, t * P:t * P + P], XN[:, t, k * P:k * P + P], ident)
                mm.then_inc(cat_turned_k, 1)

        def turn_copy(eng, ks):
            for k in ks:
                eng.wait_ge(cat_turned_k, k + 1)
                if eng.engine == nc.scalar.engine:
                    eng.activation(HT[:, k, :], PS[:, k, :], ACT.Copy)
                else:
                    eng.tensor_copy(HT[:, k, :], PS[:, k, :])

        def turned_meet(eng):
            eng.drain().then_inc(cat_turned, 1)
            eng.wait_ge(cat_turned, ENGINES)

        L2 = SEG
        ODD1 = slots[:, 1, :, :].rearrange("p k n -> p (k n)")
        ODD45 = slots[:, 4:6, :, :].rearrange("p s k n -> p (s k n)")
        XNF = XN[:].rearrange("p t n -> p (t n)")
        CATT, oTW, oZA, oSG, oPV, oPD, oLW, oBON = split(XNF, [KD * L2, T, T, L2, 12, 12, 384, L2])
        oG, oC, oE, oB, oKD, oPP, oPX, oS, oWS, oUS, oRZ, oF = split(
            SCR[:, :], [2 * T] * 6 + [T, 256, 256, 256, L2, 32])
        oXT, oMK, oNN, oTA = split(ODD45, [2048, 2048, 2048, 2048])
        oTB, oKZ, oVZ, oKK, oVT = split(ODD1, [2048, T, T, T, T])
        G_, C_, E_, B_, KD_, PP_, PX_ = [b.rearrange("p (d n) -> p d n", d=2) for b in (oG, oC, oE, oB, oKD, oPP, oPX)]
        BT_, KT_ = E_, G_
        ST_, WS_, US_ = [b.rearrange("p (d n) -> p d n", d=2) for b in (oS, oWS, oUS)]
        XT_, MK_, NN_ = [b.rearrange("p (d h c n) -> p d h c n", d=2, h=2, c=4) for b in (oXT, oMK, oNN)]
        LTS, XX, MT, T1 = zip(*[[x.rearrange("p (c n) -> p c n", c=4) for x in split(b, [512] * 4)] for b in (oTA, oTB)])
        ZP = [b.rearrange("p (s n) -> p s n", s=2) for b in split(oTA, [516, 516, 516])]
        MIXT, AVG = split(oTB, [512, 512])
        FZ = oXT[:, 0:512].rearrange("p (t n) -> p t n", t=2)
        FB = oMK[:, 0:1024].rearrange("p (m n) -> p m n", m=2)
        oMID, oDN, oFF = [x.rearrange("p (d c) -> p d c", d=2) for x in split(oF, [8, 8, 8])]
        pre = {k: sem(f"pre_{k}") for k in ("proj", "stored", "mixed", "four", "four_stored", "four_tok",
                                            "four_tok_stored", "four_ch")}
        rw = {k: sem(f"rw_{k}") for k in (
            "small", "derived", "proj", "lora", "zp", "tanh_w", "tanh_a", "sq", "kksum", "kkrs", "v", "vturned",
            "vstored", "expo", "exps", "hat", "tok", "tok_stored", "gram", "lt", "gram_read", "mt", "t1",
            "t1s", "p", "x", "w", "ws", "u", "us", "ds", "s", "y", "yb", "mean", "ysq", "var", "rstd", "bonus", "g2")}
        odd_part = sem("odd_part")
        RORD = ((0, 1, 2, 3), (1, 0, 3, 2))
        NL = len(LEVELS)

        def odd_meet(eng, value):
            eng.drain().then_inc(odd_part, 1)
            eng.wait_ge(odd_part, value)

        def odd_pre_pe(pe):
            pe.wait_ge(w_ready[2], ODD_BASE[2] + 16)
            for x in range(3):
                c0 = L2 if x == 2 else 0
                for k in range(KD):
                    mm = pe.matmul(PS[:, x, c0:T], slots[:, 2, k, x * P:x * P + P], HT[:, k, c0:T],
                                   start=(k == 0), stop=(k == KD - 1))
                mm.then_inc(pre["proj"], 1)
            pe.wait_ge(w_ready[3], ODD_BASE[3] + 16)
            for t in range(2):
                for k in range(KD):
                    mm = pe.matmul(PS[:, 3 + t, 0:FOUR], HT[:, k, L2 + t * P:L2 + t * P + P], slots[:, 3, k, 0:FOUR],
                                   start=(k == 0), stop=(k == KD - 1))
            mm.then_inc(pre["four"], 1)
            pe.wait_ge(pre["four_stored"], 1)
            tok = cst("dft_tok").rearrange("p (t n) -> p t n", t=2)
            for m in range(2):
                for t in range(2):
                    mm = pe.matmul(PS[:, 5 + m, :], FZ[:, t, m * P:m * P + P], tok[:, t, :],
                                   start=(t == 0), stop=(t == 1))
            mm.then_inc(pre["four_tok"], 1)
            pe.wait_ge(pre["four_tok_stored"], 1)
            for m in range(2):
                for s in range(2):
                    mm = pe.matmul(PS[:, 7, m * L2:m * L2 + L2], cst("dft_ch")[:, s * P:s * P + P],
                                   FB[:, m, s * L2:s * L2 + L2], start=(s == 0), stop=(s == 1))
            mm.then_inc(pre["four_ch"], 1)

        def odd_pre_act(act):
            for x in range(3):
                s0 = 1 if x == 2 else 0
                act.wait_ge(pre["proj"], x + 1)
                act.activation(ZP[x][:, s0:2, 1:L2 + 1], PS[:, x, s0 * L2:T].rearrange("p (s n) -> p s n", n=L2),
                               ACT.Copy).then_inc(pre["stored"], 1)
            act.wait_ge(pre["four"], 1)
            act.activation(FZ, PS[:, 3:5, 0:FOUR], ACT.Copy).then_inc(pre["four_stored"], 1)
            act.wait_ge(pre["four_tok"], 1)
            act.activation(FB, PS[:, 5:7, :], ACT.Copy).then_inc(pre["four_tok_stored"], 1)
            act.wait_ge(pre["four_ch"], 1)
            act.activation(CATT[:, 0:2 * L2], PS[:, 7, :], ACT.Copy)
            act.wait_ge(pre["mixed"], 1)
            act.activation(oTW, oTW, ACT.Tanh)
            act.activation(oSG, oSG, ACT.Tanh, scale=0.5)

        def shift_mix(dve, out, zp, s0, mu_half, one_mu):
            n = 2 - s0
            t3 = MIXT[:, 0:n * L2].rearrange("p (s n) -> p s n", n=L2)
            a3 = AVG[:, 0:n * L2].rearrange("p (s n) -> p s n", n=L2)
            dve.tensor_scalar(t3, zp[:, s0:2, 1:L2 + 1], one_mu, None, ALU.mult)
            dve.tensor_tensor(a3, zp[:, s0:2, 0:L2], zp[:, s0:2, 2:L2 + 2], ALU.add)
            dve.drain()
            return dve.scalar_tensor_tensor(out.rearrange("p (s n) -> p s n", n=L2), a3, mu_half, t3, ALU.mult, ALU.add)

        def zero_edges(dve):
            for z in ZP:
                dve.memset(z[:, :, 0:1], 0.0)
                dve.memset(z[:, :, L2 + 1:L2 + 2], 0.0)

        def odd_pre_dve(dve):
            zero_edges(dve)
            mu = prm("lora_mu")
            dve.tensor_scalar(oPD[:, 0:3], mu, 0.5, None, ALU.mult)
            dve.tensor_scalar(oPD[:, 3:6], mu, -1.0, 1.0, ALU.mult, ALU.add)
            dve.wait_ge(pre["stored"], 3)
            dve.drain()
            for x, dst in enumerate((oTW, oZA, oSG)):
                ins = shift_mix(dve, dst, ZP[x], 1 if x == 2 else 0, oPD[:, x:x + 1], oPD[:, 3 + x:4 + x])
                dve.drain()
            dve.drain().then_inc(pre["mixed"], 1)

        def pair_pe(pe, i):
            pe.wait_ge(w_ready[0], i * 48 + ODD_BASE[0] + 48)
            for x, bank in ((1, 1), (2, 2), (0, 0)):
                c0 = L2 if x == 0 else 0
                for k in range(KD):
                    mm = pe.matmul(PS[:, bank, c0:T], slots[:, 0, k, x * P:x * P + P], HT[:, k, c0:T],
                                   start=(k == 0), stop=(k == KD - 1))
                mm.then_inc(rw["proj"], 1)
            pe.wait_ge(rw["small"], i * 32 + 32)
            for x, src, bank in ((0, oTW, 3), (1, oZA, 5)):
                for d in range(2):
                    q = slice(64 * d, 64 * d + 64)
                    mm = pe.matmul(PS[:, bank + d, :], oLW[q, x * P:x * P + P], src[q, :], start=True, stop=True)
                mm.then_inc(rw["lora"], 1)
            pe.wait_ge(rw["sq"], i + 1)
            pe.matmul(PS[:, 7, :], head_ones, E_[:, 0, :], start=True, stop=True).then_inc(rw["kksum"], 1)
            pe.wait_ge(rw["v"], i + 1)
            pe.wait_ge(rw["zp"], 3 * i + 3)
            for c in range(4):
                mm = pe.transpose(PS[:, 0, c * P:c * P + P], oVZ[:, c * P:c * P + P], ident)
            mm.then_inc(rw["vturned"], 1)
            pe.wait_ge(rw["hat"], i + 1)
            for b, src in enumerate((B_, KD_)):
                for d in range(2):
                    for c in range(4):
                        mm = pe.transpose(PS[:, 1 + 2 * b + d, c * P:c * P + P], src[:, d, c * P:c * P + P], ident)
                    mm.then_inc(rw["tok"], 1)
            pe.wait_ge(rw["tok_stored"], 4 * i + 4)
            pe.wait_ge(rw["vstored"], i + 1)
            for d in range(2):
                for h in range(2):
                    q = slice(64 * h, 64 * h + 64)
                    if d == 1:
                        pe.wait_ge(rw["x"], 24 * i + 11 + h)
                    for c in range(4):
                        cc = slice(c * P, c * P + P)
                        for bank, l, r in ((0, B_, PP_), (1, KD_, PP_), (2, PP_, B_)):
                            mm = pe.matmul(PS[:, 4 * h + bank, cc], l[q, d, cc], r[q, d, cc], start=True, stop=True)
                    for c in range(2):
                        for bank, l in ((0, B_), (2, KD_)):
                            mm = pe.matmul(PS[:, 4 * h + 3, (bank + c) * P:(bank + c) * P + P],
                                           l[q, d, L2 + c * P:L2 + c * P + P], PX_[q, d, c * P:c * P + P],
                                           start=True, stop=True)
                    mm.then_inc(rw["gram"], 1)
                for n in range(1, NL):
                    lv = (2 * i + d) * (NL - 1) * 2 + 2 * (n - 1)
                    for h in range(2):
                        if n == 1:
                            pe.wait_ge(rw["gram_read"], 4 * i + 2 * d + h + 1)
                        else:
                            pe.wait_ge(rw["x"], lv - 2 + h + 1)
                        pe.wait_ge(rw["mt"], lv + h + 1)
                        for c in range(4):
                            mm = pe.matmul(PS[:, 4 * h, c * P:c * P + P], MT[h][:, c, :], XX[h][:, c, :],
                                           start=True, stop=True)
                        mm.then_inc(rw["t1"], 1)
                    for h in range(2):
                        pe.wait_ge(rw["t1s"], lv + h + 1)
                        for c in range(4):
                            cc = slice(c * P, c * P + P)
                            mm = pe.matmul(PS[:, 4 * h + 2, cc], T1[h][:, c, :], XT_[:, d, h, c, :], start=True, stop=True)
                            if n < NL - 1:
                                mm = pe.matmul(PS[:, 4 * h + 1, cc], XT_[:, d, h, c, :], T1[h][:, c, :],
                                               start=True, stop=True)
                        mm.then_inc(rw["p"], 1)
            pe.wait_ge(rw["x"], 24 * i + 24)
            for m in range(4):
                step = [(d, RORD[d][m]) for d in range(2)]
                for d, c in step:
                    if m > 0:
                        pe.wait_ge(rw["s"], 6 * i + 2 * (m - 1) + d + 1)
                        pe.matmul(PS[:, d, 0:P], PP_[:, d, c * P:c * P + P], ST_[:, d, :], start=True, stop=False,
                                  skip_group_check=True)
                    for h in range(2):
                        mm = pe.matmul(PS[:, d, 64 * h:64 * h + 64], MK_[:, d, h, c, :], oVT[:, c * P + 64 * h:c * P + 64 * h + 64],
                                       start=(m == 0), stop=True, skip_group_check=True)
                    mm.then_inc(rw["w"], 1)
                for d, c in step:
                    pe.wait_ge(rw["ws"], 8 * i + 2 * m + d + 1)
                    for h in range(2):
                        mm = pe.matmul(PS[:, 2 + d, 64 * h:64 * h + 64], XT_[:, d, h, c, :], WS_[:, d, 64 * h:64 * h + 64],
                                       start=True, stop=True)
                    mm.then_inc(rw["u"], 1)
                for d, c in step:
                    vt = oVT[:, c * P:c * P + P]
                    pe.wait_ge(rw["us"], 8 * i + 2 * m + d + 1)
                    if m >= 2:
                        mm = pe.matmul(PS[:, 4 + c, 0:P], ST_[:, d, :], PX_[:, d, (c - 2) * P:(c - 1) * P],
                                       start=(m == 2), stop=False, skip_group_check=True)
                        for h in range(2):
                            o = PS[64 * h:64 * h + 64, 4 + c, 0:P]
                            pe.matmul(o, US_[:, d, 64 * h:64 * h + 64], NN_[:, d, h, c - 2, :], start=False, stop=False,
                                      skip_group_check=True)
                            mm = pe.matmul(o, vt[:, 64 * h:64 * h + 64], NN_[:, d, h, c, :], start=False, stop=(m == 3),
                                           skip_group_check=True)
                        if m == 3:
                            mm.then_inc(rw["y"], 1)
                    if m < 3:
                        pe.matmul(PS[:, 4 + d, 0:P], BT_[:, d, c * P:c * P + P], US_[:, d, :], start=True, stop=False)
                        pe.matmul(PS[:, 4 + d, 0:P], KT_[:, d, c * P:c * P + P], vt, start=False,
                                  stop=True).then_inc(rw["ds"], 1)
            pe.matmul(PS[:, 0, 0:L2], oLW[:, 256:384], oSG, start=True, stop=True).then_inc(rw["g2"], 1)
            pe.matmul(PS[:, 1, 0:L2], head_ones, oBON, start=True, stop=True).then_inc(rw["bonus"], 1)
            pe.wait_ge(rw["yb"], i + 1)
            pe.matmul(PS[:, 2, 0:L2], head_ones, oPX[:, 0:L2], start=True, stop=True).then_inc(rw["mean"], 1)
            pe.wait_ge(rw["ysq"], i + 1)
            pe.matmul(PS[:, 3, 0:L2], head_ones, oPX[:, L2:2 * L2], start=True, stop=True).then_inc(rw["var"], 1)

        def pair_act(act, i):
            act.wait_ge(rw["proj"], 3 * i + 1)
            for x, bank in ((1, 1), (2, 2), (0, 0)):
                s0 = 1 if x == 0 else 0
                act.wait_ge(rw["proj"], 3 * i + {1: 1, 2: 2, 0: 3}[x])
                act.activation(ZP[x][:, s0:2, 1:L2 + 1], PS[:, bank, s0 * L2:T].rearrange("p (s n) -> p s n", n=L2),
                               ACT.Copy).then_inc(rw["zp"], 1)
            act.wait_ge(rw["derived"], i + 1)
            for x, dst, bank in ((0, G_, 3), (1, B_, 5)):
                act.wait_ge(rw["lora"], 2 * i + x + 1)
                for d in range(2):
                    ins = act.activation(dst[:, d, :], PS[:, bank + d, :], ACT.Tanh, scale=0.5,
                                         bias=oPD[:, 2 * x + d:2 * x + d + 1])
                ins.then_inc(rw["tanh_w"] if x == 0 else rw["tanh_a"], 1)
            act.wait_ge(rw["kksum"], i + 1)
            act.activation(E_[:, 1, :], PS[:, 7, :], ACT.Ln, bias=EPS[:, 1:2])
            act.drain()
            act.activation(E_[:, 1, :], E_[:, 1, :], ACT.Exp, scale=-0.5).then_inc(rw["kkrs"], 1)
            act.wait_ge(rw["vturned"], i + 1)
            act.activation(oVT, PS[:, 0, :], ACT.Copy).then_inc(rw["vstored"], 1)
            act.wait_ge(rw["expo"], i + 1)
            lat = slice(L2, T)
            act.activation(PP_[:, 0, :], G_[:, 0, :], ACT.Exp)
            act.activation(PP_[:, 1, :], E_[:, 1, :], ACT.Exp, scale=-1.0)
            act.activation(PX_[:, 0, 0:L2], E_[:, 0, lat], ACT.Exp)
            act.activation(PX_[:, 1, 0:L2], G_[:, 1, lat], ACT.Exp, scale=-1.0)
            act.activation(C_[:, 0, :], E_[:, 0, :], ACT.Exp, scale=-1.0)
            act.activation(C_[:, 1, :], G_[:, 1, :], ACT.Exp)
            act.activation(oFF, oFF, ACT.Exp).then_inc(rw["exps"], 1)
            for b, dst in enumerate((BT_, KT_)):
                for d in range(2):
                    act.wait_ge(rw["tok"], 4 * i + 2 * b + d + 1)
                    act.activation(dst[:, d, :], PS[:, 1 + 2 * b + d, :], ACT.Copy).then_inc(rw["tok_stored"], 1)
            for d in range(2):
                for h in range(2):
                    act.wait_ge(rw["gram"], 4 * i + 2 * d + h + 1)
                    act.activation(LTS[h], PS[:, 4 * h, :].rearrange("p (c n) -> p c n", c=4),
                                   ACT.Copy).then_inc(rw["lt"], 1)
                for n in range(1, NL):
                    lv = (2 * i + d) * (NL - 1) * 2 + 2 * (n - 1)
                    for h in range(2):
                        act.wait_ge(rw["t1"], lv + h + 1)
                        act.activation(T1[h], PS[:, 4 * h, :].rearrange("p (c n) -> p c n", c=4),
                                       ACT.Copy).then_inc(rw["t1s"], 1)
            for m in range(4):
                for d in range(2):
                    act.wait_ge(rw["w"], 8 * i + 2 * m + d + 1)
                    act.activation(WS_[:, d, :], PS[:, d, 0:P], ACT.Copy).then_inc(rw["ws"], 1)
                for d in range(2):
                    act.wait_ge(rw["u"], 8 * i + 2 * m + d + 1)
                    act.activation(US_[:, d, :], PS[:, 2 + d, 0:P], ACT.Copy, scale=-1.0).then_inc(rw["us"], 1)
            act.wait_ge(rw["var"], i + 1)
            act.activation(oPP[:, 0:L2], PS[:, 3, 0:L2], ACT.Ln, scale=1.0 / 64, bias=EPS[:, 2:3])
            act.drain()
            act.activation(oPP[:, 0:L2], oPP[:, 0:L2], ACT.Exp, scale=-0.5).then_inc(rw["rstd"], 1)

        def pair_pool(pool, i):
            lvl = cst("level").rearrange("p (d l n) -> p d l n", d=2, l=NL)
            for d in range(2):
                for n in range(1, NL):
                    lv = (2 * i + d) * (NL - 1) * 2 + 2 * (n - 1)
                    mask = lvl[:, d, n, :].rearrange("p (o n) -> p o n", o=1).broadcast_to([P, 4, P])
                    for h in range(2):
                        if n == 1:
                            pool.wait_ge(rw["lt"], 4 * i + 2 * d + h + 1)
                        else:
                            pool.wait_ge(rw["t1"], lv - 2 + h + 1)
                        pool.tensor_tensor(MT[h], LTS[h], mask, ALU.mult).then_inc(rw["mt"], 1)

        def pair_dve(dve, i):
            drain = dve.drain
            zero_edges(dve)
            dve.wait_ge(rw["small"], 32 * i + 32)
            dve.tensor_scalar(oPD[:, 0:4], oPV[:, 3:7], 0.5, None, ALU.mult)
            dve.tensor_scalar(oPD[:, 4:7], oPV[:, 0:3], 0.5, None, ALU.mult)
            dve.tensor_scalar(oPD[:, 7:10], oPV[:, 0:3], -1.0, 1.0, ALU.mult, ALU.add)
            dve.tensor_scalar(oPD[:, 10:11], oPV[:, 8:9], -1.0, 1.0, ALU.mult, ALU.add).then_inc(rw["derived"], 1)
            drain()
            dve.wait_ge(rw["zp"], 3 * i + 1)
            shift_mix(dve, oKZ, ZP[1], 0, oPD[:, 5:6], oPD[:, 8:9])
            drain()
            dve.tensor_scalar(oKK, oKZ, oPV[:, 7:8], None, ALU.mult)
            drain()
            dve.tensor_tensor(E_[:, 0, :], oKK, oKK, ALU.mult).then_inc(rw["sq"], 1)
            dve.wait_ge(rw["zp"], 3 * i + 2)
            shift_mix(dve, oVZ, ZP[2], 0, oPD[:, 6:7], oPD[:, 9:10]).then_inc(rw["v"], 1)
            drain()
            dve.wait_ge(rw["zp"], 3 * i + 3)
            shift_mix(dve, oRZ, ZP[0], 1, oPD[:, 4:5], oPD[:, 7:8])
            dve.wait_ge(rw["tanh_w"], i + 1)
            dve.tensor_scalar(oG, oG, 1.0, -0.5 * EXP_M05, ALU.add, ALU.mult)
            drain()
            for d in range(2):
                dve.tensor_tensor_scan(C_[:, d, :], cst("reset128"), G_[:, d, :], 0.0, ALU.mult, ALU.add)
            dve.wait_ge(rw["kkrs"], i + 1)
            dve.tensor_tensor(oKK, oKK, E_[:, 1, :], ALU.mult)
            drain()
            cv = oC.rearrange("p (n s) -> p n s", s=P)
            c4 = oC.rearrange("p (d c s) -> p d c s", d=2, s=P)
            dve.tensor_tensor(oE.rearrange("p (n s) -> p n s", s=P), cv, cv[:, :, 63:64].broadcast_to([P, 8, P]),
                              ALU.subtract)
            dve.tensor_copy(oMID, c4[:, :, :, 63])
            dve.tensor_tensor(oDN, c4[:, :, :, 127], c4[:, :, :, 63], ALU.subtract)
            drain()
            dve.tensor_tensor(oG, oE, oG, ALU.subtract)
            for d in range(2):
                a, b = (oDN, oMID) if d == 0 else (oMID, oDN)
                for c, e in zip(RORD[d], RORD[d][1:]):
                    dve.tensor_tensor(oFF[:, d, c:c + 1], a[:, d, c:c + 1], b[:, d, e:e + 1], ALU.add)
                dve.memset(oFF[:, d, RORD[d][3]:RORD[d][3] + 1], 0.0)
            drain().then_inc(rw["expo"], 1)
            dve.wait_ge(rw["tanh_a"], i + 1)
            dve.tensor_scalar(oB, oB, 0.5, 0.5, ALU.mult, ALU.add)
            drain()
            dve.tensor_scalar(oKD, oB, oPV[:, 8:9], oPD[:, 10:11], ALU.mult, ALU.add)
            drain()
            for d in range(2):
                dve.tensor_tensor(KD_[:, d, :], KD_[:, d, :], oKZ, ALU.mult)
                dve.tensor_tensor(B_[:, d, :], B_[:, d, :], oKK, ALU.mult)
            drain()
            dve.tensor_tensor(oBON, KD_[:, 0, L2:T], KD_[:, 1, L2:T], ALU.add)
            drain()
            dve.scalar_tensor_tensor(oBON, oBON, oPV[:, 9:10], oRZ, ALU.mult, ALU.mult)
            dve.wait_ge(rw["exps"], i + 1)
            dve.tensor_tensor(oB, oB, oC, ALU.mult)
            dve.tensor_tensor(oKD, oKD, oC, ALU.mult)
            for d in range(2):
                dve.tensor_tensor(PP_[:, d, :], PP_[:, d, :], oKK, ALU.mult)
                dve.tensor_tensor(PX_[:, d, 0:L2], PX_[:, d, 0:L2], oRZ, ALU.mult)
            drain().then_inc(rw["hat"], 1)
            lvl = cst("level").rearrange("p (d l n) -> p d l n", d=2, l=NL)

            def four(ap, n=4):
                return ap.rearrange("p (o n) -> p o n", o=1).broadcast_to([P, n, P])

            for d in range(2):
                for h in range(2):
                    dve.wait_ge(rw["gram"], 4 * i + 2 * d + h + 1)
                    bank = [PS[:, 4 * h + b, :].rearrange("p (c n) -> p c n", c=4) for b in range(4)]
                    dve.tensor_tensor(XX[h], bank[2], four(lvl[:, 1 - d, 0, :]), ALU.mult)
                    dve.tensor_tensor(MK_[:, d, h], bank[1], four(cst("strict")[:, d * P:d * P + P]), ALU.mult)
                    dve.tensor_tensor(NN_[:, d, h], bank[3], four(cst("incl")[:, d * P:d * P + P]), ALU.mult)
                    dve.wait_ge(rw["lt"], 4 * i + 2 * d + h + 1)
                    dve.tensor_tensor(XT_[:, d, h], LTS[h], four(lvl[:, d, 0, :]), ALU.mult)
                    drain()
                    dve.tensor_tensor(XX[h], four(ident), XX[h], ALU.subtract)
                    dve.tensor_tensor(XT_[:, d, h], four(ident), XT_[:, d, h], ALU.subtract)
                    drain().then_inc(rw["gram_read"], 1)
                for n in range(1, NL):
                    lv = (2 * i + d) * (NL - 1) * 2 + 2 * (n - 1)
                    for h in range(2):
                        dve.wait_ge(rw["p"], lv + h + 1)
                        if n < NL - 1:
                            dve.tensor_tensor(XX[h], XX[h], PS[:, 4 * h + 1, :].rearrange("p (c n) -> p c n", c=4),
                                              ALU.subtract)
                        dve.tensor_tensor(XT_[:, d, h], XT_[:, d, h],
                                          PS[:, 4 * h + 2, :].rearrange("p (c n) -> p c n", c=4),
                                          ALU.subtract).then_inc(rw["x"], 1)
                    drain()
            for m in range(3):
                for d in range(2):
                    c = RORD[d][m]
                    f = oFF[:, d, c:c + 1]
                    dve.wait_ge(rw["ds"], 6 * i + 2 * m + d + 1)
                    tmp = C_[:, d, 0:P]
                    dst = tmp if m > 0 else ST_[:, d, :]
                    ins = dve.scalar_tensor_tensor(dst, PS[:, 4 + d, 0:P], f, head_ones, ALU.mult, ALU.mult)
                    if m > 0:
                        drain()
                        ins = dve.scalar_tensor_tensor(ST_[:, d, :], ST_[:, d, :], f, tmp, ALU.mult, ALU.add)
                    ins.then_inc(rw["s"], 1)
            y, sq = oPX[:, 0:L2], oPX[:, L2:2 * L2]
            dve.wait_ge(rw["bonus"], i + 1)
            dve.tensor_tensor(oC[:, 0:L2], PS[:, 1, 0:L2], oVZ[:, L2:T], ALU.mult)
            drain()
            dve.wait_ge(rw["y"], 2 * i + 2)
            dve.tensor_tensor(y.rearrange("p (c n) -> p c n", c=2), oC[:, 0:L2].rearrange("p (c n) -> p c n", c=2),
                              PS[:, 6:8, 0:P], ALU.add).then_inc(rw["yb"], 1)
            drain()
            dve.wait_ge(rw["mean"], i + 1)
            dve.scalar_tensor_tensor(y, PS[:, 2, 0:L2], -1.0 / 64, y, ALU.mult, ALU.add)
            drain()
            dve.tensor_tensor(sq, y, y, ALU.mult).then_inc(rw["ysq"], 1)
            dve.wait_ge(rw["rstd"], i + 1)
            dve.tensor_tensor(y, y, oPP[:, 0:L2], ALU.mult)
            drain()
            dve.tensor_scalar(y, y, oPV[:, 10:11], oPV[:, 11:12], ALU.mult, ALU.add)
            drain()
            dve.tensor_tensor(CATT[:, ds(i * L2 + 2 * L2, L2)], y, PS[:, 0, 0:L2], ALU.mult)

        def weights_odd(sp):
            w = odd_w_in[0]
            rk = FOUR + 3 * RW_DIM
            sp.wait_ge(phase, ENGINES * 8)
            weights_cols(sp, 2, 0, w, rk, 384)
            weights_cols(sp, 3, 0, w, 0, FOUR)
            sp.wait_ge(phase, ENGINES * 10)
            for i in range(NPAIR):
                if i > 0:
                    sp.wait_ge(rw["proj"], 3 * i)
                for x in range(3):
                    weights_cols(sp, 0, x * P, w, FOUR + x * RW_DIM + i * P, P)
                if i > 0:
                    sp.wait_ge(odd_part, 3 * i)
                sp.dma_start(oPV, pair_small[i]).then_inc(rw["small"], 16)
                sp.dma_start(oLW, pair_w[i]).then_inc(rw["small"], 16)
            sp.wait_ge(pre["four"], 1)
            for h in range(2):
                weights_cols(sp, 2 + h, 0, odd_w_out[0], 512 * h, 512)
            weights_moe(sp, 1)

        OUT1_READY = [ODD_BASE[2] + 32, ODD_BASE[3] + 32]

        def odd_part_pe(pe):
            norm_pe(pe, 2, ALL)
            meet(pe, 9)
            odd_pre_pe(pe)
            meet(pe, 10)
            with pe.Fori(0, NPAIR) as i:
                pair_pe(pe, i)
                odd_meet(pe, i * 3 + 3)
            meet(pe, 11)
            gate_pe(pe, 2, (0,))
            meet(pe, 12)
            out_pe(pe, 1, LAT, 2, OUT1_READY, CATT.rearrange("p (k n) -> p k n", k=KD))
            meet(pe, 13)
            norm_pe(pe, 3, LAT)
            meet(pe, 14)
            router_pe(pe, 1, LAT)
            meet(pe, 15)
            moe_pe(pe, 1)
            meet(pe, 16)

        def odd_part_act(act):
            norm_act(act, 2, ALL)
            meet(act, 9)
            odd_pre_act(act)
            meet(act, 10)
            with act.Fori(0, NPAIR) as i:
                pair_act(act, i)
                odd_meet(act, i * 3 + 3)
            meet(act, 11)
            gate_act(act, 2, (0,))
            meet(act, 12)
            meet(act, 13)
            norm_act(act, 3, LAT)
            meet(act, 14)
            router_act(act, 1, LAT)
            meet(act, 15)
            moe_act(act, 1)
            meet(act, 16)

        def odd_part_dve(dve):
            norm_dve(dve, 2, ALL)
            meet(dve, 9)
            odd_pre_dve(dve)
            meet(dve, 10)
            dve.tensor_scalar(oSG, oSG, 0.5, 0.5, ALU.mult, ALU.add)
            with dve.Fori(0, NPAIR) as i:
                pair_dve(dve, i)
                odd_meet(dve, i * 3 + 3)
            meet(dve, 11)
            gate_dve(dve, 2, (0,))
            meet(dve, 12)
            out_dve(dve, 1, LAT)
            meet(dve, 13)
            norm_dve(dve, 3, LAT)
            meet(dve, 14)
            router_dve(dve, 1, LAT)
            meet(dve, 15)
            moe_dve(dve, 1)
            moe_end_dve(dve, 1, LAT)
            meet(dve, 16)

        def weights_ada(sp):
            for n in range(DEPTH * N_ADA):
                lay, b = n // N_ADA, n % N_ADA
                if n >= NSLOT:
                    sp.wait_ge(ada_rows, n - NSLOT + 1)
                sp.dma_start(slots[:, b % NSLOT, :, :], ada_w[lay, :, b * 512:b * 512 + 512]
                             .rearrange("(k p) n -> p k n", p=P)).then_inc(w_ready[b % NSLOT], 16)

        def weights_cols(sp, s, at, w, c0, width):
            sp.dma_start(slots[:, s, :, at:at + width],
                         w[:, c0:c0 + width].rearrange("(k p) n -> p k n", p=P)).then_inc(w_ready[s], 16)

        def weights_even(sp):
            w = even_w_in[0]
            for g in range(2):
                if g == 0:
                    sp.wait_ge(ada_rows, 2 * N_ADA - 5)
                else:
                    sp.wait_ge(gla["proj"], 7)
                for at, c0, width in ((0, 128 * g, 128), (128, 256 + 128 * g, 128), (256, 512 + 256 * g, 256)):
                    weights_cols(sp, 0, at, w, c0, width)
                if g == 0:
                    sp.wait_ge(ada_rows, 2 * N_ADA - 4)
                weights_cols(sp, 1, 0, w, 1024 + 256 * g, 256)
                weights_cols(sp, 1, 256, w, 1536, 32)
                if g == 1:
                    sp.wait_ge(gla["logits"], 1)
                    sp.wait_ge(gla["expo"], 1)
                sp.dma_start(GW[:, :], gla_small[g]).then_inc(gla["small"], 16)
                if g == 0:
                    sp.wait_ge(ada_rows, 2 * N_ADA - 3)
                else:
                    sp.wait_ge(att["proj"], NT)
                for at, c0, width in ((0, 1568 + 256 * g, 256), (256, 2080 + 64 * g, 64), (320, 2208 + 64 * g, 64)):
                    weights_cols(sp, 2, at, w, c0, width)
            sp.wait_ge(gla["proj"], 14)
            for h in range(2):
                weights_cols(sp, h, 0, even_w_out[0], 512 * h, 512)

        def weights_moe(sp, n):
            ev = moe_ev
            J, b = jobs_of(sp, n)
            sg, su, sd = MOE_SLOTS

            def load_hg(j):
                sp.dma_start(mHG, hg[ds(j * P, P), :] if not isinstance(j, int) else hg[j * P:j * P + P, :]
                             ).then_inc(ev["hg_loaded"], 16)

            sp.wait_ge(phase, ENGINES * MOE_START[n])
            sp.wait_ge(rt_ev["rows_scattered"], 16 * TOP_K * (4 if n == 0 else 6))
            load_hg(0)
            with sp.Fori(0, J) as j:
                q = b + j
                e = sp.value_load(JOBS[0:1, ds(j + 32 * n, 1)], min_val=0, max_val=N_EXP - 1)
                for s, w, free, ready in ((sg, moe_w_gate, "gate_done", "w_gate"), (su, moe_w_up, "up_done", "w_up")):
                    sp.wait_ge(ev[free], q + 1)
                    sp.dma_start(slots[:, s, :, :], w[n, ds(e, 1), :, :].rearrange("e (k p) n -> p (e k) n", p=P)
                                 ).then_inc(ev[ready], 16)
                sp.wait_ge(ev["x_turned"], q + n + 1)
                load_hg(j + 1)
                sp.wait_ge(ev["down_done"], q * 2 + 2)
                sp.dma_start(slots[:, sd, :, :].rearrange("p (f h) n -> p f (h n)", h=2),
                             moe_w_down[n, ds(e, 1), :, :].rearrange("e (f p) n -> p (e f) n", p=P)
                             ).then_inc(ev["w_down"], 16)

        MOE_START = (7, 15)
        LAST_PHASE = 16
        block = stack.enter_context(nc.Block())
        ALL, LAT = list(range(NT)), [2, 3]

        def even_meet(eng, value):
            eng.drain().then_inc(even_part, 1)
            eng.wait_ge(even_part, value)

        @block.sync
        def _(sp):
            sp.dma_start(X[:, 0:2, :], ctx_in[0].rearrange("(t p) n -> p t n", p=P)).then_inc(in_ready, 16)
            sp.dma_start(X[:, 2:4, :], x[0].rearrange("(t p) n -> p t n", p=P)).then_inc(in_ready, 16)
            sp.dma_start(CST[:, :], consts).then_inc(in_ready, 16)
            sp.dma_start(PRM[:, :], params).then_inc(in_ready, 16)
            sp.dma_start(ROW[:, :], rows.partition_broadcast(P)).then_inc(in_ready, 16)
            weights_ada(sp)
            weights_even(sp)
            weights_moe(sp, 0)
            weights_odd(sp)
            sp.wait_ge(phase, 3 * LAST_PHASE)
            sp.dma_start(out[0].rearrange("(t p) n -> p t n", p=P), X[:, 2:4, :]).then_inc(out_stored, 16)
            sp.wait_ge(out_stored, 16)

        @block.tensor
        def _(pe):
            pe.wait_ge(in_ready, 80)
            ada_pe(pe)
            meet(pe, 1)
            norm_pe(pe, 0, ALL)
            meet(pe, 2)
            with pe.Fori(0, 2) as i:
                gla_pe(pe, i, EVEN_BASE)
                even_meet(pe, i * 6 + 3)
                att_pe(pe, i, EVEN_BASE)
                even_meet(pe, i * 6 + 6)
            meet(pe, 3)
            gate_pe(pe, 0, (0, 1))
            meet(pe, 4)
            turn_pe(pe)
            turned_meet(pe)
            out_pe(pe, 0, ALL, 0, OUT0_READY, HT)
            meet(pe, 5)
            norm_pe(pe, 1, ALL)
            meet(pe, 6)
            router_pe(pe, 0, ALL)
            meet(pe, 7)
            moe_pe(pe, 0)
            meet(pe, 8)
            odd_part_pe(pe)

        @block.scalar
        def _(act):
            act.wait_ge(zeros_ready, 1)
            for j in range(MAX_JOBS + 1):
                act.dma_start(hg[j * P:j * P + P, :], XN[:, 0, :]).then_inc(hg_zeroed, 16)
            act.wait_ge(in_ready, 80)
            cond = prm("cond").rearrange("p (k v) -> p k v", v=2)
            act.activation(COND[:], cond, ACT.Tanh, scale=0.5).then_inc(cond_th, 1)
            ada_act(act)
            meet(act, 1)
            act.wait_ge(hg_zeroed, 16 * (MAX_JOBS + 1))
            norm_act(act, 0, ALL)
            meet(act, 2)
            with act.Fori(0, 2) as i:
                gla_act(act, i)
                even_meet(act, i * 6 + 3)
                att_act(act, i)
                even_meet(act, i * 6 + 6)
            meet(act, 3)
            gate_act(act, 0, (0, 1))
            meet(act, 4)
            turn_copy(act, range(0, KD, 2))
            turned_meet(act)
            meet(act, 5)
            norm_act(act, 1, ALL)
            meet(act, 6)
            router_act(act, 0, ALL)
            meet(act, 7)
            moe_act(act, 0)
            meet(act, 8)
            odd_part_act(act)

        @block.gpsimd
        def _(pool):
            pool.memset(XN[:], 0.0)
            pool.drain().then_inc(zeros_ready, 1)
            pool.wait_ge(in_ready, 80)
            pool.wait_ge(phase, ENGINES * 6)
            rows_pool(pool, 0, ALL)
            back_pool(pool, 0, ALL)
            with pool.Fori(0, NPAIR) as i:
                pair_pool(pool, i)
            pool.wait_ge(phase, ENGINES * 14)
            rows_pool(pool, 1, LAT)
            back_pool(pool, 1, LAT)

        @block.vector
        def _(dve):
            for c, value in enumerate((NORM_EPS, L2_EPS, GN_EPS, 0.0)):
                dve.memset(EPS[:, c:c + 1], value)
            dve.wait_ge(in_ready, 80)
            dve.wait_ge(cond_th, 1)
            cond = prm("cond").rearrange("p (k v) -> p k v", v=2)
            dve.scalar_tensor_tensor(COND[:], COND[:], 1.0, cond, ALU.add, ALU.mult)
            dve.drain()
            dve.tensor_scalar(COND[:], COND[:], 0.5, None, ALU.mult).then_inc(cond_ready, 1)
            ada_dve(dve)
            meet(dve, 1)
            dve.wait_ge(hg_zeroed, 16 * (MAX_JOBS + 1))
            norm_dve(dve, 0, ALL)
            meet(dve, 2)
            with dve.Fori(0, 2) as i:
                gla_dve(dve, i)
                even_meet(dve, i * 6 + 3)
                att_dve(dve, i)
                even_meet(dve, i * 6 + 6)
            meet(dve, 3)
            gate_dve(dve, 0, (0, 1))
            meet(dve, 4)
            turn_copy(dve, range(1, KD, 2))
            turned_meet(dve)
            out_dve(dve, 0, ALL)
            meet(dve, 5)
            norm_dve(dve, 1, ALL)
            meet(dve, 6)
            router_dve(dve, 0, ALL)
            meet(dve, 7)
            moe_dve(dve, 0)
            moe_end_dve(dve, 0, ALL)
            meet(dve, 8)
            odd_part_dve(dve)


def kernel(**inputs):
    import concourse.bacc as _bacc
    from concourse import mybir as _mybir
    from concourse.bass_utils import run_bass_kernel_spmd as _run

    a = {k: np.ascontiguousarray(v) for k, v in inputs.items()}

    def cols(v):
        return v.reshape(*v.shape[:-1], -1, P)

    norm = np.stack([a["norm_mix"][0], a["norm_ffn"][0], a["norm_mix"][1], a["norm_ffn"][1]])
    mu = a["rwkv_mu"][0]
    params = np.concatenate([
        cols(norm).reshape(-1, P).T,
        np.stack([a["c"][0].reshape(KD, P), a["c_ctx"].reshape(KD, P)], 1).reshape(-1, P).T,
        cols(a["ada_b"]).reshape(-1, P).T,
        mu[3 * RW_DIM:].reshape(3, P).T,
        a["router_w"].reshape(KD, P, 16).transpose(1, 0, 2).reshape(P, -1)], 1)
    rows = np.concatenate([a["router_b"], a["att_sink"][0], np.tile(a["att_q_norm"][0], GRP), a["att_k_norm"][0],
                           a["gla_out_norm"][0]])
    gla_small = np.zeros((2, P, 260), np.float32)
    for g in range(2):
        gla_small[g, 0:16, 0:256] = a["gla_dec_w"][0][:, :, g * P:g * P + P].transpose(1, 0, 2).reshape(16, 256)
        gla_small[g, :, 256:258] = a["gla_dec_b"][0][:, g * P:g * P + P].T
    vecs = [mu[0:RW_DIM], mu[RW_DIM:2 * RW_DIM], mu[2 * RW_DIM:3 * RW_DIM], a["rwkv_w0"][0][0], a["rwkv_w0"][0][1],
            a["rwkv_a0"][0][0], a["rwkv_a0"][0][1], a["rwkv_kk_scale"][0], a["rwkv_k_a"][0],
            a["rwkv_r_k"][0].reshape(-1), a["rwkv_ln_g"][0], a["rwkv_ln_b"][0]]
    pair_small = np.stack([v.reshape(NPAIR, P) for v in vecs], 2)
    pair_w = np.stack([a["rwkv_w2"][0].reshape(P, NPAIR, P), a["rwkv_a2"][0].reshape(P, NPAIR, P),
                       a["rwkv_g2"][0].reshape(P, NPAIR, P)], 0).transpose(2, 1, 0, 3).reshape(NPAIR, P, 3 * P)
    laid = {"x": a["x"], "ctx": a["ctx"]}
    for k in ("ada_w", "even_w_in", "even_w_out", "odd_w_in", "odd_w_out", "moe_w_gate", "moe_w_up", "moe_w_down"):
        laid[k] = a[k]
    laid.update(consts=shape_constants(), params=params, rows=rows, gla_small=gla_small, pair_small=pair_small,
                pair_w=pair_w)

    nc = _bacc.Bacc("TRN2", target_bir_lowering=False, num_devices=1)
    arrays, args = {}, []
    for name, v in laid.items():
        v = np.ascontiguousarray(v)
        arrays[f"in_{name}_dram"] = v
        args.append(nc.dram_tensor(f"in_{name}_dram", v.shape, _mybir.dt.from_np(v.dtype), kind="ExternalInput").ap())
    args.append(nc.dram_tensor("out_0_dram", (1, SEG, D), F32, kind="ExternalOutput").ap())
    build(nc, *args)
    r = _run(nc, [arrays], core_ids=[0])
    return r.results[0]["out_0_dram"]
```

```python
from contextlib import ExitStack

import numpy as np

import concourse.bass as bass
from concourse import mybir

P = 128
D = 1024
KD = D // P
T = 512
NT = T // P
SEG = 256
DEPTH = 2
NSLOT = 6

GLA_DK, GLA_DV, GLA_TAU = 32, 64, 16.0
GLA_C = 32
NCH = T // GLA_C
ATT_H, ATT_KV, HD = 8, 2, 64
GRP = ATT_H // ATT_KV
RW_DIM, NPAIR = 768, 6
FOUR = 256
N_EXP, TOP_K = 16, 2
MAX_JOBS = 24
NORM_EPS = 1e-6
L2_EPS = 1e-12
GN_EPS = 64e-5
BIG = 1e30
LEVELS = (1, 2, 4, 8, 16, 32, 64)
EXP_M05 = float(np.exp(-0.5))

F32, I32, U32 = mybir.dt.float32, mybir.dt.int32, mybir.dt.uint32
ALU = mybir.AluOpType
ACT = mybir.ActivationFunctionType
AX = mybir.AxisListType
ds = bass.ds

CONST_COLS = [("ident", P), ("ones", P), ("head_ones", P), ("att_mask", 2 * P), ("level", 14 * P),
              ("strict", 2 * P), ("incl", 2 * P), ("gla_incl", 2 * P), ("chunk", 4),
              ("reset32", T), ("reset128", T), ("dft_tok", 2 * T), ("dft_ch", 2 * P),
              ("rope", 2 * 2 * 32), ("first4", 4), ("first16", 16), ("job_index", MAX_JOBS)]
PARAM_COLS = [("norm", 4 * KD), ("cond", 2 * KD), ("ada_b", 96), ("lora_mu", 3), ("router", KD * 16),
              ("pair", NPAIR * 12)]
ROW_COLS = [("router_b", 16), ("sink", 8), ("qk_gain", 5 * HD), ("gla_gain", GLA_DV)]


def columns(table):
    at, n = {}, 0
    for name, width in table:
        at[name] = (n, n + width)
        n += width
    return at, n


def shape_constants():
    at, n = columns(CONST_COLS)
    c = np.zeros((P, n), np.float32)

    def put(name, a):
        c[:, at[name][0]:at[name][1]] = a.reshape(P, -1)

    a, b = np.arange(P)[:, None], np.arange(P)[None, :]
    put("ident", (a == b).astype(np.float32))
    put("ones", np.ones((P, P), np.float32))
    put("head_ones", (a // 64 == b // 64).astype(np.float32))
    put("att_mask", np.stack([np.where(b <= a, 0.0, -BIG), np.where(b >= a, 0.0, -BIG)], 1).astype(np.float32))
    low = [((a // (2 * m) == b // (2 * m)) & (a // m % 2 == 1) & (b // m % 2 == 0)).astype(np.float32) for m in LEVELS]
    put("level", np.stack([m.T for m in low] + low, 1))
    put("strict", np.stack([a < b, a > b], 1).astype(np.float32))
    put("incl", np.stack([a <= b, a >= b], 1).astype(np.float32))
    same = a // GLA_C == b // GLA_C
    put("gla_incl", np.stack([same & (a <= b), same & (a >= b)], 1).astype(np.float32))
    put("chunk", (a // GLA_C == np.arange(4)[None, :]).astype(np.float32))
    t = np.arange(T)[None, :]
    put("reset32", np.broadcast_to(t % GLA_C != 0, (P, T)).astype(np.float32))
    put("reset128", np.broadcast_to(t % P != 0, (P, T)).astype(np.float32))
    ang = 2 * np.pi * (np.outer(np.arange(SEG), np.arange(SEG)) % SEG) / SEG
    tok = np.concatenate([np.cos(ang), np.sin(ang)], 1) / np.sqrt(SEG)
    put("dft_tok", tok.reshape(2, P, T).transpose(1, 0, 2).astype(np.float32))
    ch = 2 * np.pi * (np.outer(np.arange(64), np.arange(64)) % 64) / 64
    both = np.zeros((P, 2, P))
    for h in range(2):
        s = slice(64 * h, 64 * h + 64)
        both[s, 0, s], both[s, 1, s] = np.cos(ch) / 8, -np.sin(ch) / 8
    put("dft_ch", both.astype(np.float32))
    n_freq = HD // 4
    inv = (np.float32(10000.0) ** (-np.arange(n_freq, dtype=np.float32) / np.float32(n_freq))).astype(np.float32)
    pos = np.arange(SEG)
    rot = np.concatenate([(pos // 64).astype(np.float32)[:, None] * inv,
                          (pos % 64).astype(np.float32)[:, None] * inv], -1)
    rope = np.stack([np.cos(rot), np.sin(rot)], 0).astype(np.float32)
    put("rope", rope.reshape(2, 2, P, 32).transpose(2, 0, 1, 3))
    put("first4", np.broadcast_to(np.arange(4, 0, -1, dtype=np.float32), (P, 4)))
    put("first16", np.broadcast_to(np.arange(16, 0, -1, dtype=np.float32), (P, 16)))
    put("job_index", np.broadcast_to(np.arange(MAX_JOBS, dtype=np.float32), (P, MAX_JOBS)))
    return c


def build(nc, x, ctx_in, ada_w, even_w_in, even_w_out, odd_w_in, odd_w_out, moe_w_gate, moe_w_up, moe_w_down,
          consts, params, rows, gla_small, pair_w, out):
    CA, CN = columns(CONST_COLS)
    PA, PN = columns(PARAM_COLS)
    RA, RN = columns(ROW_COLS)

    with ExitStack() as stack:
        def sb(name, shape):
            return stack.enter_context(nc.sbuf_tensor(name, shape, F32))

        def sem(name):
            return stack.enter_context(nc.semaphore(name))

        PS = stack.enter_context(nc.psum_tensor("PS", [P, 8, 512], F32))
        slots = sb("slots", [P, NSLOT, KD, 512])
        X = sb("X", [P, NT, D])
        HT = sb("HT", [P, KD, T])
        XN = sb("XN", [P, NT, D])
        SCR = sb("SCR", [P, 8192])
        CST = sb("CST", [P, CN])
        PRM = sb("PRM", [P, PN])
        ROW = sb("ROW", [P, RN])
        COND = sb("COND", [P, KD, 2])
        MODC = sb("MODC", [P, DEPTH * 96])
        GAIN = sb("GAIN", [P, 4, KD, 2])
        SS = sb("SS", [P, 64])
        RS = sb("RS", [P, 64])
        EPS = sb("EPS", [P, 4])

        def cst(name):
            return CST[:, CA[name][0]:CA[name][1]]

        def prm(name):
            return PRM[:, PA[name][0]:PA[name][1]]

        def row(name):
            return ROW[:, RA[name][0]:RA[name][1]]

        ident, ones, head_ones = cst("ident"), cst("ones"), cst("head_ones")
        mod = MODC[:].rearrange("p (l m v) -> p l m v", l=DEPTH, v=2)

        def split(buf, sizes):
            pieces, n = [], 0
            for s in sizes:
                pieces.append(buf[:, n:n + s])
                n += s
            assert n <= buf.shape[1], (n, buf.shape)
            return pieces

        w_ready = [sem(f"w_ready{s}") for s in range(NSLOT)]
        prm_ready, cst_ready, in_ready = sem("prm_ready"), sem("cst_ready"), sem("in_ready")
        phase = sem("phase")
        out_stored = sem("out_stored")

        ENGINES = 3

        def meet(eng, n):
            eng.drain().then_inc(phase, 1)
            eng.wait_ge(phase, ENGINES * n)

        ada_rows, ada_copied = sem("ada_rows"), sem("ada_copied")
        ada_turned, ada_stored = sem("ada_turned"), sem("ada_stored")
        cond_th, cond_ready = sem("cond_th"), sem("cond_ready")
        norm_ev = {k: sem(k) for k in ("rstd_ready", "xn_ready", "xt_turned")}
        gate_ev = {k: sem(k) for k in ("gate_diag", "gate_spread", "gate_copied")}
        cat_turned = sem("cat_turned")
        proj_ev = {k: sem(k) for k in ("out_done", "out_added", "out_in_x")}
        rt_ev = {k: sem(k) for k in ("logits_done", "logits_exp", "rows_turned", "rows_copied", "mask_ready",
                                     "ranks_done", "jobs_ready", "rows_ready", "rows_scattered")}
        rows_back = [sem("rows_back_context"), sem("rows_back_latents")]
        end_ev = {k: sem(k) for k in ("first_scaled", "rows_gated", "x_added")}
        END_BEFORE = (0, NT)
        moe_ev = {k: sem(k) for k in (
            "w_gate", "w_up", "w_down", "hg_loaded", "x_turned", "x_copied", "gate_done", "tanh", "up_done", "hidden",
            "hid_turned", "hid_copied", "down_done", "o_copied", "o_stored")}
        zeros_ready, hg_zeroed = sem("zeros_ready"), sem("hg_zeroed")
        XN_BEFORE = (0, 4, 8, 12)
        OUT_BEFORE = (0, 8)

        ADA_ROW = SCR[:, 0:1024].rearrange("p (b n) -> p b n", b=2)
        N_ADA = 12

        def ada_pe(pe):
            pe.wait_ge(cond_ready, 1)
            for i in range(DEPTH):
                for b in range(N_ADA + 1):
                    if b < N_ADA:
                        pe.wait_ge(w_ready[b % NSLOT], i * 32 + 16 * (b // NSLOT + 1))
                        if i * N_ADA + b >= 2:
                            pe.wait_ge(ada_copied, i * N_ADA + b - 1)
                        for k in range(KD):
                            mm = pe.matmul(PS[0:2, b % 2, :], COND[:, k, :], slots[:, b % NSLOT, k, :],
                                           start=(k == 0), stop=(k == KD - 1))
                        mm.then_inc(ada_rows, 1)
                    if b >= 1:
                        if i == 0 and b == 1:
                            pe.wait_ge(cst_ready, 16)
                        pe.wait_ge(ada_copied, i * N_ADA + b)
                        if i * N_ADA + b >= 3:
                            pe.wait_ge(ada_stored, i * N_ADA + b - 2)
                        for q in range(4):
                            mm = pe.matmul(PS[:, 2 + b % 2, 2 * q:2 * q + 2], ADA_ROW[0:2, (b - 1) % 2, q * P:q * P + P],
                                           ident[0:2, 0:2], start=True, stop=True)
                        mm.then_inc(ada_turned, 1)

        NORM0_AT = DEPTH * N_ADA - 3

        def square_act(act, t):
            act.activation(XN[:, t, :], X[:, t, :], ACT.Square, accum_out=SS[:, t:t + 1])

        def rstd_act(act, n, tiles):
            act.drain()
            a, b = tiles[0], tiles[-1] + 1
            act.activation(RS[:, a:b], SS[:, a:b], ACT.Ln, scale=1.0 / D, bias=EPS[:, 0:1])
            act.drain()
            act.activation(RS[:, a:b], RS[:, a:b], ACT.Exp, scale=-0.5).then_inc(norm_ev["rstd_ready"], 1)

        def xn_dve(dve, n, tiles):
            dve.wait_ge(norm_ev["rstd_ready"], n + 1)
            for t in tiles:
                dve.tensor_scalar(XN[:, t, :], X[:, t, :], RS[:, t:t + 1], None,
                                  ALU.mult).then_inc(norm_ev["xn_ready"], 1)

        def ada_act(act):
            for i in range(DEPTH):
                for b in range(N_ADA):
                    act.wait_ge(ada_rows, i * N_ADA + b + 1)
                    if i * N_ADA + b >= 2:
                        act.wait_ge(ada_turned, i * N_ADA + b - 1)
                    act.activation(ADA_ROW[0:2, b % 2, :], PS[0:2, b % 2, :], ACT.Copy).then_inc(ada_copied, 1)
                    if i * N_ADA + b == NORM0_AT:
                        act.wait_ge(in_ready, 48)
                        for t in range(NT):
                            square_act(act, t)
                        rstd_act(act, 0, list(range(NT)))

        def ada_dve(dve):
            bias = prm("ada_b")
            for i in range(DEPTH):
                for b in range(N_ADA):
                    dve.wait_ge(ada_turned, i * N_ADA + b + 1)
                    dve.tensor_tensor(MODC[:, i * 96 + b * 8:i * 96 + b * 8 + 8].rearrange("p (m v) -> p m v", v=2),
                                      PS[:, 2 + (b + 1) % 2, 0:8].rearrange("p (m v) -> p m v", v=2),
                                      bias[:, i * 48 + b * 4:i * 48 + b * 4 + 4].rearrange("p (m o) -> p m o", o=1)
                                      .broadcast_to([P, 4, 2]), ALU.add).then_inc(ada_stored, 1)
                    if i * N_ADA + b == NORM0_AT:
                        dve.wait_ge(in_ready, 48)
                        xn_dve(dve, 0, list(range(NT)))
            dve.drain()
            for n in range(4):
                lay, which = n // 2, n % 2
                g = prm("norm")[:, n * KD:(n + 1) * KD].rearrange("p (k o) -> p k o", o=1)
                m = KD * (3 * which + 1)
                dve.scalar_tensor_tensor(GAIN[:, n, :, :], mod[:, lay, m:m + KD, :], 1.0,
                                         g.broadcast_to([P, KD, 2]), ALU.add, ALU.mult)

        def sides_of(tiles):
            return ((1, 0), (0, SEG)) if 0 in tiles else ((0, SEG),)

        def norm_act(act, n, tiles):
            ev = norm_ev
            if n > 0:
                rstd_act(act, n, tiles)
            lay, m = n // 2, KD * 3 * (n % 2)
            for k in range(0, KD, 2):
                act.wait_ge(ev["xt_turned"], KD * n + k + 1)
                for v, c0 in sides_of(tiles):
                    act.activation(HT[:, k, c0:c0 + SEG], PS[:, k, c0:c0 + SEG], ACT.Identity,
                                   bias=mod[:, lay, m + k, v:v + 1], scale=GAIN[:, n, k, v:v + 1])

        def norm_dve(dve, n, tiles):
            ev = norm_ev
            if n > 0:
                xn_dve(dve, n, tiles)
            lay, m = n // 2, KD * 3 * (n % 2)
            for k in range(1, KD, 2):
                dve.wait_ge(ev["xt_turned"], KD * n + k + 1)
                for v, c0 in sides_of(tiles):
                    dve.tensor_scalar(HT[:, k, c0:c0 + SEG], PS[:, k, c0:c0 + SEG], GAIN[:, n, k, v:v + 1],
                                      mod[:, lay, m + k, v:v + 1], ALU.mult, ALU.add)

        def norm_pe(pe, n, tiles):
            ev = norm_ev
            pe.wait_ge(ev["xn_ready"], XN_BEFORE[n] + len(tiles))
            for k in range(KD):
                for t in tiles:
                    mm = pe.transpose(PS[:, k, t * P:t * P + P], XN[:, t, k * P:k * P + P], ident)
                mm.then_inc(ev["xt_turned"], 1)

        GATE = SCR[:, 0:2 * D].rearrange("p (v n) -> p v n", v=2)
        DIAG = SCR[:, 2 * D:4 * D].rearrange("p (v n) -> p v n", v=2)

        def gate_dve(dve, n, sides):
            lay, part = n // 2, 2 + 3 * (n % 2)
            for v in sides:
                for k in range(KD):
                    ins = dve.tensor_scalar(DIAG[:, v, k * P:k * P + P], ident,
                                            mod[:, lay, part * KD + k, v:v + 1], None, ALU.mult)
            ins.then_inc(gate_ev["gate_diag"], 1)

        def gate_pe(pe, n, sides):
            pe.wait_ge(gate_ev["gate_diag"], n + 1)
            for v in sides:
                for h in range(2):
                    mm = pe.matmul(PS[:, 2 * v + h, :], ones, DIAG[:, v, h * 512:h * 512 + 512], start=True, stop=True)
            mm.then_inc(gate_ev["gate_spread"], 1)

        def gate_act(act, n, sides):
            act.wait_ge(gate_ev["gate_spread"], n + 1)
            for v in sides:
                ins = act.activation(GATE[:, v, :].rearrange("p (h n) -> p h n", h=2), PS[:, 2 * v:2 * v + 2, :], ACT.Copy)
            ins.then_inc(gate_ev["gate_copied"], 1)

        def out_pe(pe, n, tiles, out_slots, ready, cat):
            ev = proj_ev
            for j, (t, h) in enumerate((t, h) for t in tiles for h in range(2)):
                if j < 2:
                    pe.wait_ge(w_ready[out_slots[j]], ready[j])
                if j >= 4:
                    pe.wait_ge(ev["out_added"], OUT_BEFORE[n] + j - 3)
                for k in range(KD):
                    a = (t - tiles[0]) * P
                    mm = pe.matmul(PS[:, 4 + j % 4, :], cat[:, k, a:a + P], slots[:, out_slots[h], k, :],
                                   start=(k == 0), stop=(k == KD - 1))
                mm.then_inc(ev["out_done"], 1)

        def out_dve(dve, n, tiles):
            ev = proj_ev
            dve.wait_ge(gate_ev["gate_copied"], 2 * n + 1)
            TMP = SCR[:, 4096:8192].rearrange("p (b n) -> p b n", b=8)
            for j, (t, h) in enumerate((t, h) for t in tiles for h in range(2)):
                v = 1 if t < 2 else 0
                cols = slice(h * 512, h * 512 + 512)
                dve.wait_ge(ev["out_done"], OUT_BEFORE[n] + j + 1)
                dve.tensor_tensor(TMP[:, j, :], PS[:, 4 + j % 4, :], GATE[:, v, cols],
                                  ALU.mult).then_inc(ev["out_added"], 1)
                dve.wait_ge(ev["out_added"], OUT_BEFORE[n] + j + 1)
                dve.tensor_tensor(X[:, t, cols], X[:, t, cols], TMP[:, j, :], ALU.add).then_inc(ev["out_in_x"], 1)

        def out_act(act, n, tiles):
            for i, t in enumerate(tiles):
                act.wait_ge(proj_ev["out_in_x"], OUT_BEFORE[n] + 2 * i + 2)
                square_act(act, t)

        RSC = slots[:, 5, :, :].rearrange("p k n -> p (k n)")
        mTH, mTG, mHID, mHIDT, mOB, mHGT, mHG = split(SCR[:, 2 * D:], [512, 512, 512, 512, D, D, D])
        HIDT = mHIDT.rearrange("p (f n) -> p f n", f=4)
        HGT = mHGT.rearrange("p (k n) -> p k n", k=KD)
        BACK = slots[:, 0:2, :, :].rearrange("p s k n -> p s (k n)").rearrange("p s (t n) -> p s t n", t=NT)
        MASK = sb("MASK", [P, NT, N_EXP])
        ROWI = stack.enter_context(nc.sbuf_tensor("ROWI", [P, TOP_K * NT], U32))
        JOBS = stack.enter_context(nc.sbuf_tensor("JOBS", [P, DEPTH * 32], I32))
        GSEL = sb("GSEL", [P, TOP_K * NT])
        ZCOLS = 128
        ZEROS = SCR[:, 8192 - ZCOLS:8192]
        hg = nc.dram_tensor("hg", (P * (MAX_JOBS + 1), D), F32, kind="Internal").ap()

        def router_pe(pe, n, tiles):
            for t in tiles:
                for k in range(KD):
                    mm = pe.matmul(PS[:, 7, t * 16:t * 16 + 16], HT[:, k, t * P:t * P + P],
                                   prm("router")[:, k * 16:k * 16 + 16], start=(k == 0), stop=(k == KD - 1))
            mm.then_inc(rt_ev["logits_done"], 1)
            for j, (t, h) in enumerate((t, h) for t in tiles for h in range(2)):
                if j >= 4:
                    pe.wait_ge(rt_ev["rows_copied"], OUT_BEFORE[n] + j - 3)
                for q in range(4):
                    k = 4 * h + q
                    mm = pe.transpose(PS[:, j % 4, q * P:q * P + P], HT[:, k, t * P:t * P + P], ident)
                mm.then_inc(rt_ev["rows_turned"], 1)
            pe.wait_ge(rt_ev["mask_ready"], n + 1)
            for t in tiles:
                for s in range(tiles[0], t):
                    pe.matmul(PS[:, 6, t * 16:t * 16 + 16], ones, MASK[:, s, :], start=(s == tiles[0]), stop=False)
                pe.matmul(PS[:, 6, t * 16:t * 16 + 16], cst("strict")[:, 0:P], MASK[:, t, :],
                          start=(t == tiles[0]), stop=True)
            for t in tiles:
                mm = pe.matmul(PS[:, 6, 64:80], ones, MASK[:, t, :], start=(t == tiles[0]), stop=(t == tiles[-1]))
            mm.then_inc(rt_ev["ranks_done"], 1)
            pe.wait_ge(rt_ev["rows_copied"], OUT_BEFORE[n] + 2 * len(tiles))
            gate_pe(pe, 2 * n + 1, (0, 1) if n == 0 else (0,))

        def router_act(act, n, tiles):
            a, b = tiles[0] * 16, tiles[-1] * 16 + 16
            act.wait_ge(rt_ev["logits_done"], n + 1)
            act.activation(RSC[:, a:b], PS[:, 7, a:b], ACT.Exp, scale=-1.0).then_inc(rt_ev["logits_exp"], 1)
            for j, (t, h) in enumerate((t, h) for t in tiles for h in range(2)):
                act.wait_ge(rt_ev["rows_turned"], OUT_BEFORE[n] + j + 1)
                act.activation(XN[:, t, h * 512:h * 512 + 512], PS[:, j % 4, :],
                               ACT.Copy).then_inc(rt_ev["rows_copied"], 1)
            gate_act(act, 2 * n + 1, (0, 1) if n == 0 else (0,))

        def router_dve(dve, n, tiles):
            drain = dve.drain
            nt = len(tiles)
            ng = nt * 4
            a = tiles[0] * 16
            LG, sc, sel, ms, eq, key, o1, o2, rk = [x[:, a:a + nt * 16] for x in split(RSC, [64] * 9)]
            w = RSC[:, 576:2304]
            pr = w[:, 0:ng * 6].rearrange("p (g c) -> p g c", c=6)
            gs, geq, bg, m1, m2, m3, cnt, jobs, ends, base = [
                x[:, 0:z] for x, z in zip(split(w[:, 96:], [16] * 10), (ng, ng, ng, nt, nt, nt, 16, 16, 16, 16))]
            ej = w[:, 288:288 + MAX_JOBS * 16].rearrange("p (j e) -> p j e", e=16)
            ejs = w[:, 700:700 + 32]
            rowf = w[:, 740:740 + TOP_K * NT]

            def v3(ap, c):
                return ap.rearrange("p (t c) -> p t c", c=c)

            def wide(ap, m, c):
                return ap.rearrange("p (t o) -> p t o", o=1).broadcast_to([P, m, c])

            def narrow(ap, m, c):
                return ap.rearrange("p (o c) -> p o c", o=1).broadcast_to([P, m, c])

            dve.wait_ge(rt_ev["logits_exp"], n + 1)
            dve.tensor_scalar(sc, LG, 1.0, None, ALU.add)
            drain()
            dve.reciprocal(sc, sc)
            drain()
            dve.tensor_tensor(v3(sel, 16), v3(sc, 16), narrow(row("router_b"), nt, 16), ALU.add)
            drain()
            s4 = v3(sel, 4)
            dve.tensor_tensor(pr[:, :, 0:3], s4[:, :, 1:4], s4[:, :, 0:1].broadcast_to([P, ng, 3]), ALU.add)
            dve.tensor_tensor(pr[:, :, 3:5], s4[:, :, 2:4], s4[:, :, 1:2].broadcast_to([P, ng, 2]), ALU.add)
            dve.tensor_tensor(pr[:, :, 5:6], s4[:, :, 3:4], s4[:, :, 2:3], ALU.add)
            drain()
            dve.tensor_reduce(gs, pr, AX.X, ALU.max)
            drain()

            def one_hot(out, scores, c, weights, m):
                dve.tensor_reduce(m, v3(scores, c), AX.X, ALU.max)
                drain()
                e = geq if c == 4 else eq
                dve.tensor_tensor(v3(e, c), v3(scores, c), wide(m, nt, c), ALU.is_equal)
                drain()
                dve.tensor_tensor(v3(e, c), v3(e, c), narrow(weights, nt, c), ALU.mult)
                drain()
                dve.tensor_reduce(m2, v3(e, c), AX.X, ALU.max)
                drain()
                dve.tensor_tensor(v3(out, c), v3(e, c), wide(m2, nt, c), ALU.is_equal)
                drain()

            one_hot(bg, gs, 4, cst("first4"), m1)
            dve.tensor_tensor(v3(ms, 4), s4, wide(bg, ng, 4), ALU.mult)
            dve.tensor_scalar(geq, bg, -1.0, BIG, ALU.add, ALU.mult)
            drain()
            dve.tensor_tensor(v3(ms, 4), v3(ms, 4), wide(geq, ng, 4), ALU.add)
            drain()
            one_hot(o1, ms, 16, cst("first16"), m1)
            dve.tensor_scalar(key, o1, -2 * BIG, None, ALU.mult)
            drain()
            dve.tensor_tensor(ms, ms, key, ALU.add)
            drain()
            one_hot(o2, ms, 16, cst("first16"), m1)
            dve.tensor_tensor(MASK[:, tiles[0]:tiles[0] + nt, :], v3(o1, 16), v3(o2, 16),
                              ALU.add).then_inc(rt_ev["mask_ready"], 1)
            gsel = GSEL[:].rearrange("p (k t) -> p k t", k=TOP_K)[:, :, tiles[0]:tiles[0] + nt]
            for k, o in enumerate((o1, o2)):
                dve.tensor_tensor(key, o, sc, ALU.mult)
                drain()
                dve.tensor_reduce(gsel[:, k, :], v3(key, 16), AX.X, ALU.add)
                drain()
            dve.tensor_tensor(m3, gsel[:, 0, :], gsel[:, 1, :], ALU.add)
            drain()
            dve.reciprocal(m3, m3)
            drain()
            for k in range(TOP_K):
                dve.tensor_tensor(gsel[:, k, :], gsel[:, k, :], m3, ALU.mult)
            dve.wait_ge(rt_ev["ranks_done"], n + 1)
            dve.tensor_copy(rk, PS[:, 6, a:a + nt * 16])
            dve.tensor_copy(cnt, PS[:, 6, 64:80])
            drain()
            dve.tensor_scalar(jobs, cnt, 0.0, None, ALU.is_gt)
            drain()
            for full in range(P, nt * P, P):
                dve.scalar_tensor_tensor(jobs, cnt, float(full), jobs, ALU.is_gt, ALU.add)
                drain()
            dve.tensor_tensor_scan(ends, ones[:, 0:16], jobs, 0.0, ALU.mult, ALU.add)
            drain()
            dve.tensor_tensor(base, ends, jobs, ALU.subtract)
            dve.tensor_tensor(ej, narrow(ends, MAX_JOBS, 16), wide(cst("job_index"), MAX_JOBS, 16), ALU.is_le)
            drain()
            dve.tensor_reduce(ejs[:, 0:MAX_JOBS], ej, AX.X, ALU.add)
            drain()
            dve.tensor_scalar(ejs[:, 0:MAX_JOBS], ejs[:, 0:MAX_JOBS], float(N_EXP - 1), None, ALU.min)
            dve.tensor_copy(ejs[:, MAX_JOBS:MAX_JOBS + 1], ends[:, 15:16])
            dve.scalar_tensor_tensor(v3(rk, 16), narrow(base, nt, 16), float(P), v3(rk, 16), ALU.mult, ALU.add)
            drain()
            dve.tensor_copy(JOBS[:, 32 * n:32 * n + MAX_JOBS + 1], ejs[:, 0:MAX_JOBS + 1]).then_inc(rt_ev["jobs_ready"], 1)
            for k, o in enumerate((o1, o2)):
                dve.tensor_tensor(key, o, rk, ALU.mult)
                drain()
                dve.tensor_reduce(rowf[:, k * NT + tiles[0]:k * NT + tiles[0] + nt], v3(key, 16), AX.X, ALU.add)
                drain()
            for k in range(TOP_K):
                c = slice(k * NT + tiles[0], k * NT + tiles[0] + nt)
                ins = dve.tensor_copy(ROWI[:, c], rowf[:, c])
            ins.then_inc(rt_ev["rows_ready"], 1)

        def rows_pool(pool, n, tiles):
            for v in ((0, 1) if n == 0 else (0,)):
                for k in range(KD):
                    ins = pool.tensor_scalar(DIAG[:, v, k * P:k * P + P], ident,
                                             mod[:, n, 5 * KD + k, v:v + 1], None, ALU.mult)
            ins.then_inc(gate_ev["gate_diag"], 1)
            pool.wait_ge(rt_ev["rows_copied"], OUT_BEFORE[n] + 2 * len(tiles))
            pool.wait_ge(rt_ev["rows_ready"], n + 1)
            for k in range(TOP_K):
                for t in tiles:
                    pool.indirect_dma_start(hg, bass.IndirectOffsetOnAxis(ROWI[:, k * NT + t:k * NT + t + 1], 0),
                                            XN[:, t, :], None).then_inc(rt_ev["rows_scattered"], 16)

        def back_pool(pool, n, tiles):
            J, b = jobs_of(pool, n)
            pool.wait_ge(moe_ev["o_stored"], (b + J) * 16 + 16)
            pool.tensor_tensor(SS[:, 60:61], ident[:, 0:1], ident[:, 0:1], ALU.mult)
            for t in tiles:
                for k in range(TOP_K):
                    pool.indirect_dma_start(BACK[:, k, t, :], None, hg,
                                            bass.IndirectOffsetOnAxis(ROWI[:, k * NT + t:k * NT + t + 1], 0)
                                            ).then_inc(rows_back[t // 2], 16)
            for i, t in enumerate(tiles):
                pool.wait_ge(end_ev["rows_gated"], END_BEFORE[n] + i + 1)
                pool.tensor_tensor(X[:, t, :], X[:, t, :], XN[:, t, :], ALU.add).then_inc(end_ev["x_added"], 1)

        def jobs_of(eng, n):
            eng.wait_ge(rt_ev["jobs_ready"], n + 1)
            J = [eng.value_load(JOBS[0:1, 32 * x + MAX_JOBS:32 * x + MAX_JOBS + 1], min_val=1, max_val=MAX_JOBS)
                 for x in range(n, -1, -1)]
            return J[0], (J[1] if n == 1 else 0)

        MOE_SLOTS = (2, 3, 4)

        def moe_pe(pe, n):
            ev = moe_ev
            J, b = jobs_of(pe, n)
            sg, su, sd = MOE_SLOTS
            if n == 0:
                pe.drain().then_inc(ev["gate_done"], 1)
                pe.drain().then_inc(ev["up_done"], 1)
                pe.drain().then_inc(ev["down_done"], 2)

            def turn(j):
                pe.wait_ge(ev["hg_loaded"], (b + j) * 16 + 16 * (n + 1))
                for k in range(KD):
                    mm = pe.transpose(PS[:, k // 4, k % 4 * P:k % 4 * P + P], mHG[:, k * P:k * P + P], ident)
                mm.then_inc(ev["x_turned"], 1)

            turn(0)
            with pe.Fori(0, J) as j:
                q = b + j
                pe.wait_ge(ev["x_copied"], q * 2 + 2 * (n + 1))
                pe.wait_ge(ev["w_gate"], q * 16 + 16)
                for k in range(KD):
                    mm = pe.matmul(PS[:, 2, :], HGT[:, k, :], slots[:, sg, k, :], start=(k == 0), stop=(k == KD - 1))
                mm.then_inc(ev["gate_done"], 1)
                pe.wait_ge(ev["w_up"], q * 16 + 16)
                for k in range(KD):
                    mm = pe.matmul(PS[:, 3, :], HGT[:, k, :], slots[:, su, k, :], start=(k == 0), stop=(k == KD - 1))
                mm.then_inc(ev["up_done"], 1)
                turn(j + 1)
                pe.wait_ge(ev["hidden"], q + 1)
                for f in range(4):
                    mm = pe.transpose(PS[:, 4, f * P:f * P + P], mHID[:, f * P:f * P + P], ident)
                mm.then_inc(ev["hid_turned"], 1)
                pe.wait_ge(ev["hid_copied"], q + 1)
                pe.wait_ge(ev["w_down"], q * 16 + 16)
                pe.wait_ge(ev["o_copied"], q * 2 + 2)
                wd = slots[:, sd, :, :].rearrange("p (f h) n -> p f h n", h=2)
                for h in range(2):
                    for f in range(4):
                        mm = pe.matmul(PS[:, 5 + h, :], HIDT[:, f, :], wd[:, f, h, :], start=(f == 0), stop=(f == 3))
                    mm.then_inc(ev["down_done"], 1)

        def moe_act(act, n):
            ev = moe_ev
            J, b = jobs_of(act, n)

            def copy_x(j):
                act.wait_ge(ev["x_turned"], b + j + n + 1)
                act.activation(mHGT[:, 0:512], PS[:, 0, :], ACT.Copy).then_inc(ev["x_copied"], 1)

            act.wait_ge(rt_ev["rows_scattered"], 16 * TOP_K * (4 if n == 0 else 6))
            act.dma_start(mHG, hg[0:P, :]).then_inc(ev["hg_loaded"], 16)
            copy_x(0)
            with act.Fori(0, J) as j:
                q = b + j
                act.wait_ge(ev["gate_done"], q + 2)
                act.activation(mTH, PS[:, 2, :], ACT.Tanh, scale=0.5).then_inc(ev["tanh"], 1)
                copy_x(j + 1)
                act.wait_ge(ev["hid_turned"], q + 1)
                act.activation(mHIDT, PS[:, 4, :], ACT.Copy).then_inc(ev["hid_copied"], 1)
                act.wait_ge(ev["down_done"], q * 2 + 3)
                act.wait_ge(ev["o_stored"], q * 16 + 16)
                act.activation(mOB[:, 0:512], PS[:, 5, :], ACT.Copy).then_inc(ev["o_copied"], 1)
                act.wait_ge(ev["o_copied"], q * 2 + 4)
                act.dma_start(hg[ds(j * P, P), :], mOB).then_inc(ev["o_stored"], 16)

        def moe_dve(dve, n):
            ev = moe_ev
            J, b = jobs_of(dve, n)
            if n == 0:
                dve.drain().then_inc(ev["o_copied"], 2)
                dve.drain().then_inc(ev["o_stored"], 16)

            def copy_x(j):
                dve.wait_ge(ev["x_turned"], b + j + n + 1)
                dve.tensor_copy(mHGT[:, 512:1024], PS[:, 1, :]).then_inc(ev["x_copied"], 1)

            copy_x(0)
            with dve.Fori(0, J) as j:
                q = b + j
                dve.wait_ge(ev["tanh"], q + 1)
                dve.scalar_tensor_tensor(mTG, mTH, 1.0, PS[:, 2, :], ALU.add, ALU.mult)
                dve.drain()
                dve.wait_ge(ev["up_done"], q + 2)
                dve.scalar_tensor_tensor(mHID, mTG, 0.5, PS[:, 3, :], ALU.mult, ALU.mult).then_inc(ev["hidden"], 1)
                copy_x(j + 1)
                dve.wait_ge(ev["down_done"], q * 2 + 4)
                dve.wait_ge(ev["o_stored"], q * 16 + 16)
                dve.tensor_copy(mOB[:, 512:1024], PS[:, 6, :]).then_inc(ev["o_copied"], 1)

        def moe_end_act(act, n, tiles):
            for t in tiles:
                act.wait_ge(rows_back[t // 2], 16 * 2 * TOP_K * (n + 1))
                act.activation(XN[:, t, :], BACK[:, 0, t, :], ACT.Copy,
                               scale=GSEL[:, t:t + 1]).then_inc(end_ev["first_scaled"], 1)
            if n == 0:
                for i, t in enumerate(tiles):
                    act.wait_ge(end_ev["x_added"], i + 1)
                    square_act(act, t)

        def moe_end_dve(dve, n, tiles):
            dve.wait_ge(gate_ev["gate_copied"], 2 * n + 2)
            for i, t in enumerate(tiles):
                y = XN[:, t, :]
                dve.wait_ge(end_ev["first_scaled"], END_BEFORE[n] + i + 1)
                dve.scalar_tensor_tensor(y, BACK[:, 1, t, :], GSEL[:, NT + t:NT + t + 1], y, ALU.mult, ALU.add)
                dve.drain()
                dve.tensor_tensor(y, y, GATE[:, 1 if t < 2 else 0, :], ALU.mult).then_inc(end_ev["rows_gated"], 1)

        EVEN_BASE = [64] * NSLOT
        OUT0_READY = [64 + 96 + 16, 64 + 64 + 16]
        ODD_BASE = [OUT0_READY[0], OUT0_READY[1], 64 + 96, 64, 64, 64]

        ESC = slots[:, 3:6, :, :].rearrange("p s k n -> p (s k n)")
        eU, eQX, eATT, eQK, eO, aAQ, aM = split(ESC, [2048, 2048, 4096, 1024, 1024, 1536, 128])
        U5 = eU.rearrange("p (d b e n) -> p d b e n", d=2, b=2, n=8)
        ATT5 = eATT.rearrange("p (d h t q) -> p d h t q", d=2, h=4, t=NT)
        QK = eQK.rearrange("p (a n) -> p a n", a=2)
        KT2 = QK
        O3 = eO.rearrange("p (t n) -> p t n", t=NT)
        gVG, gA, gC, gG, gQH, gKH, gF, gW = split(SCR[:, :], [2048, 1024, 1024, 1024, 1024, 1024, 128, 260])
        QX = eQX.rearrange("p (h n) -> p h n", h=4)
        VX = eATT.rearrange("p (t h e c) -> p t h e c", t=NT, h=4, c=4)
        gFE = SCR[:, 2048:4096]
        VG = gVG.rearrange("p (t n) -> p t n", t=NT)
        A2, C2, G2, QH, KH = [b.rearrange("p (d n) -> p d n", d=2) for b in (gA, gC, gG, gQH, gKH)]
        ZD = QH
        F3 = gF[:, 0:34].rearrange("p (d n) -> p d n", d=2)
        DN = gF[:, 34:66].rearrange("p (d n) -> p d n", d=2)
        GW = gW
        gla = {k: sem(f"gla_{k}") for k in (
            "small", "abs", "proj", "qkv_stored", "zd", "logits", "soft", "expo", "exp", "kh", "kturned", "ktok", "ds",
            "scanned", "states", "factors", "vx", "qx", "from_states", "att", "att_masked", "out", "out_stored", "ss", "rstd")}
        att = {k: sem(f"att_{k}") for k in (
            "proj", "stored", "ss", "rstd", "qk", "turned", "tstored", "scores", "max", "exp", "es", "sink_less_max", "pturned",
            "pt_stored", "pv", "out")}
        loop_meet = sem("loop_meet")
        aR, aSQ = gFE[:, 0:1280], gFE[:, 0:1280]
        aQT, aP = split(ESC[:, 4096:9216], [2560, 2048])
        AQ = aAQ.rearrange("p (t n) -> p t n", t=NT)
        SQ = aSQ.rearrange("p (t n) -> p t n", t=NT)
        QT = aQT.rearrange("p (h n) -> p h n", h=5)
        PB = aP.rearrange("p (b j n) -> p b j n", b=2, j=2)
        PTB = gFE.rearrange("p (b j n) -> p b j n", b=2, j=2)
        RT = [r.rearrange("p (t h n) -> p t h n", t=2, h=5) for r in split(aR, [320] * 4)]
        aMX, aNM, aRS, aES, aRD, aSK, aNS = split(aM, [16] * 5 + [4, 4])
        ORD = (list(range(NCH)), list(range(NCH // 2 - 1, -1, -1)) + list(range(NCH - 1, NCH // 2 - 1, -1)))

        def gla_pe(pe, i, base):
            def w_wait(s, n, per):
                pe.wait_ge(w_ready[s], i * per + base[s] + n)

            w_wait(0, 48, 48)
            for a in range(2):
                for k in range(KD):
                    mm = pe.matmul(PS[:, a, :], slots[:, 0, k, a * P:a * P + P], HT[:, k, :],
                                   start=(k == 0), stop=(k == KD - 1))
                mm.then_inc(gla["proj"], 1)
            w_wait(1, 32, 32)
            for k in range(KD):
                mm = pe.matmul(PS[0:32, 2, :], slots[:, 1, k, 256:288], HT[:, k, :], start=(k == 0), stop=(k == KD - 1))
            mm.then_inc(gla["proj"], 1)
            for t in range(NT):
                for s, c0 in ((0, 256), (1, 0)):
                    for k in range(KD):
                        mm = pe.matmul(PS[:, 4 + t, 256 * s:256 * s + 256], HT[:, k, t * P:t * P + P],
                                       slots[:, s, k, c0:c0 + 256], start=(k == 0), stop=(k == KD - 1))
                mm.then_inc(gla["proj"], 1)
            pe.wait_ge(gla["small"], 16 * i + 16)
            pe.wait_ge(gla["zd"], i + 1)
            for d in range(2):
                mm = pe.matmul(PS[:, 2 + d, :], GW[0:32, d * P:d * P + P], ZD[0:32, 0, :], start=True, stop=True)
            mm.then_inc(gla["logits"], 1)
            w_wait(2, 48, 48)
            pe.wait_ge(gla["qkv_stored"], 6 * i + 6)
            for t in range(NT):
                for k in range(KD):
                    mm = pe.matmul(PS[:, 4 + t, 0:384], HT[:, k, t * P:t * P + P], slots[:, 2, k, 0:384],
                                   start=(k == 0), stop=(k == KD - 1))
                mm.then_inc(att["proj"], 1)
            pe.wait_ge(gla["kh"], i + 1)
            for d in range(2):
                for t in range(NT):
                    mm = pe.transpose(PS[:, d, t * P:t * P + P], KH[:, d, t * P:t * P + P], ident)
                mm.then_inc(gla["kturned"], 1)
            pe.wait_ge(gla["vx"], i + 1)
            for d in range(2):
                pe.wait_ge(gla["ktok"], 2 * i + d + 1)
                for j, n in enumerate(ORD[d]):
                    t, c = n // 4, n % 4
                    for h in range(4):
                        mm = pe.matmul(PS[32 * h:32 * h + 32, 2 - 2 * d + j // 8, :]
                                       .rearrange("p (e n) -> p e n", n=8)[:, :, j % 8],
                                       KT2[:, d, t * P + 32 * h:t * P + 32 * h + 32], VX[:, t, h, :, c],
                                       start=True, stop=True)
                mm.then_inc(gla["ds"], 1)

            def scores(d):
                pe.wait_ge(gla["qx"], 2 * i + d + 1)
                for hp in range(2):
                    if d == 0:
                        pe.wait_ge(gla["scanned"], 2 * i + hp + 1)
                    else:
                        pe.wait_ge(gla["att_masked"], 4 * i + hp + 1)
                    if hp == 1:
                        pe.wait_ge(gla["states"], 2 * i + d + 1)
                        pe.wait_ge(att["stored"], NT * i + NT)
                    for h in (2 * hp, 2 * hp + 1):
                        for t in range(NT):
                            mm = pe.matmul(PS[:, (2 + h) % 4, t * P:t * P + P], KH[:, d, t * P:t * P + P],
                                           QX[:, h, t * P:t * P + P], start=True, stop=True)
                    mm.then_inc(gla["att"], 1)

            def from_states(d):
                for j, n in enumerate(ORD[d]):
                    t, c = n // 4, n % 4
                    z = (j - 1) % NCH
                    for h in range(4):
                        mm = pe.matmul(PS[32 * c:32 * c + 32, 4 + t, 64 * h:64 * h + 64],
                                       QX[:, h, t * P + 32 * c:t * P + 32 * c + 32], U5[:, d, z // 8, :, z % 8],
                                       start=(d == 0 and h == 0), stop=False, skip_group_check=True)
                mm.then_inc(gla["from_states"], 1)

            def within(d):
                pe.wait_ge(gla["att_masked"], 4 * i + 2 * d + 2)
                for t in range(NT):
                    for h in range(4):
                        mm = pe.matmul(PS[:, 4 + t, 64 * h:64 * h + 64], ATT5[:, d, h, t, :], VG[:, t, 64 * h:64 * h + 64],
                                       start=False, stop=(d == 1 and h == 3), skip_group_check=True)
                return mm

            scores(0)
            from_states(0)
            within(0)
            scores(1)
            from_states(1)
            within(1).then_inc(gla["out"], 1)

        def att_store(act, i, t):
            act.wait_ge(att["proj"], NT * i + t + 1)
            act.activation(AQ[:, t, :], PS[:, 4 + t, 0:384], ACT.Copy).then_inc(att["stored"], 1)

        def gla_act(act, i):
            for a in range(2):
                act.wait_ge(gla["proj"], 7 * i + a + 1)
                act.activation(QK[:, a, :], PS[:, a, :], ACT.Copy,
                               scale=GLA_DK ** -0.5 if a == 0 else 1.0).then_inc(gla["qkv_stored"], 1)
            for t in range(NT):
                act.wait_ge(gla["proj"], 7 * i + 4 + t)
                act.activation(VG[:, t, :], PS[:, 4 + t, :], ACT.Copy).then_inc(gla["qkv_stored"], 1)
            act.wait_ge(gla["logits"], i + 1)
            act.wait_ge(gla["small"], 16 * i + 16)
            for d in range(2):
                act.activation(A2[:, d, :], PS[:, 2 + d, :], ACT.Abs,
                               bias=GW[:, 256 + d:257 + d]).then_inc(gla["abs"], 1)
            act.drain()
            act.activation(gA, gA, ACT.Exp, scale=-1.0)
            act.drain()
            act.activation(gA, gA, ACT.Ln, bias=1.0).then_inc(gla["soft"], 1)
            for t in range(2):
                att_store(act, i, t)
            act.wait_ge(gla["expo"], i + 1)
            act.activation(gQH, gA, ACT.Exp, scale=1.0 / GLA_TAU)
            act.activation(gKH, gA, ACT.Exp, scale=-1.0 / GLA_TAU)
            act.activation(gF[:, 0:34], gF[:, 0:34], ACT.Exp, scale=1.0 / GLA_TAU).then_inc(gla["exp"], 1)
            for t in range(2, NT):
                att_store(act, i, t)
            for d in range(2):
                act.wait_ge(gla["kturned"], 2 * i + d + 1)
                act.activation(KT2[:, d, :], PS[:, d, :], ACT.Copy).then_inc(gla["ktok"], 1)
            for d in range(2):
                if d == 1:
                    act.wait_ge(gla["from_states"], 2 * i + 1)
                for h in range(4):
                    q = slice(32 * h, 32 * h + 32)
                    ins = act.activation(QX[q, h, :], QH[q, d, :], ACT.Copy)
                ins.then_inc(gla["qx"], 1)
            act.wait_ge(att["ss"], i + 1)
            act.activation(RS[:, 32:52], SS[:, 32:52], ACT.Ln, scale=1.0 / HD, bias=EPS[:, 0:1])
            act.drain()
            act.activation(RS[:, 32:52], RS[:, 32:52], ACT.Exp, scale=-0.5).then_inc(att["rstd"], 1)
            act.wait_ge(gla["out"], i + 1)
            act.activation(O3, PS[:, 4:8, 0:256], ACT.Copy).then_inc(gla["out_stored"], 1)

        def att_rows_dve(dve, i):
            drain = dve.drain
            dve.tensor_copy(aSK, row("sink")[:, ds(i * GRP, GRP)])
            drain()
            dve.tensor_scalar(aNS, aSK, -1.0, None, ALU.mult)
            dve.wait_ge(att["stored"], NT * i + NT)
            qk = AQ[:, :, 0:320]
            dve.tensor_tensor(SQ, qk, qk, ALU.mult)
            drain()
            dve.tensor_reduce(SS[:, 32:52], aSQ.rearrange("p (g e) -> p g e", e=HD), AX.X, ALU.add).then_inc(att["ss"], 1)
            dve.wait_ge(att["rstd"], i + 1)
            for t in range(NT):
                a3 = AQ[:, t, 0:320].rearrange("p (h e) -> p h e", h=5)
                dve.tensor_tensor(a3, a3, RS[:, 32 + 5 * t:37 + 5 * t].rearrange("p (h o) -> p h o", o=1)
                                  .broadcast_to([P, 5, HD]), ALU.mult)
            drain()
            dve.tensor_tensor(qk, qk, row("qk_gain").rearrange("p (o n) -> p o n", o=1).broadcast_to([P, NT, 320]),
                              ALU.mult)
            drain()
            r4 = cst("rope").rearrange("p (c t n) -> p c t n", c=2, t=2)
            for t in range(2):
                a3 = AQ[:, 2 + t, 0:320].rearrange("p (h e) -> p h e", h=5)
                a, b = a3[:, :, 0:32], a3[:, :, 32:64]
                c, s = [r4[:, x, t, :].rearrange("p (o n) -> p o n", o=1).broadcast_to([P, 5, 32]) for x in range(2)]
                for buf, u, v in ((0, a, c), (1, b, s), (2, a, s), (3, b, c)):
                    dve.tensor_tensor(RT[buf][:, t, :, :], u, v, ALU.mult)
            drain()
            for t in range(2):
                a3 = AQ[:, 2 + t, 0:320].rearrange("p (h e) -> p h e", h=5)
                dve.tensor_tensor(a3[:, :, 0:32], RT[0][:, t, :, :], RT[1][:, t, :, :], ALU.subtract)
                ins = dve.tensor_tensor(a3[:, :, 32:64], RT[2][:, t, :, :], RT[3][:, t, :, :], ALU.add)
            ins.then_inc(att["qk"], 1)

        def gla_pool(pool, i):
            pool.wait_ge(gla["qkv_stored"], 6 * i + 6)
            chunk = cst("chunk").rearrange("p (o c) -> p o c", o=1).broadcast_to([P, 256, 4])
            for t in range(NT):
                pool.tensor_tensor(VX[:, t].rearrange("p h e c -> p (h e) c"),
                                   VG[:, t, 0:256].rearrange("p (v o) -> p v o", o=1).broadcast_to([P, 256, 4]),
                                   chunk, ALU.mult)
            pool.drain().then_inc(gla["vx"], 1)
            pool.wait_ge(gla["exp"], i + 1)
            fe = gFE.rearrange("p (d b e n) -> p d b e n", d=2, b=2, n=8)
            for d in range(2):
                for b in range(2):
                    f = F3[:, d, 8 * b:8 * b + 8].rearrange("p (o n) -> p o n", o=1).broadcast_to([P, GLA_DV, 8])
                    one = ones[:, 0:8].rearrange("p (o n) -> p o n", o=1).broadcast_to([P, GLA_DV, 8])
                    pool.tensor_tensor(fe[:, d, b], f, one, ALU.mult)
            pool.drain()
            pool.memset(gFE.rearrange("p (m n) -> p m n", n=8)[:, :, 0:1], 0.0)
            pool.drain().then_inc(gla["factors"], 1)

        def gla_dve(dve, i):
            drain = dve.drain
            dve.wait_ge(gla["proj"], 7 * i + 3)
            dve.tensor_copy(ZD[0:32, 0, :], PS[0:32, 2, :]).then_inc(gla["zd"], 1)
            dve.wait_ge(gla["small"], 16 * i + 16)
            dve.wait_ge(gla["abs"], 2 * i + 2)
            for d in range(2):
                dve.tensor_scalar(G2[:, d, :], PS[:, 2 + d, :], GW[:, 256 + d:257 + d], 0.0, ALU.add, ALU.min)
            drain()
            dve.wait_ge(gla["soft"], i + 1)
            dve.tensor_tensor(gG, gG, gA, ALU.subtract)
            drain()
            for d in range(2):
                dve.tensor_tensor_scan(C2[:, d, :], cst("reset32"), G2[:, d, :], 0.0, ALU.mult, ALU.add)
            drain()
            cv = gC.rearrange("p (n s) -> p n s", s=GLA_C)
            dve.tensor_tensor(gA.rearrange("p (n s) -> p n s", s=GLA_C), cv,
                              cv[:, :, 15:16].broadcast_to([P, 2 * NCH, GLA_C]), ALU.subtract)
            c4 = gC.rearrange("p (d n s) -> p d n s", d=2, s=GLA_C)
            dve.tensor_tensor(DN, c4[:, :, :, 31], c4[:, :, :, 15], ALU.subtract)
            drain()
            dve.tensor_tensor(A2[:, 1, :], G2[:, 1, :], A2[:, 1, :], ALU.subtract)
            dve.memset(F3[:, :, 0:1], 0.0)
            dve.memset(F3[:, :, NCH:NCH + 1], 0.0)
            dve.tensor_tensor(F3[:, 0, 1:NCH], DN[:, 0, 0:NCH - 1], c4[:, 0, 1:NCH, 15], ALU.add)
            for j in range(1, NCH):
                a = ORD[1][j - 1]
                z = (a - 1) % NCH
                dve.tensor_tensor(F3[:, 1, j:j + 1], DN[:, 1, z:z + 1], c4[:, 1, a:a + 1, 15], ALU.add)
            drain()
            dve.tensor_scalar(gA, gA, 85.0 * GLA_TAU, -85.0 * GLA_TAU, ALU.min, ALU.max).then_inc(gla["expo"], 1)
            dve.wait_ge(gla["exp"], i + 1)
            dve.wait_ge(gla["qkv_stored"], 6 * i + 6)
            for d in range(2):
                dve.tensor_tensor(QH[:, d, :], QH[:, d, :], QK[:, 0, :], ALU.mult)
                ins = dve.tensor_tensor(KH[:, d, :], KH[:, d, :], QK[:, 1, :], ALU.mult)
            ins.then_inc(gla["kh"], 1)
            dve.memset(F3[:, :, NCH:NCH + 1], 0.0)
            drain()
            dve.wait_ge(gla["factors"], i + 1)
            for d in range(2):
                dve.wait_ge(gla["ds"], 2 * i + d + 1)
                for b in range(2):
                    u = PS[:, 2 - 2 * d + b, :]
                    if b == 1:
                        u0 = u.rearrange("p (e n) -> p e n", n=8)[:, :, 0]
                        dve.scalar_tensor_tensor(u0, U5[:, d, 0, :, 7], F3[:, d, 8:9], u0, ALU.mult, ALU.add)
                        drain()
                    k = (2 * d + b) * 512
                    ins = dve.tensor_tensor_scan(eU[:, k:k + 512], gFE[:, k:k + 512], u, 0.0, ALU.mult, ALU.add)
                    if b == 1:
                        ins.then_inc(gla["scanned"], 1)
                    drain()
                for b in range(2):
                    f = F3[:, d, 8 * b + 1:8 * b + 9].rearrange("p (o n) -> p o n", o=1).broadcast_to([P, GLA_DV, 8])
                    ins = dve.tensor_tensor(U5[:, d, b], U5[:, d, b], f, ALU.mult)
                ins.then_inc(gla["states"], 1)
            for d in range(2):
                mask = (cst("gla_incl")[:, d * P:d * P + P].rearrange("p (o q) -> p o q", o=1)
                        .broadcast_to([P, 2 * NT, P]))
                for hp in range(2):
                    b = 2 - 2 * hp
                    dve.wait_ge(gla["att"], 4 * i + 2 * d + hp + 1)
                    dve.tensor_tensor(ATT5[:, d, 2 * hp:2 * hp + 2].rearrange("p h t q -> p (h t) q"),
                                      PS[:, b:b + 2, :].rearrange("p h (t q) -> p (h t) q", t=NT),
                                      mask, ALU.mult).then_inc(gla["att_masked"], 1)
            att_rows_dve(dve, i)
            dve.wait_ge(gla["out_stored"], i + 1)
            o16 = eO.rearrange("p (g e) -> p g e", e=GLA_DV)
            q16 = gQH.rearrange("p (g e) -> p g e", e=GLA_DV)
            dve.tensor_tensor(gQH, eO, eO, ALU.mult)
            drain()
            dve.tensor_reduce(SS[:, 0:16], q16, AX.X, ALU.add).then_inc(gla["ss"], 1)
            dve.wait_ge(gla["rstd"], i + 1)
            dve.tensor_tensor(o16, o16, RS[:, 0:16].rearrange("p (g o) -> p g o", o=1).broadcast_to([P, 16, GLA_DV]),
                              ALU.mult)
            dve.scalar_tensor_tensor(QH[:, :, :].rearrange("p d (t n) -> p (d t) n", t=2),
                                     gKH.rearrange("p (t n) -> p t n", t=NT), 1.0, VG[:, :, 256:512], ALU.add, ALU.mult)
            drain()
            dve.tensor_tensor(o16, o16, row("gla_gain").rearrange("p (o e) -> p o e", o=1).broadcast_to([P, 16, GLA_DV]),
                              ALU.mult)
            drain()
            dve.scalar_tensor_tensor(XN[:, :, ds(i * 256, 256)], O3, 0.5,
                                     gQH.rearrange("p (t n) -> p t n", t=NT), ALU.mult, ALU.mult)

        GROUPS = [(hp, t) for hp in range(GRP // 2) for t in range(NT)]
        NG = len(GROUPS)

        def keys_of(t):
            return T if t >= 2 else SEG

        def att_pe(pe, i):
            pe.wait_ge(gla["out_stored"], i + 1)
            pe.wait_ge(att["qk"], i + 1)
            for h in range(5):
                for t in range(NT):
                    src, dst = AQ[:, t, h * HD:h * HD + HD], PS[0:HD, (4 + h) % 8, t * P:t * P + P]
                    if h == 0 and t == 0:
                        mm = pe.matmul(dst, src, ident, start=True, stop=True)
                    else:
                        mm = pe.transpose(dst, src, ident)
                mm.then_inc(att["turned"], 1)
            pe.wait_ge(att["tstored"], 5 * i + 5)
            for g in range(NG + 2):
                if g < NG:
                    hp, t = GROUPS[g]
                    if g >= 2:
                        pe.wait_ge(att["exp"], NG * i + g - 1)
                    for j in range(2):
                        mm = pe.matmul(PS[:, 2 * (g % 2) + j, 0:keys_of(t)], QT[0:HD, 2 * hp + j, t * P:t * P + P],
                                       QT[0:HD, 4, 0:keys_of(t)], start=True, stop=True)
                    mm.then_inc(att["scores"], 1)
                if 1 <= g <= NG:
                    v = g - 1
                    pe.wait_ge(att["exp"], NG * i + v + 1)
                    if v >= 1:
                        pe.wait_ge(att["pt_stored"], NG * i + v)
                    for j in range(2):
                        for c in range(keys_of(GROUPS[v][1]) // P):
                            mm = pe.transpose(PS[:, 4 + j, c * P:c * P + P], PB[:, v % 2, j, c * P:c * P + P], ident)
                    mm.then_inc(att["pturned"], 1)
                if g >= 2:
                    v = g - 2
                    pe.wait_ge(att["pt_stored"], NG * i + v + 1)
                    if v >= 2:
                        pe.wait_ge(att["out"], NG * i + v - 1)
                    nt = keys_of(GROUPS[v][1]) // P
                    for j in range(2):
                        for c in range(nt):
                            mm = pe.matmul(PS[:, 6 + v % 2, j * HD:j * HD + HD], PTB[:, v % 2, j, c * P:c * P + P],
                                           AQ[:, c, 320:384], start=(c == 0), stop=(c == nt - 1))
                    mm.then_inc(att["pv"], 1)

        def att_act(act, i):
            for h in range(5):
                act.wait_ge(att["turned"], 5 * i + h + 1)
                act.activation(QT[0:HD, h, :], PS[0:HD, (4 + h) % 8, :], ACT.Copy).then_inc(att["tstored"], 1)
            act.wait_ge(gla["ss"], i + 1)
            act.activation(RS[:, 0:16], SS[:, 0:16], ACT.Ln, scale=1.0 / GLA_DV, bias=EPS[:, 0:1])
            act.drain()
            act.activation(RS[:, 0:16], RS[:, 0:16], ACT.Exp, scale=-0.5)
            act.activation(gKH.rearrange("p (t n) -> p t n", t=NT), VG[:, :, 256:512], ACT.Tanh,
                           scale=0.5).then_inc(gla["rstd"], 1)
            for g in range(NG + 1):
                if g < NG:
                    hp, t = GROUPS[g]
                    nk = keys_of(t)
                    act.wait_ge(att["max"], NG * i + g + 1)
                    if g >= 2:
                        act.wait_ge(att["pturned"], NG * i + g - 1)
                    for j in range(2):
                        m = 4 * t + 2 * hp + j
                        ins = act.activation(PB[:, g % 2, j, 0:nk], PS[:, 2 * (g % 2) + j, 0:nk], ACT.Exp,
                                             scale=HD ** -0.5, bias=aNM[:, m:m + 1], accum_out=aRS[:, m:m + 1])
                    ins.then_inc(att["exp"], 1)
                if g >= 1:
                    v = g - 1
                    nk = keys_of(GROUPS[v][1])
                    act.wait_ge(att["pturned"], NG * i + v + 1)
                    if v >= 2:
                        act.wait_ge(att["pv"], NG * i + v - 1)
                    act.activation(PTB[:, v % 2, :, 0:nk], PS[:, 4:6, 0:nk], ACT.Copy).then_inc(att["pt_stored"], 1)
            act.wait_ge(att["sink_less_max"], i + 1)
            act.activation(aES, aES, ACT.Exp).then_inc(att["es"], 1)

        def att_dve(dve, i):
            drain = dve.drain
            for g in range(NG + 2):
                if g < NG:
                    hp, t = GROUPS[g]
                    b = 2 * (g % 2)
                    m = slice(4 * t + 2 * hp, 4 * t + 2 * hp + 2)
                    dve.wait_ge(att["scores"], NG * i + g + 1)
                    if t >= 2:
                        kt = 5 - t
                        blk = PS[:, b:b + 2, kt * P:kt * P + P]
                        dve.tensor_tensor(blk, blk, cst("att_mask")[:, (t - 2) * P:(t - 1) * P]
                                          .rearrange("p (o n) -> p o n", o=1).broadcast_to([P, 2, P]), ALU.add)
                        drain()
                    dve.tensor_reduce(aMX[:, m], PS[:, b:b + 2, 0:keys_of(t)], AX.X, ALU.max)
                    drain()
                    dve.scalar_tensor_tensor(aNM[:, m], aMX[:, m], -(HD ** -0.5), aNS[:, 2 * hp:2 * hp + 2],
                                             ALU.mult, ALU.min).then_inc(att["max"], 1)
                if g >= 2:
                    v = g - 2
                    hp, t = GROUPS[v]
                    dve.wait_ge(att["pv"], NG * i + v + 1)
                    dve.tensor_copy(AQ[:, t, hp * P:hp * P + P], PS[:, 6 + v % 2, 0:P]).then_inc(att["out"], 1)
                if g == NG:
                    th = [x.rearrange("p (t h) -> p t h", h=GRP) for x in (aES, aNM)]
                    dve.tensor_tensor(th[0], th[1], aSK.rearrange("p (o h) -> p o h", o=1).broadcast_to([P, NT, GRP]),
                                      ALU.add).then_inc(att["sink_less_max"], 1)
            dve.wait_ge(att["es"], i + 1)
            dve.tensor_tensor(aRD, aRS, aES, ALU.add)
            drain()
            dve.reciprocal(aRD, aRD)
            drain()
            for t in range(NT):
                dve.tensor_tensor(XN[:, t, ds(i * 256 + 512, 256)].rearrange("p (h e) -> p h e", h=GRP),
                                  AQ[:, t, 0:256].rearrange("p (h e) -> p h e", h=GRP),
                                  aRD[:, 4 * t:4 * t + 4].rearrange("p (h o) -> p h o", o=1).broadcast_to([P, GRP, HD]),
                                  ALU.mult)

        def turn_pe(pe):
            for k in range(KD):
                for t in range(NT):
                    mm = pe.transpose(PS[:, k, t * P:t * P + P], XN[:, t, k * P:k * P + P], ident)
                mm.then_inc(cat_turned, 1)

        def turn_copy(eng, ks):
            for k in ks:
                eng.wait_ge(cat_turned, k + 1)
                if eng.engine == nc.scalar.engine:
                    eng.activation(HT[:, k, :], PS[:, k, :], ACT.Copy)
                else:
                    eng.tensor_copy(HT[:, k, :], PS[:, k, :])

        def turned_meet(eng):
            eng.drain().then_inc(loop_meet, 1)
            eng.wait_ge(loop_meet, ENGINES * 3)

        L2 = SEG
        ODD1 = slots[:, 1, :, :].rearrange("p k n -> p (k n)")
        ODD45 = slots[:, 4:6, :, :].rearrange("p s k n -> p (s k n)")
        XNF = XN[:].rearrange("p t n -> p (t n)")
        CATT, oTW, oZA, oSG, oPV, oPD, oLW, oBON = split(XNF, [KD * L2, T, T, L2, 12, 12, 384, L2])
        oPPZ, oPXZ, oGT = split(slots[:, 2, :, :].rearrange("p k n -> p (k n)"), [4 * T, 4 * L2, L2])
        PPZ = oPPZ.rearrange("p (h d n) -> p h d n", h=2, d=2)
        PXZ = oPXZ.rearrange("p (h d n) -> p h d n", h=2, d=2)
        oG, oC, oE, oB, oKD, oPP, oPX, oS, oWS, oUS, oRZ, oF = split(
            SCR[:, :], [2 * T] * 6 + [T, 256, 256, 256, L2, 32])
        oXT, oMK, oNN, oTA = split(ODD45, [2048, 2048, 2048, 2048])
        oTB, oKZ, oVZ, oKK, oVT = split(ODD1, [2048, T, T, T, T])
        G_, C_, E_, B_, KD_, PP_, PX_ = [b.rearrange("p (d n) -> p d n", d=2) for b in (oG, oC, oE, oB, oKD, oPP, oPX)]
        BT_, KT_ = E_, G_
        ST_, WS_, US_ = [b.rearrange("p (d n) -> p d n", d=2) for b in (oS, oWS, oUS)]
        XT_, MK_, NN_ = [b.rearrange("p (d h c n) -> p d h c n", d=2, h=2, c=4) for b in (oXT, oMK, oNN)]
        LTS, XX, T1 = [[x.rearrange("p (c n) -> p c n", c=4) for b in bufs for x in split(b, [512] * (b.shape[1] // 512))]
                       for bufs in ((oTA,), (oTB,), (oC, oB))]
        ZP = [b.rearrange("p (s n) -> p s n", s=2) for b in split(oTA, [516, 516, 516])]
        MIXT, AVG = split(oTB, [512, 512])
        MIXT2, AVG2, KKH, KKS = split(oNN, [512, 512, 512, 512])
        FZ = oXT[:, 0:512].rearrange("p (t n) -> p t n", t=2)
        FB = oMK[:, 0:1024].rearrange("p (m n) -> p m n", m=2)
        oMID, oDN, oFF = [x.rearrange("p (d c) -> p d c", d=2) for x in split(oF, [8, 8, 8])]
        pre = {k: sem(f"pre_{k}") for k in ("proj", "stored", "mixed", "four", "four_stored", "four_tok",
                                            "four_tok_stored", "four_ch")}
        rw = {k: sem(f"rw_{k}") for k in (
            "small", "derived", "proj", "lora", "zp", "tanh_w", "tanh_a", "sq", "kksum", "kkrs", "v", "vturned",
            "vstored", "expo", "exps", "hat", "tok", "tok_stored", "gram", "lt", "gram_read", "xt0", "x0_turned", "x0",
            "t1", "t1s", "p", "x", "xt_turned", "xt", "w", "ws", "u", "us", "ds", "s", "y", "yb", "mean", "ysq", "var", "rstd", "bonus", "g2",
            "g2s", "rz", "kd_scale", "kd", "padded")}
        RORD = ((0, 1, 2, 3), (1, 0, 3, 2))
        NL = len(LEVELS)

        def odd_meet(eng, value):
            eng.drain().then_inc(loop_meet, 1)
            eng.wait_ge(loop_meet, value)

        def odd_pre_pe(pe):
            pe.wait_ge(w_ready[2], ODD_BASE[2] + 16)
            for x in range(3):
                c0 = L2 if x == 2 else 0
                for k in range(KD):
                    mm = pe.matmul(PS[:, x, c0:T], slots[:, 2, k, x * P:x * P + P], HT[:, k, c0:T],
                                   start=(k == 0), stop=(k == KD - 1))
                mm.then_inc(pre["proj"], 1)
            pe.wait_ge(w_ready[3], ODD_BASE[3] + 16)
            for t in range(2):
                for k in range(KD):
                    mm = pe.matmul(PS[:, 3 + t, 0:FOUR], HT[:, k, L2 + t * P:L2 + t * P + P], slots[:, 3, k, 0:FOUR],
                                   start=(k == 0), stop=(k == KD - 1))
            mm.then_inc(pre["four"], 1)
            pe.wait_ge(pre["four_stored"], 1)
            tok = cst("dft_tok").rearrange("p (t n) -> p t n", t=2)
            for m in range(2):
                for t in range(2):
                    mm = pe.matmul(PS[:, 5 + m, :], FZ[:, t, m * P:m * P + P], tok[:, t, :],
                                   start=(t == 0), stop=(t == 1))
            mm.then_inc(pre["four_tok"], 1)
            pe.wait_ge(pre["four_tok_stored"], 1)
            for m in range(2):
                for s in range(2):
                    mm = pe.matmul(PS[:, 7, m * L2:m * L2 + L2], cst("dft_ch")[:, s * P:s * P + P],
                                   FB[:, m, s * L2:s * L2 + L2], start=(s == 0), stop=(s == 1))
            mm.then_inc(pre["four_ch"], 1)

        def odd_pre_act(act):
            for x in range(3):
                s0 = 1 if x == 2 else 0
                act.wait_ge(pre["proj"], x + 1)
                act.activation(ZP[x][:, s0:2, 1:L2 + 1], PS[:, x, s0 * L2:T].rearrange("p (s n) -> p s n", n=L2),
                               ACT.Copy).then_inc(pre["stored"], 1)
            act.wait_ge(pre["four"], 1)
            act.activation(FZ, PS[:, 3:5, 0:FOUR], ACT.Copy).then_inc(pre["four_stored"], 1)
            act.wait_ge(pre["four_tok"], 1)
            act.activation(FB, PS[:, 5:7, :], ACT.Copy).then_inc(pre["four_tok_stored"], 1)
            act.wait_ge(pre["four_ch"], 1)
            act.activation(CATT[:, 0:2 * L2], PS[:, 7, :], ACT.Copy)
            act.wait_ge(pre["mixed"], 1)
            act.activation(oTW, oTW, ACT.Tanh)
            act.activation(oSG, oSG, ACT.Tanh, scale=0.5)

        def shift_mix(eng, out, zp, s0, mu_half, one_mu, scratch=(MIXT, AVG)):
            n = 2 - s0
            t3 = scratch[0][:, 0:n * L2].rearrange("p (s n) -> p s n", n=L2)
            a3 = scratch[1][:, 0:n * L2].rearrange("p (s n) -> p s n", n=L2)
            eng.tensor_tensor(a3, zp[:, s0:2, 0:L2], zp[:, s0:2, 2:L2 + 2], ALU.add)
            eng.tensor_scalar(t3, zp[:, s0:2, 1:L2 + 1], one_mu, None, ALU.mult)
            eng.drain()
            if eng.engine == nc.gpsimd.engine:
                eng.tensor_scalar(a3, a3, mu_half, None, ALU.mult)
                eng.drain()
                return eng.tensor_tensor(out.rearrange("p (s n) -> p s n", n=L2), a3, t3, ALU.add)
            return eng.scalar_tensor_tensor(out.rearrange("p (s n) -> p s n", n=L2), a3, mu_half, t3, ALU.mult, ALU.add)

        def zero_edges(dve):
            for z in ZP:
                dve.memset(z[:, :, 0:1], 0.0)
                dve.memset(z[:, :, L2 + 1:L2 + 2], 0.0)

        def odd_pre_dve(dve):
            zero_edges(dve)
            mu = prm("lora_mu")
            dve.tensor_scalar(oPD[:, 0:3], mu, 0.5, None, ALU.mult)
            dve.tensor_scalar(oPD[:, 3:6], mu, -1.0, 1.0, ALU.mult, ALU.add)
            dve.wait_ge(pre["stored"], 3)
            dve.drain()
            for x, dst in enumerate((oTW, oZA, oSG)):
                ins = shift_mix(dve, dst, ZP[x], 1 if x == 2 else 0, oPD[:, x:x + 1], oPD[:, 3 + x:4 + x])
                dve.drain()
            dve.drain().then_inc(pre["mixed"], 1)

        PROJ = ((1, 4), (2, 5), (0, 3))
        PBANK = dict(PROJ)

        def proj_pe(pe, x):
            c0 = L2 if x == 0 else 0
            for k in range(KD):
                mm = pe.matmul(PS[:, PBANK[x], c0:T], slots[:, 0, k, x * P:x * P + P], HT[:, k, c0:T],
                               start=(k == 0), stop=(k == KD - 1))
            mm.then_inc(rw["proj"], 1)

        def proj_act(act, i, x):
            s0 = 1 if x == 0 else 0
            act.wait_ge(rw["proj"], 3 * i + {1: 1, 2: 2, 0: 3}[x])
            act.activation(ZP[x][:, s0:2, 1:L2 + 1], PS[:, PBANK[x], s0 * L2:T].rearrange("p (s n) -> p s n", n=L2),
                           ACT.Copy).then_inc(rw["zp"], 1)

        def pair_pe(pe, i, ahead):
            for x, src, bank in ((0, oTW, 0), (1, oZA, 6)):
                if x == 0:
                    pe.wait_ge(rw["small"], i * 16 + 16)
                for d in range(2):
                    q = slice(64 * d, 64 * d + 64)
                    mm = pe.matmul(PS[:, bank + d, :], oLW[q, x * P:x * P + P], src[q, :], start=True, stop=True)
                mm.then_inc(rw["lora"], 1)
            pe.wait_ge(rw["sq"], i + 1)
            pe.matmul(PS[:, 2, :], head_ones, KKS, start=True, stop=True).then_inc(rw["kksum"], 1)
            pe.wait_ge(rw["zp"], 3 * i + 3)
            pe.matmul(PS[:, 3, 0:L2], oLW[:, 256:384], oSG, start=True, stop=True).then_inc(rw["g2"], 1)
            pe.wait_ge(rw["v"], i + 1)
            pe.wait_ge(rw["tanh_w"], i + 1)
            for c in range(4):
                mm = pe.transpose(PS[:, 0, c * P:c * P + P], oVZ[:, c * P:c * P + P], ident)
            mm.then_inc(rw["vturned"], 1)
            pe.wait_ge(rw["g2s"], i + 1)
            pe.wait_ge(rw["hat"], i + 1)
            for b, src in enumerate((B_, KD_)):
                for d in range(2):
                    for c in range(4):
                        mm = pe.transpose(PS[:, 1 + 2 * b + d, c * P:c * P + P], src[:, d, c * P:c * P + P], ident)
                    mm.then_inc(rw["tok"], 1)
            pe.wait_ge(rw["tok_stored"], 4 * i + 4)
            pe.wait_ge(rw["vstored"], i + 1)
            def gram(p):
                d, h = p // 2, p % 2
                pe.wait_ge(rw["padded"], 4 * i + p + 1)
                if p >= 2:
                    pe.wait_ge(rw["gram_read"], 4 * i + p - 1)
                for c in range(4):
                    cc = slice(c * P, c * P + P)
                    for bank, l in ((0, B_), (1, KD_)):
                        pe.matmul(PS[:, 4 * h + bank, cc], l[:, d, cc], PPZ[:, h, d, cc], start=True, stop=True)
                for c in range(2):
                    for bank, l in ((0, B_), (2, KD_)):
                        mm = pe.matmul(PS[:, 4 * h + 3, (bank + c) * P:(bank + c) * P + P],
                                       l[:, d, L2 + c * P:L2 + c * P + P], PXZ[:, h, d, c * P:c * P + P],
                                       start=True, stop=True)
                mm.then_inc(rw["gram"], 1)

            def turn_x0(p):
                pe.wait_ge(rw["xt0"], 4 * i + p + 1)
                if p >= 2:
                    pe.wait_ge(rw["x0"], 4 * i + p - 1)
                for c in range(4):
                    mm = pe.transpose(PS[:, 4 * (p % 2) + 2, c * P:c * P + P], XT_[:, p // 2, p % 2, c, :], ident)
                mm.then_inc(rw["x0_turned"], 1)

            gram(0)
            gram(1)
            gram(2)
            turn_x0(0)
            gram(3)
            for p in range(1, 4):
                turn_x0(p)
            for n in range(1, NL):
                lv = 4 * (6 * i + n - 1)
                for p in range(4):
                    if n == 1:
                        pe.wait_ge(rw["x0"], 4 * i + p + 1)
                    else:
                        pe.wait_ge(rw["x"], lv - 4 + p + 1)
                    if n == 1 and p == 0:
                        pe.wait_ge(rw["gram_read"], 4 * i + 4)
                    for c in range(4):
                        mm = pe.matmul(PS[:, p, c * P:c * P + P], LTS[p][:, c, :], XX[p][:, c, :], start=True, stop=True)
                    mm.then_inc(rw["t1"], 1)
                    if n > 1:
                        if n == 2 and p == 0:
                            pe.wait_ge(rw["x0"], 4 * i + 4)
                        for c in range(4):
                            mm = pe.transpose(PS[:, 4 + p, c * P:c * P + P], XX[p][:, c, :], ident)
                        mm.then_inc(rw["xt_turned"], 1)
                for p in range(4):
                    pe.wait_ge(rw["t1s"], lv + p + 1)
                    if n > 1:
                        pe.wait_ge(rw["xt"], 4 * (5 * i + n - 2) + p + 1)
                    for c in range(4):
                        xt = XT_[:, p // 2, p % 2, c, :]
                        l, r = (xt, T1[p][:, c, :]) if n < NL - 1 else (T1[p][:, c, :], xt)
                        mm = pe.matmul(PS[:, p, c * P:c * P + P], l, r, start=True, stop=True)
                    mm.then_inc(rw["p"], 1)
            pe.wait_ge(rw["x"], 24 * i + 24)
            for m in range(4):
                step = [(d, RORD[d][m]) for d in range(2)]
                for d, c in step:
                    if m > 0:
                        pe.wait_ge(rw["s"], 6 * i + 2 * (m - 1) + d + 1)
                        pe.matmul(PS[:, d, 0:P], PP_[:, d, c * P:c * P + P], ST_[:, d, :], start=True, stop=False,
                                  skip_group_check=True)
                    for h in range(2):
                        mm = pe.matmul(PS[:, d, 64 * h:64 * h + 64], MK_[:, d, h, c, :], oVT[:, c * P + 64 * h:c * P + 64 * h + 64],
                                       start=(m == 0), stop=True, skip_group_check=True)
                    mm.then_inc(rw["w"], 1)
                for d, c in step:
                    pe.wait_ge(rw["ws"], 8 * i + 2 * m + d + 1)
                    for h in range(2):
                        mm = pe.matmul(PS[:, 2 + d, 64 * h:64 * h + 64], XT_[:, d, h, c, :], WS_[:, d, 64 * h:64 * h + 64],
                                       start=True, stop=True)
                    mm.then_inc(rw["u"], 1)
                for d, c in step:
                    vt = oVT[:, c * P:c * P + P]
                    pe.wait_ge(rw["us"], 8 * i + 2 * m + d + 1)
                    if m >= 2:
                        mm = pe.matmul(PS[:, 4 + c, 0:P], ST_[:, d, :], PX_[:, d, (c - 2) * P:(c - 1) * P],
                                       start=(m == 2), stop=False, skip_group_check=True)
                        for h in range(2):
                            o = PS[64 * h:64 * h + 64, 4 + c, 0:P]
                            pe.matmul(o, US_[:, d, 64 * h:64 * h + 64], NN_[:, d, h, c - 2, :], start=False, stop=False,
                                      skip_group_check=True)
                            mm = pe.matmul(o, vt[:, 64 * h:64 * h + 64], NN_[:, d, h, c, :], start=False, stop=(m == 3),
                                           skip_group_check=True)
                        if m == 3:
                            mm.then_inc(rw["y"], 1)
                    if m < 3:
                        pe.matmul(PS[:, 4 + d, 0:P], BT_[:, d, c * P:c * P + P], US_[:, d, :], start=True, stop=False)
                        pe.matmul(PS[:, 4 + d, 0:P], KT_[:, d, c * P:c * P + P], vt, start=False,
                                  stop=True).then_inc(rw["ds"], 1)
            pe.matmul(PS[:, 1, 0:L2], head_ones, oBON, start=True, stop=True).then_inc(rw["bonus"], 1)
            if ahead:
                pe.wait_ge(w_ready[0], i * 48 + ODD_BASE[0] + 96)
                pe.wait_ge(rw["s"], 6 * i + 6)
                proj_pe(pe, 1)
            pe.wait_ge(rw["yb"], i + 1)
            pe.matmul(PS[:, 2, 0:L2], head_ones, oPX[:, 0:L2], start=True, stop=True).then_inc(rw["mean"], 1)
            if ahead:
                proj_pe(pe, 2)
            pe.wait_ge(rw["ysq"], i + 1)
            pe.matmul(PS[:, 2, 0:L2], head_ones, oPX[:, L2:2 * L2], start=True, stop=True).then_inc(rw["var"], 1)
            if ahead:
                pe.wait_ge(rw["us"], 8 * i + 8)
                proj_pe(pe, 0)

        def pair_act(act, i, ahead):
            act.wait_ge(rw["derived"], i + 1)
            for x, dst, bank in ((0, G_, 0), (1, B_, 6)):
                act.wait_ge(rw["lora"], 2 * i + x + 1)
                for d in range(2):
                    ins = act.activation(dst[:, d, :], PS[:, bank + d, :], ACT.Tanh, scale=0.5,
                                         bias=oPD[:, 2 * x + d:2 * x + d + 1])
                ins.then_inc(rw["tanh_w"] if x == 0 else rw["tanh_a"], 1)
            act.wait_ge(rw["kksum"], i + 1)
            act.activation(KKS, PS[:, 2, :], ACT.Ln, bias=EPS[:, 1:2])
            act.drain()
            act.activation(KKS, KKS, ACT.Exp, scale=-0.5).then_inc(rw["kkrs"], 1)
            act.wait_ge(rw["g2"], i + 1)
            act.activation(oGT, PS[:, 3, 0:L2], ACT.Copy).then_inc(rw["g2s"], 1)
            act.wait_ge(rw["vturned"], i + 1)
            act.activation(oVT, PS[:, 0, :], ACT.Copy).then_inc(rw["vstored"], 1)
            act.wait_ge(rw["expo"], i + 1)
            lat = slice(L2, T)
            act.activation(PP_[:, 0, :], G_[:, 0, :], ACT.Exp)
            act.activation(PP_[:, 1, :], E_[:, 1, :], ACT.Exp, scale=-1.0)
            act.activation(PX_[:, 0, 0:L2], E_[:, 0, lat], ACT.Exp)
            act.activation(PX_[:, 1, 0:L2], G_[:, 1, lat], ACT.Exp, scale=-1.0)
            act.activation(C_[:, 0, :], E_[:, 0, :], ACT.Exp, scale=-1.0)
            act.activation(C_[:, 1, :], G_[:, 1, :], ACT.Exp)
            act.activation(oFF, oFF, ACT.Exp).then_inc(rw["exps"], 1)
            act.wait_ge(rw["hat"], i + 1)
            for d in range(2):
                for h in range(2):
                    q = slice(64 * h, 64 * h + 64)
                    act.activation(PPZ[q, h, d, :], PP_[q, d, :], ACT.Copy)
                    act.activation(PXZ[q, h, d, :], PX_[q, d, 0:L2], ACT.Copy).then_inc(rw["padded"], 1)
            for b, dst in enumerate((BT_, KT_)):
                for d in range(2):
                    act.wait_ge(rw["tok"], 4 * i + 2 * b + d + 1)
                    act.activation(dst[:, d, :], PS[:, 1 + 2 * b + d, :], ACT.Copy).then_inc(rw["tok_stored"], 1)
            for p in range(4):
                act.wait_ge(rw["x0_turned"], 4 * i + p + 1)
                act.activation(XX[p], PS[:, 4 * (p % 2) + 2, :].rearrange("p (c n) -> p c n", c=4),
                               ACT.Copy).then_inc(rw["x0"], 1)
            for n in range(2, NL):
                for p in range(4):
                    act.wait_ge(rw["xt_turned"], 4 * (5 * i + n - 2) + p + 1)
                    act.activation(XT_[:, p // 2, p % 2], PS[:, 4 + p, :].rearrange("p (c n) -> p c n", c=4),
                                   ACT.Copy).then_inc(rw["xt"], 1)
            for m in range(4):
                for d in range(2):
                    act.wait_ge(rw["w"], 8 * i + 2 * m + d + 1)
                    act.activation(WS_[:, d, :], PS[:, d, 0:P], ACT.Copy).then_inc(rw["ws"], 1)
                for d in range(2):
                    act.wait_ge(rw["u"], 8 * i + 2 * m + d + 1)
                    act.activation(US_[:, d, :], PS[:, 2 + d, 0:P], ACT.Copy, scale=-1.0).then_inc(rw["us"], 1)
            if ahead:
                proj_act(act, i + 1, 1)
                proj_act(act, i + 1, 2)
            act.wait_ge(rw["var"], i + 1)
            act.activation(oPP[:, 0:L2], PS[:, 2, 0:L2], ACT.Ln, scale=1.0 / 64, bias=EPS[:, 2:3])
            act.drain()
            act.activation(oPP[:, 0:L2], oPP[:, 0:L2], ACT.Exp, scale=-0.5).then_inc(rw["rstd"], 1)
            if ahead:
                proj_act(act, i + 1, 0)

        def pair_pool(pool, i):
            pool.wait_ge(rw["derived"], i + 1)
            pool.wait_ge(rw["zp"], 3 * i + 2)
            shift_mix(pool, oVZ, ZP[2], 0, oPD[:, 6:7], oPD[:, 9:10], (MIXT2, AVG2)).then_inc(rw["v"], 1)
            pool.drain()
            pool.wait_ge(rw["zp"], 3 * i + 3)
            shift_mix(pool, oRZ, ZP[0], 1, oPD[:, 4:5], oPD[:, 7:8], (MIXT2, AVG2)).then_inc(rw["rz"], 1)
            pool.wait_ge(rw["kd_scale"], i + 1)
            for d in range(2):
                pool.tensor_tensor(KD_[:, d, :], KD_[:, d, :], oKZ, ALU.mult)
            pool.drain()
            pool.tensor_tensor(oBON, KD_[:, 0, L2:T], KD_[:, 1, L2:T], ALU.add).then_inc(rw["kd"], 1)
            pool.drain()
            pool.tensor_scalar(oBON, oBON, oPV[:, 9:10], None, ALU.mult)
            pool.drain()
            pool.tensor_tensor(oBON, oBON, oRZ, ALU.mult)
            lvl = cst("level").rearrange("p (d l n) -> p d l n", d=2, l=NL)
            eye = ident.rearrange("p (o n) -> p o n", o=1).broadcast_to([P, 4, P])
            for p in range(4):
                d, h = p // 2, p % 2
                mask = lvl[:, d, 0, :].rearrange("p (o n) -> p o n", o=1).broadcast_to([P, 4, P])
                pool.wait_ge(rw["lt"], 4 * i + p + 1)
                pool.tensor_tensor(XT_[:, d, h], LTS[p], mask, ALU.mult)
                pool.drain()
                pool.tensor_tensor(XT_[:, d, h], eye, XT_[:, d, h], ALU.subtract).then_inc(rw["xt0"], 1)

        def pair_dve(dve, i):
            drain = dve.drain
            dve.tensor_copy(oPV, prm("pair")[:, ds(i * 12, 12)] if not isinstance(i, int)
                            else prm("pair")[:, i * 12:i * 12 + 12])
            drain()
            dve.tensor_scalar(oPD[:, 0:4], oPV[:, 3:7], 0.5, None, ALU.mult)
            dve.tensor_scalar(oPD[:, 4:7], oPV[:, 0:3], 0.5, None, ALU.mult)
            dve.tensor_scalar(oPD[:, 7:10], oPV[:, 0:3], -1.0, 1.0, ALU.mult, ALU.add)
            dve.tensor_scalar(oPD[:, 11:12], oPV[:, 8:9], 0.5, None, ALU.mult)
            dve.tensor_scalar(oPD[:, 10:11], oPV[:, 8:9], -0.5, 1.0, ALU.mult, ALU.add).then_inc(rw["derived"], 1)
            drain()
            dve.wait_ge(rw["zp"], 3 * i + 1)
            shift_mix(dve, oKZ, ZP[1], 0, oPD[:, 5:6], oPD[:, 8:9])
            drain()
            dve.tensor_scalar(oKK, oKZ, oPV[:, 7:8], None, ALU.mult)
            drain()
            dve.tensor_tensor(KKS, oKK, oKK, ALU.mult).then_inc(rw["sq"], 1)
            dve.wait_ge(rw["tanh_w"], i + 1)
            dve.tensor_scalar(oG, oG, 1.0, -0.5 * EXP_M05, ALU.add, ALU.mult)
            drain()
            for d in range(2):
                dve.tensor_tensor_scan(C_[:, d, :], cst("reset128"), G_[:, d, :], 0.0, ALU.mult, ALU.add)
            drain()
            cv = oC.rearrange("p (n s) -> p n s", s=P)
            c4 = oC.rearrange("p (d c s) -> p d c s", d=2, s=P)
            dve.tensor_tensor(oE.rearrange("p (n s) -> p n s", s=P), cv, cv[:, :, 63:64].broadcast_to([P, 8, P]),
                              ALU.subtract)
            dve.tensor_copy(oMID, c4[:, :, :, 63])
            dve.tensor_tensor(oDN, c4[:, :, :, 127], c4[:, :, :, 63], ALU.subtract)
            drain()
            dve.tensor_tensor(oG, oE, oG, ALU.subtract)
            for d in range(2):
                a, b = (oDN, oMID) if d == 0 else (oMID, oDN)
                for c, e in zip(RORD[d], RORD[d][1:]):
                    dve.tensor_tensor(oFF[:, d, c:c + 1], a[:, d, c:c + 1], b[:, d, e:e + 1], ALU.add)
                dve.memset(oFF[:, d, RORD[d][3]:RORD[d][3] + 1], 0.0)
            drain().then_inc(rw["expo"], 1)
            dve.wait_ge(rw["kkrs"], i + 1)
            dve.tensor_tensor(oKK, oKK, KKS, ALU.mult)
            drain()
            dve.tensor_scalar(KKH, oKK, 0.5, None, ALU.mult)
            dve.wait_ge(rw["tanh_a"], i + 1)
            dve.tensor_scalar(oKD, oB, oPD[:, 11:12], oPD[:, 10:11], ALU.mult, ALU.add).then_inc(rw["kd_scale"], 1)
            drain()
            for d in range(2):
                dve.scalar_tensor_tensor(B_[:, d, :], B_[:, d, :], 1.0, KKH, ALU.add, ALU.mult)
            drain()
            dve.wait_ge(rw["exps"], i + 1)
            dve.tensor_tensor(oB, oB, oC, ALU.mult)
            dve.wait_ge(rw["rz"], i + 1)
            for d in range(2):
                dve.tensor_tensor(PP_[:, d, :], PP_[:, d, :], oKK, ALU.mult)
                dve.tensor_tensor(PX_[:, d, 0:L2], PX_[:, d, 0:L2], oRZ, ALU.mult)
            dve.wait_ge(rw["kd"], i + 1)
            dve.tensor_tensor(oKD, oKD, oC, ALU.mult)
            drain().then_inc(rw["hat"], 1)
            lvl = cst("level").rearrange("p (d l n) -> p d l n", d=2, l=NL)

            def four(ap, n=4):
                return ap.rearrange("p (o n) -> p o n", o=1).broadcast_to([P, n, P])

            for p in range(4):
                d, h = p // 2, p % 2
                strict = four(cst("strict")[:, d * P:d * P + P])
                dve.wait_ge(rw["gram"], 4 * i + p + 1)
                bank = [PS[:, 4 * h + b, :].rearrange("p (c n) -> p c n", c=4) for b in range(4)]
                dve.tensor_tensor(LTS[p], bank[0], strict, ALU.mult).then_inc(rw["lt"], 1)
                dve.tensor_tensor(MK_[:, d, h], bank[1], strict, ALU.mult)
                dve.tensor_tensor(NN_[:, d, h], bank[3], four(cst("incl")[:, d * P:d * P + P]),
                                  ALU.mult).then_inc(rw["gram_read"], 1)
            for n in range(1, NL):
                lv = 4 * (6 * i + n - 1)
                for p in range(4):
                    dve.wait_ge(rw["t1"], lv + p + 1)
                    dve.tensor_tensor(T1[p], PS[:, p, :].rearrange("p (c n) -> p c n", c=4),
                                      four(lvl[:, 1 - p // 2, n, :]), ALU.mult).then_inc(rw["t1s"], 1)
                for p in range(4):
                    dve.wait_ge(rw["p"], lv + p + 1)
                    x = XX[p] if n < NL - 1 else XT_[:, p // 2, p % 2]
                    dve.tensor_tensor(x, x, PS[:, p, :].rearrange("p (c n) -> p c n", c=4),
                                      ALU.subtract).then_inc(rw["x"], 1)
            zero_edges(dve)
            for m in range(3):
                for d in range(2):
                    c = RORD[d][m]
                    f = oFF[:, d, c:c + 1]
                    dve.wait_ge(rw["ds"], 6 * i + 2 * m + d + 1)
                    tmp = C_[:, d, 0:P]
                    dst = tmp if m > 0 else ST_[:, d, :]
                    ins = dve.scalar_tensor_tensor(dst, PS[:, 4 + d, 0:P], f, head_ones, ALU.mult, ALU.mult)
                    if m > 0:
                        drain()
                        ins = dve.scalar_tensor_tensor(ST_[:, d, :], ST_[:, d, :], f, tmp, ALU.mult, ALU.add)
                    ins.then_inc(rw["s"], 1)
            y, sq = oPX[:, 0:L2], oPX[:, L2:2 * L2]
            dve.wait_ge(rw["bonus"], i + 1)
            dve.tensor_tensor(oC[:, 0:L2], PS[:, 1, 0:L2], oVZ[:, L2:T], ALU.mult)
            drain()
            dve.wait_ge(rw["y"], 2 * i + 2)
            dve.tensor_tensor(y.rearrange("p (c n) -> p c n", c=2), oC[:, 0:L2].rearrange("p (c n) -> p c n", c=2),
                              PS[:, 6:8, 0:P], ALU.add).then_inc(rw["yb"], 1)
            drain()
            dve.wait_ge(rw["mean"], i + 1)
            dve.scalar_tensor_tensor(y, PS[:, 2, 0:L2], -1.0 / 64, y, ALU.mult, ALU.add)
            drain()
            dve.tensor_tensor(sq, y, y, ALU.mult).then_inc(rw["ysq"], 1)
            dve.wait_ge(rw["rstd"], i + 1)
            dve.tensor_tensor(y, y, oPP[:, 0:L2], ALU.mult)
            drain()
            dve.tensor_scalar(y, y, oPV[:, 10:11], oPV[:, 11:12], ALU.mult, ALU.add)
            drain()
            dve.wait_ge(rw["g2s"], i + 1)
            dve.tensor_tensor(CATT[:, ds(i * L2 + 2 * L2, L2)] if not isinstance(i, int)
                              else CATT[:, (i + 2) * L2:(i + 3) * L2], y, oGT, ALU.mult)

        def weights_odd(sp):
            w = odd_w_in[0]
            rk = FOUR + 3 * RW_DIM
            sp.wait_ge(phase, ENGINES * 8)
            weights_cols(sp, 2, 0, w, rk, 384)
            weights_cols(sp, 3, 0, w, 0, FOUR)
            sp.wait_ge(phase, ENGINES * 10)
            for i in range(NPAIR):
                if i > 0:
                    sp.wait_ge(rw["proj"], 3 * i)
                for x in range(3):
                    weights_cols(sp, 0, x * P, w, FOUR + x * RW_DIM + i * P, P)
                if i > 0:
                    sp.wait_ge(rw["g2"], i)
                sp.dma_start(oLW, pair_w[i]).then_inc(rw["small"], 16)
            sp.wait_ge(pre["four"], 1)
            sp.wait_ge(rw["proj"], 3 * NPAIR)
            for h, s in enumerate(OUT1_SLOTS):
                weights_cols(sp, s, 0, odd_w_out[0], 512 * h, 512)
            weights_moe(sp, 1)

        OUT1_SLOTS = (3, 0)
        OUT1_READY = [ODD_BASE[3] + 32, ODD_BASE[0] + 48 * NPAIR + 16]

        def odd_part_pe(pe):
            norm_pe(pe, 2, ALL)
            meet(pe, 9)
            odd_pre_pe(pe)
            meet(pe, 10)
            pe.wait_ge(w_ready[0], ODD_BASE[0] + 48)
            for x in (1, 2, 0):
                proj_pe(pe, x)
            pe.wait_ge(zeros_ready, 3)
            with pe.Fori(0, NPAIR - 1) as i:
                pair_pe(pe, i, True)
                odd_meet(pe, i * 3 + ENGINES * 4)
            pair_pe(pe, NPAIR - 1, False)
            meet(pe, 11)
            gate_pe(pe, 2, (0,))
            meet(pe, 12)
            out_pe(pe, 1, LAT, OUT1_SLOTS, OUT1_READY, CATT.rearrange("p (k n) -> p k n", k=KD))
            meet(pe, 13)
            norm_pe(pe, 3, LAT)
            meet(pe, 14)
            router_pe(pe, 1, LAT)
            meet(pe, 15)
            moe_pe(pe, 1)
            meet(pe, 16)

        def odd_part_act(act):
            norm_act(act, 2, ALL)
            meet(act, 9)
            odd_pre_act(act)
            meet(act, 10)
            for x in (1, 2, 0):
                proj_act(act, 0, x)
            with act.Fori(0, NPAIR - 1) as i:
                pair_act(act, i, True)
                odd_meet(act, i * 3 + ENGINES * 4)
            pair_act(act, NPAIR - 1, False)
            meet(act, 11)
            gate_act(act, 2, (0,))
            meet(act, 12)
            out_act(act, 1, LAT)
            meet(act, 13)
            norm_act(act, 3, LAT)
            meet(act, 14)
            router_act(act, 1, LAT)
            meet(act, 15)
            moe_act(act, 1)
            moe_end_act(act, 1, LAT)
            meet(act, 16)

        def odd_part_dve(dve):
            norm_dve(dve, 2, ALL)
            meet(dve, 9)
            odd_pre_dve(dve)
            meet(dve, 10)
            dve.tensor_scalar(oSG, oSG, 0.5, 0.5, ALU.mult, ALU.add)
            with dve.Fori(0, NPAIR - 1) as i:
                pair_dve(dve, i)
                odd_meet(dve, i * 3 + ENGINES * 4)
            pair_dve(dve, NPAIR - 1)
            meet(dve, 11)
            gate_dve(dve, 2, (0,))
            meet(dve, 12)
            out_dve(dve, 1, LAT)
            meet(dve, 13)
            norm_dve(dve, 3, LAT)
            meet(dve, 14)
            router_dve(dve, 1, LAT)
            meet(dve, 15)
            moe_dve(dve, 1)
            moe_end_dve(dve, 1, LAT)
            meet(dve, 16)

        def weights_ada(sp, blocks):
            for n in blocks:
                lay, b = n // N_ADA, n % N_ADA
                if n >= NSLOT:
                    sp.wait_ge(ada_rows, n - NSLOT + 1)
                sp.dma_start(slots[:, b % NSLOT, :, :], ada_w[lay, :, b * 512:b * 512 + 512]
                             .rearrange("(k p) n -> p k n", p=P)).then_inc(w_ready[b % NSLOT], 16)

        def weights_cols(sp, s, at, w, c0, width):
            sp.dma_start(slots[:, s, :, at:at + width],
                         w[:, c0:c0 + width].rearrange("(k p) n -> p k n", p=P)).then_inc(w_ready[s], 16)

        def weights_even(sp):
            w = even_w_in[0]
            for g in range(2):
                if g == 0:
                    sp.wait_ge(ada_rows, 2 * N_ADA - 5)
                else:
                    sp.wait_ge(gla["proj"], 7)
                for at, c0, width in ((0, 128 * g, 128), (128, 256 + 128 * g, 128), (256, 512 + 256 * g, 256)):
                    weights_cols(sp, 0, at, w, c0, width)
                if g == 0:
                    sp.wait_ge(ada_rows, 2 * N_ADA - 4)
                weights_cols(sp, 1, 0, w, 1024 + 256 * g, 256)
                weights_cols(sp, 1, 256, w, 1536, 32)
                if g == 1:
                    sp.wait_ge(gla["logits"], 1)
                    sp.wait_ge(gla["expo"], 1)
                sp.dma_start(GW[:, :], gla_small[g]).then_inc(gla["small"], 16)
                if g == 0:
                    sp.wait_ge(ada_rows, 2 * N_ADA - 3)
                else:
                    sp.wait_ge(att["proj"], NT)
                for at, c0, width in ((0, 1568 + 256 * g, 256), (256, 2080 + 64 * g, 64), (320, 2208 + 64 * g, 64)):
                    weights_cols(sp, 2, at, w, c0, width)
                if g == 0:
                    sp.wait_ge(zeros_ready, 1)
                    for j in range(MAX_JOBS + 1):
                        sp.dma_start(hg[j * P:j * P + P, :].rearrange("p (a n) -> p a n", n=ZCOLS),
                                     ZEROS.rearrange("p (o n) -> p o n", o=1).broadcast_to([P, D // ZCOLS, ZCOLS])
                                     ).then_inc(hg_zeroed, 16)
            sp.wait_ge(gla["proj"], 14)
            for h in range(2):
                weights_cols(sp, h, 0, even_w_out[0], 512 * h, 512)

        def weights_moe(sp, n):
            ev = moe_ev
            J, b = jobs_of(sp, n)
            sg, su, sd = MOE_SLOTS

            def load_hg(j):
                sp.dma_start(mHG, hg[ds(j * P, P), :]).then_inc(ev["hg_loaded"], 16)

            sp.wait_ge(phase, ENGINES * ROUTER_START[n])
            with sp.Fori(0, J) as j:
                q = b + j
                e = sp.value_load(JOBS[0:1, ds(j + 32 * n, 1)], min_val=0, max_val=N_EXP - 1)
                for s, w, free, ready in ((sg, moe_w_gate, "gate_done", "w_gate"), (su, moe_w_up, "up_done", "w_up")):
                    if s == su:
                        sp.wait_ge(ev["x_turned"], q + n + 1)
                    sp.wait_ge(ev[free], q + 1)
                    sp.dma_start(slots[:, s, :, :], w[n, ds(e, 1), :, :].rearrange("e (k p) n -> p (e k) n", p=P)
                                 ).then_inc(ev[ready], 16)
                load_hg(j + 1)
                sp.wait_ge(ev["down_done"], q * 2 + 2)
                sp.dma_start(slots[:, sd, :, :].rearrange("p (f h) n -> p f (h n)", h=2),
                             moe_w_down[n, ds(e, 1), :, :].rearrange("e (f p) n -> p (e f) n", p=P)
                             ).then_inc(ev["w_down"], 16)

        ROUTER_START = (6, 14)
        block = stack.enter_context(nc.Block())
        ALL, LAT = list(range(NT)), [2, 3]

        def even_meet(eng, value):
            eng.drain().then_inc(loop_meet, 1)
            eng.wait_ge(loop_meet, value)

        @block.sync
        def _(sp):
            sp.dma_start(PRM[:, :], params).then_inc(prm_ready, 16)
            weights_ada(sp, range(0, 1))
            sp.dma_start(CST[:, :], consts).then_inc(cst_ready, 16)
            weights_ada(sp, range(1, DEPTH * N_ADA - 3))
            sp.dma_start(X[:, 0:2, :], ctx_in[0].rearrange("(t p) n -> p t n", p=P)).then_inc(in_ready, 16)
            sp.dma_start(X[:, 2:4, :], x[0].rearrange("(t p) n -> p t n", p=P)).then_inc(in_ready, 16)
            sp.dma_start(ROW[:, :], rows.partition_broadcast(P)).then_inc(in_ready, 16)
            weights_ada(sp, range(DEPTH * N_ADA - 3, DEPTH * N_ADA))
            weights_even(sp)
            weights_moe(sp, 0)
            weights_odd(sp)
            for t in range(2):
                sp.wait_ge(end_ev["x_added"], NT + t + 1)
                sp.dma_start(out[0, t * P:t * P + P, :], X[:, 2 + t, :]).then_inc(out_stored, 16)
            sp.wait_ge(out_stored, 32)

        @block.tensor
        def _(pe):
            ada_pe(pe)
            meet(pe, 1)
            norm_pe(pe, 0, ALL)
            meet(pe, 2)
            with pe.Fori(0, 2) as i:
                gla_pe(pe, i, EVEN_BASE)
                att_pe(pe, i)
                even_meet(pe, i * 3 + 3)
            meet(pe, 3)
            gate_pe(pe, 0, (0, 1))
            meet(pe, 4)
            turn_pe(pe)
            turned_meet(pe)
            out_pe(pe, 0, ALL, (0, 1), OUT0_READY, HT)
            meet(pe, 5)
            norm_pe(pe, 1, ALL)
            meet(pe, 6)
            router_pe(pe, 0, ALL)
            meet(pe, 7)
            moe_pe(pe, 0)
            meet(pe, 8)
            odd_part_pe(pe)

        @block.scalar
        def _(act):
            act.wait_ge(prm_ready, 16)
            cond = prm("cond").rearrange("p (k v) -> p k v", v=2)
            act.activation(COND[:], cond, ACT.Tanh, scale=0.5).then_inc(cond_th, 1)
            ada_act(act)
            meet(act, 1)
            act.wait_ge(in_ready, 48)
            norm_act(act, 0, ALL)
            act.wait_ge(zeros_ready, 2)
            meet(act, 2)
            with act.Fori(0, 2) as i:
                gla_act(act, i)
                att_act(act, i)
                even_meet(act, i * 3 + 3)
            meet(act, 3)
            gate_act(act, 0, (0, 1))
            meet(act, 4)
            turn_copy(act, range(0, KD, 2))
            turned_meet(act)
            out_act(act, 0, ALL)
            meet(act, 5)
            norm_act(act, 1, ALL)
            meet(act, 6)
            router_act(act, 0, ALL)
            meet(act, 7)
            moe_act(act, 0)
            moe_end_act(act, 0, ALL)
            meet(act, 8)
            odd_part_act(act)

        @block.gpsimd
        def _(pool):
            pool.memset(ZEROS, 0.0)
            pool.drain().then_inc(zeros_ready, 1)
            pool.wait_ge(in_ready, 48)
            pool.wait_ge(phase, ENGINES * 1)
            pool.memset(eQX, 0.0)
            pool.drain().then_inc(zeros_ready, 1)
            with pool.Fori(0, 2) as i:
                gla_pool(pool, i)
            pool.wait_ge(phase, ENGINES * 6)
            rows_pool(pool, 0, ALL)
            back_pool(pool, 0, ALL)
            pool.wait_ge(phase, ENGINES * 10)
            pool.memset(oPPZ, 0.0)
            pool.memset(oPXZ, 0.0)
            pool.drain().then_inc(zeros_ready, 1)
            with pool.Fori(0, NPAIR) as i:
                pair_pool(pool, i)
            pool.wait_ge(phase, ENGINES * 14)
            rows_pool(pool, 1, LAT)
            back_pool(pool, 1, LAT)

        @block.vector
        def _(dve):
            for c, value in enumerate((NORM_EPS, L2_EPS, GN_EPS, 0.0)):
                dve.memset(EPS[:, c:c + 1], value)
            dve.wait_ge(prm_ready, 16)
            dve.wait_ge(cond_th, 1)
            cond = prm("cond").rearrange("p (k v) -> p k v", v=2)
            dve.scalar_tensor_tensor(COND[:], COND[:], 1.0, cond, ALU.add, ALU.mult)
            dve.drain()
            dve.tensor_scalar(COND[:], COND[:], 0.5, None, ALU.mult).then_inc(cond_ready, 1)
            ada_dve(dve)
            meet(dve, 1)
            dve.wait_ge(in_ready, 48)
            norm_dve(dve, 0, ALL)
            meet(dve, 2)
            with dve.Fori(0, 2) as i:
                gla_dve(dve, i)
                att_dve(dve, i)
                even_meet(dve, i * 3 + 3)
            meet(dve, 3)
            dve.wait_ge(hg_zeroed, 16 * (MAX_JOBS + 1))
            gate_dve(dve, 0, (0, 1))
            meet(dve, 4)
            turn_copy(dve, range(1, KD, 2))
            turned_meet(dve)
            out_dve(dve, 0, ALL)
            meet(dve, 5)
            norm_dve(dve, 1, ALL)
            meet(dve, 6)
            router_dve(dve, 0, ALL)
            meet(dve, 7)
            moe_dve(dve, 0)
            moe_end_dve(dve, 0, ALL)
            meet(dve, 8)
            odd_part_dve(dve)


def kernel(**inputs):
    import concourse.bacc as _bacc
    from concourse import mybir as _mybir
    from concourse.bass_utils import run_bass_kernel_spmd as _run

    a = {k: np.ascontiguousarray(v) for k, v in inputs.items()}

    def cols(v):
        return v.reshape(*v.shape[:-1], -1, P)

    norm = np.stack([a["norm_mix"][0], a["norm_ffn"][0], a["norm_mix"][1], a["norm_ffn"][1]])
    mu = a["rwkv_mu"][0]
    vecs = [mu[0:RW_DIM], mu[RW_DIM:2 * RW_DIM], mu[2 * RW_DIM:3 * RW_DIM], a["rwkv_w0"][0][0], a["rwkv_w0"][0][1],
            a["rwkv_a0"][0][0], a["rwkv_a0"][0][1], a["rwkv_kk_scale"][0], a["rwkv_k_a"][0],
            a["rwkv_r_k"][0].reshape(-1), a["rwkv_ln_g"][0], a["rwkv_ln_b"][0]]
    pairs = np.stack([v.reshape(NPAIR, P) for v in vecs], 0).transpose(2, 1, 0).reshape(P, -1)
    params = np.concatenate([
        cols(norm).reshape(-1, P).T,
        np.stack([a["c"][0].reshape(KD, P), a["c_ctx"].reshape(KD, P)], 1).reshape(-1, P).T,
        cols(a["ada_b"]).reshape(-1, P).T,
        mu[3 * RW_DIM:].reshape(3, P).T,
        a["router_w"].reshape(KD, P, 16).transpose(1, 0, 2).reshape(P, -1), pairs], 1)
    rows = np.concatenate([a["router_b"], a["att_sink"][0], np.tile(a["att_q_norm"][0], GRP), a["att_k_norm"][0],
                           a["gla_out_norm"][0]])
    gla_small = np.zeros((2, P, 260), np.float32)
    for g in range(2):
        for d in range(2):
            gla_small[g, 16 * d:16 * d + 16, d * P:d * P + P] = a["gla_dec_w"][0][d, :, g * P:g * P + P]
        gla_small[g, :, 256:258] = a["gla_dec_b"][0][:, g * P:g * P + P].T
    pair_w = np.stack([a["rwkv_w2"][0].reshape(P, NPAIR, P), a["rwkv_a2"][0].reshape(P, NPAIR, P),
                       a["rwkv_g2"][0].reshape(P, NPAIR, P)], 0).transpose(2, 1, 0, 3).reshape(NPAIR, P, 3 * P)
    laid = {"x": a["x"], "ctx": a["ctx"]}
    for k in ("ada_w", "even_w_in", "even_w_out", "odd_w_in", "odd_w_out", "moe_w_gate", "moe_w_up", "moe_w_down"):
        laid[k] = a[k]
    laid.update(consts=shape_constants(), params=params, rows=rows, gla_small=gla_small,
                pair_w=pair_w)

    nc = _bacc.Bacc("TRN2", target_bir_lowering=False, num_devices=1)
    arrays, args = {}, []
    for name, v in laid.items():
        v = np.ascontiguousarray(v)
        arrays[f"in_{name}_dram"] = v
        args.append(nc.dram_tensor(f"in_{name}_dram", v.shape, _mybir.dt.from_np(v.dtype), kind="ExternalInput").ap())
    args.append(nc.dram_tensor("out_0_dram", (1, SEG, D), F32, kind="ExternalOutput").ap())
    build(nc, *args)
    r = _run(nc, [arrays], core_ids=[0])
    return r.results[0]["out_0_dram"]
```
